# Optimizing a Trainium2 kernel written in Bass

```python
import jax, jax.numpy as jnp
from jax import lax
import numpy as np

D_MODEL = 1024
BATCH = 1
SEQ = 512
DEPTH = 1
DEC_BATCH = 8
DEC_SEQ = 4
PAST_LEN = 4096
PAGE_SIZE = 128

ML_HEADS = 4
ML_DK = 128
ML_DV = 128
GLA_HEADS = 4
GLA_DK = 64
GLA_DV = 128
GLA_RANK = 16
GLA_TAU = 16.0
MIX_WIDTH = ML_HEADS * ML_DV + GLA_HEADS * GLA_DV
CHUNK = 64
N_MEM = 256
XA_HEADS = 4
XA_DH = D_MODEL // XA_HEADS
D_FF = 2816
EPS = 1e-6
IN_SIZES = (ML_HEADS * ML_DK, ML_HEADS * ML_DK, ML_HEADS * ML_DV, ML_HEADS, ML_HEADS, ML_HEADS * ML_DV,
            GLA_HEADS * GLA_DK, GLA_HEADS * GLA_DK, GLA_HEADS * GLA_DV, GLA_RANK, GLA_HEADS * GLA_DV)
D_IN = sum(IN_SIZES)

kernel_name = 'hymba_mlstm_gla_macaron_memxattn_step'

def _rmsnorm(x, g):
    xf = x.astype(jnp.float32)
    y = xf * lax.rsqrt(jnp.mean(xf * xf, axis=-1, keepdims=True) + EPS)
    return (y * g.astype(jnp.float32)).astype(x.dtype)

def _head_rmsnorm(h, g):
    hf = h.astype(jnp.float32)
    y = hf * lax.rsqrt(jnp.mean(hf * hf, axis=-1, keepdims=True) + EPS)
    return y * g.astype(jnp.float32).reshape(h.shape[-2:])

def _swiglu(x, wg, wu, wd):
    return (jax.nn.silu(x @ wg) * (x @ wu)) @ wd

def _chunk_len(T):
    return CHUNK if T % CHUNK == 0 else T

def _to_chunks(a, L):
    B, T = a.shape[:2]
    return jnp.moveaxis(a.reshape((B, T // L, L) + a.shape[2:]), 1, 0)

def _from_chunks(a):
    a = jnp.moveaxis(a, 0, 1)
    return a.reshape((a.shape[0], a.shape[1] * a.shape[2]) + a.shape[3:])

def _mlstm(q, k, v, i_pre, logf, C0, n0, m0):
    L = _chunk_len(q.shape[1])
    mask = jnp.tril(jnp.ones((L, L), dtype=bool))[None, :, :, None]

    def step(carry, inp):
        C, n, m = carry
        qc, kc, vc, ic, fc = inp
        b = jnp.cumsum(fc, axis=1)
        a = b + m[:, None, :]
        Dm = jnp.where(mask, b[:, :, None, :] - b[:, None, :, :] + ic[:, None, :, :], -jnp.inf)
        mt = jnp.maximum(a, jnp.max(Dm, axis=2))
        w_inter = jnp.exp(a - mt)
        W = jnp.exp(Dm - mt[:, :, None, :])
        s = jnp.einsum('bthd,bshd->btsh', qc, kc) * W
        num = jnp.einsum('btsh,bshv->bthv', s, vc) + w_inter[..., None] * jnp.einsum('bthd,bhdv->bthv', qc, C)
        den = jnp.sum(s, axis=2) + w_inter * jnp.einsum('bthd,bhd->bth', qc, n)
        h = num / jnp.maximum(jnp.abs(den), jnp.exp(-mt))[..., None]
        wL = W[:, -1]
        iL = w_inter[:, -1]
        C_new = iL[..., None, None] * C + jnp.einsum('bsh,bshd,bshv->bhdv', wL, kc, vc)
        n_new = iL[..., None] * n + jnp.einsum('bsh,bshd->bhd', wL, kc)
        return (C_new, n_new, mt[:, -1]), h

    xs = (_to_chunks(q, L), _to_chunks(k, L), _to_chunks(v, L), _to_chunks(i_pre, L), _to_chunks(logf, L))
    init = (C0.astype(jnp.float32), n0.astype(jnp.float32), m0.astype(jnp.float32))
    (C, n, m), h = lax.scan(step, init, xs)
    return _from_chunks(h), C, n, m

def _gla(q, k, v, loga, S0):
    L = _chunk_len(q.shape[1])
    mask = jnp.tril(jnp.ones((L, L), dtype=bool))[None, :, :, None, None]

    def step(S, inp):
        qc, kc, vc, lc = inp
        Bc = jnp.cumsum(lc, axis=1)
        o_inter = jnp.einsum('bthd,bhdv->bthv', qc * jnp.exp(Bc), S)
        decay = jnp.exp(jnp.where(mask, Bc[:, :, None] - Bc[:, None, :], -jnp.inf))
        A = jnp.einsum('bthd,bshd,btshd->btsh', qc, kc, decay)
        o = o_inter + jnp.einsum('btsh,bshv->bthv', A, vc)
        BL = Bc[:, -1]
        S_new = jnp.exp(BL)[..., None] * S + jnp.einsum('bshd,bshv->bhdv', kc * jnp.exp(BL[:, None] - Bc), vc)
        return S_new, o

    xs = (_to_chunks(q, L), _to_chunks(k, L), _to_chunks(v, L), _to_chunks(loga, L))
    S, o = lax.scan(step, S0.astype(jnp.float32), xs)
    return _from_chunks(o), S

def _layer(x, mem_k, mem_v, C0, n0, m0, S0, w):
    Bsz, T, _ = x.shape
    f32 = jnp.float32
    x = x + 0.5 * _swiglu(_rmsnorm(x, w['ffn1_norm_g']), w['ffn1_w_gate'], w['ffn1_w_up'], w['ffn1_w_down'])
    z = _rmsnorm(x, w['mix_norm_g']) @ w['w_in']
    mq, mk, mv, mi, mf, mo, gq, gk, gv, ga, gg = jnp.split(z, np.cumsum(IN_SIZES)[:-1].tolist(), axis=-1)
    mq = mq.reshape(Bsz, T, ML_HEADS, ML_DK).astype(f32)
    mk = mk.reshape(Bsz, T, ML_HEADS, ML_DK).astype(f32) * (ML_DK ** -0.5)
    mv = mv.reshape(Bsz, T, ML_HEADS, ML_DV).astype(f32)
    i_pre = (mi + w['mlstm_b_i']).astype(f32)
    logf = jax.nn.log_sigmoid((mf + w['mlstm_b_f']).astype(f32))
    h_ml, C, n, m = _mlstm(mq, mk, mv, i_pre, logf, C0, n0, m0)
    y_ml = jax.nn.sigmoid(mo.astype(f32)) * _head_rmsnorm(h_ml, w['mlstm_out_g']).reshape(Bsz, T, ML_HEADS * ML_DV)
    gq = gq.reshape(Bsz, T, GLA_HEADS, GLA_DK).astype(f32) * (GLA_DK ** -0.5)
    gk = gk.reshape(Bsz, T, GLA_HEADS, GLA_DK).astype(f32)
    gv = gv.reshape(Bsz, T, GLA_HEADS, GLA_DV).astype(f32)
    loga = jax.nn.log_sigmoid((ga @ w['gla_w_a2'] + w['gla_b_a']).astype(f32)) / GLA_TAU
    loga = loga.reshape(Bsz, T, GLA_HEADS, GLA_DK)
    h_gla, S = _gla(gq, gk, gv, loga, S0)
    y_gla = jax.nn.silu(gg.astype(f32)) * _head_rmsnorm(h_gla, w['gla_out_g']).reshape(Bsz, T, GLA_HEADS * GLA_DV)
    y_mix = jnp.concatenate([y_ml, y_gla], axis=-1).astype(x.dtype)
    x = x + y_mix @ w['w_out']
    q = (_rmsnorm(x, w['xattn_norm_g']) @ w['xattn_w_q']).reshape(Bsz, T, XA_HEADS, XA_DH)
    s = jnp.einsum('bthd,bmhd->bhtm', q.astype(f32), mem_k.astype(f32)) * (XA_DH ** -0.5)
    p = jax.nn.softmax(s, axis=-1)
    o = jnp.einsum('bhtm,bmhd->bthd', p, mem_v.astype(f32)).reshape(Bsz, T, D_MODEL).astype(x.dtype)
    x = x + o @ w['xattn_w_o']
    x = x + 0.5 * _swiglu(_rmsnorm(x, w['ffn2_norm_g']), w['ffn2_w_gate'], w['ffn2_w_up'], w['ffn2_w_down'])
    return x, C.astype(C0.dtype), n.astype(n0.dtype), m.astype(m0.dtype), S.astype(S0.dtype)

def setup_inputs(seed: int = 0) -> dict:
    key = jax.random.key(seed)
    ks = list(jax.random.split(key, 40))
    ctr = [0]

    def nrm(shape, scale=1.0):
        k = ks[ctr[0]]
        ctr[0] += 1
        return scale * jax.random.normal(k, shape, jnp.float32)

    def gain(n):
        return 1.0 + 0.02 * nrm((DEPTH, n))

    d = {}
    d['x_prompt'] = nrm((BATCH, SEQ, D_MODEL))
    d['x_sample'] = nrm((DEC_BATCH, DEC_SEQ, D_MODEL))
    d['mem_prompt'] = nrm((BATCH, N_MEM, D_MODEL))
    d['cache_mem_k'] = nrm((DEPTH, DEC_BATCH, N_MEM, XA_HEADS, XA_DH))
    d['cache_mem_v'] = nrm((DEPTH, DEC_BATCH, N_MEM, XA_HEADS, XA_DH))
    d['state_mlstm_c'] = nrm((DEPTH, DEC_BATCH, ML_HEADS, ML_DK, ML_DV), 0.3)
    d['state_mlstm_n'] = nrm((DEPTH, DEC_BATCH, ML_HEADS, ML_DK), 0.3)
    d['state_mlstm_m'] = nrm((DEPTH, DEC_BATCH, ML_HEADS))
    d['state_gla_s'] = nrm((DEPTH, DEC_BATCH, GLA_HEADS, GLA_DK, GLA_DV), 0.3)
    d['ffn1_norm_g'] = gain(D_MODEL)
    d['ffn1_w_gate'] = nrm((DEPTH, D_MODEL, D_FF), D_MODEL ** -0.5)
    d['ffn1_w_up'] = nrm((DEPTH, D_MODEL, D_FF), D_MODEL ** -0.5)
    d['ffn1_w_down'] = nrm((DEPTH, D_FF, D_MODEL), D_FF ** -0.5)
    d['mix_norm_g'] = gain(D_MODEL)
    d['w_in'] = nrm((DEPTH, D_MODEL, D_IN), D_MODEL ** -0.5)
    d['mlstm_b_i'] = nrm((DEPTH, ML_HEADS), 0.1)
    d['mlstm_b_f'] = jnp.linspace(3.0, 6.0, ML_HEADS, dtype=jnp.float32)[None, :] + nrm((DEPTH, ML_HEADS), 0.1)
    d['mlstm_out_g'] = gain(ML_HEADS * ML_DV)
    d['gla_w_a2'] = nrm((DEPTH, GLA_RANK, GLA_HEADS * GLA_DK), GLA_RANK ** -0.5)
    d['gla_b_a'] = nrm((DEPTH, GLA_HEADS * GLA_DK), 0.1)
    d['gla_out_g'] = gain(GLA_HEADS * GLA_DV)
    d['w_out'] = nrm((DEPTH, MIX_WIDTH, D_MODEL), MIX_WIDTH ** -0.5)
    d['xattn_norm_g'] = gain(D_MODEL)
    d['mem_norm_g'] = gain(D_MODEL)
    d['xattn_w_q'] = nrm((DEPTH, D_MODEL, D_MODEL), D_MODEL ** -0.5)
    d['xattn_w_k'] = nrm((DEPTH, D_MODEL, D_MODEL), D_MODEL ** -0.5)
    d['xattn_w_v'] = nrm((DEPTH, D_MODEL, D_MODEL), D_MODEL ** -0.5)
    d['xattn_w_o'] = nrm((DEPTH, D_MODEL, D_MODEL), D_MODEL ** -0.5)
    d['ffn2_norm_g'] = gain(D_MODEL)
    d['ffn2_w_gate'] = nrm((DEPTH, D_MODEL, D_FF), D_MODEL ** -0.5)
    d['ffn2_w_up'] = nrm((DEPTH, D_MODEL, D_FF), D_MODEL ** -0.5)
    d['ffn2_w_down'] = nrm((DEPTH, D_FF, D_MODEL), D_FF ** -0.5)
    d['final_norm_g'] = 1.0 + 0.02 * nrm((D_MODEL,))
    return d

def reference(x_prompt, x_sample, mem_prompt, cache_mem_k, cache_mem_v, state_mlstm_c, state_mlstm_n,
              state_mlstm_m, state_gla_s, ffn1_norm_g, ffn1_w_gate, ffn1_w_up, ffn1_w_down, mix_norm_g, w_in,
              mlstm_b_i, mlstm_b_f, mlstm_out_g, gla_w_a2, gla_b_a, gla_out_g, w_out, xattn_norm_g, mem_norm_g,
              xattn_w_q, xattn_w_k, xattn_w_v, xattn_w_o, ffn2_norm_g, ffn2_w_gate, ffn2_w_up, ffn2_w_down,
              final_norm_g):
    layer_w = dict(ffn1_norm_g=ffn1_norm_g, ffn1_w_gate=ffn1_w_gate, ffn1_w_up=ffn1_w_up, ffn1_w_down=ffn1_w_down,
                   mix_norm_g=mix_norm_g, w_in=w_in, mlstm_b_i=mlstm_b_i, mlstm_b_f=mlstm_b_f,
                   mlstm_out_g=mlstm_out_g, gla_w_a2=gla_w_a2, gla_b_a=gla_b_a, gla_out_g=gla_out_g, w_out=w_out,
                   xattn_norm_g=xattn_norm_g, mem_norm_g=mem_norm_g, xattn_w_q=xattn_w_q, xattn_w_k=xattn_w_k,
                   xattn_w_v=xattn_w_v, xattn_w_o=xattn_w_o, ffn2_norm_g=ffn2_norm_g, ffn2_w_gate=ffn2_w_gate,
                   ffn2_w_up=ffn2_w_up, ffn2_w_down=ffn2_w_down)
    Bp = x_prompt.shape[0]
    dt = x_prompt.dtype
    xp, xs = x_prompt, x_sample
    mk_l, mv_l, cp_l, np_l, mp_l, sp_l, cs_l, ns_l, ms_l, ss_l = [], [], [], [], [], [], [], [], [], []
    for l in range(DEPTH):
        w = {name: arr[l] for name, arr in layer_w.items()}
        mem_n = _rmsnorm(mem_prompt, w['mem_norm_g'])
        mem_k_p = (mem_n @ w['xattn_w_k']).reshape(Bp, N_MEM, XA_HEADS, XA_DH)
        mem_v_p = (mem_n @ w['xattn_w_v']).reshape(Bp, N_MEM, XA_HEADS, XA_DH)
        c0 = jnp.zeros((Bp, ML_HEADS, ML_DK, ML_DV), dt)
        n0 = jnp.zeros((Bp, ML_HEADS, ML_DK), dt)
        m0 = jnp.zeros((Bp, ML_HEADS), dt)
        s0 = jnp.zeros((Bp, GLA_HEADS, GLA_DK, GLA_DV), dt)
        xp, c_p, n_p, m_p, s_p = _layer(xp, mem_k_p, mem_v_p, c0, n0, m0, s0, w)
        xs, c_s, n_s, m_s, s_s = _layer(xs, cache_mem_k[l], cache_mem_v[l], state_mlstm_c[l], state_mlstm_n[l],
                                        state_mlstm_m[l], state_gla_s[l], w)
        mk_l.append(mem_k_p)
        mv_l.append(mem_v_p)
        cp_l.append(c_p)
        np_l.append(n_p)
        mp_l.append(m_p)
        sp_l.append(s_p)
        cs_l.append(c_s)
        ns_l.append(n_s)
        ms_l.append(m_s)
        ss_l.append(s_s)
    y_prompt = _rmsnorm(xp, final_norm_g)
    y_sample = _rmsnorm(xs, final_norm_g)
    return (y_prompt, y_sample, jnp.stack(mk_l), jnp.stack(mv_l), jnp.stack(cp_l), jnp.stack(np_l),
            jnp.stack(mp_l), jnp.stack(sp_l), jnp.stack(cs_l), jnp.stack(ns_l), jnp.stack(ms_l), jnp.stack(ss_l))


_drawn_inputs = setup_inputs


def setup_inputs(seed=0):
    import zlib

    import numpy as np

    out = dict(_drawn_inputs(seed))
    spreads = {}
    factors = {'ffn1_norm_g': 3.903,
     'mlstm_b_i': 8.0,
     'mlstm_out_g': 8.0,
     'gla_out_g': 7.518,
     'xattn_norm_g': 8.0,
     'mem_norm_g': 2.911,
     'ffn2_norm_g': 7.805,
     'final_norm_g': 2.747}
    for name, (base, spread) in spreads.items():
        noise = np.random.default_rng([zlib.crc32(name.encode()), seed]).standard_normal(out[name].shape)
        drawn = base * np.exp(spread * noise) if base else spread * noise
        out[name] = __import__('jax').numpy.asarray(drawn.astype(out[name].dtype))
    for name, factor in factors.items():
        out[name] = (out[name] * factor).astype(out[name].dtype)
    return out
```

```python
import concourse.bass as bass
from concourse import mybir
from contextlib import ExitStack

D = 1024
ND = D // 128
TP, B, TS = 512, 8, 4
NS = B * TS
T = TP + NS
HT = T // 2
FF = 2816
NF = FF // 128
H, DK, DV, GK = 4, 128, 128, 64
L = 128
NC = TP // L
MEM = 256
EPS = 1e-6
RANK = 16
LEVELS = 6
TAU = 16.0
Z_GA, Z_GATE, Z_GQ, Z_GK, Z_GV, Z_MQ, Z_MK, Z_MV, Z_MO, Z_GG, NZ = 0, 1, 2, 4, 6, 10, 14, 18, 22, 26, 30
COL_MQ, COL_MI, COL_MF, COL_MO, COL_GQ, COL_GA, COL_GG = 0, 1536, 1540, 1544, 2056, 3080, 3096
C_ID, C_ONE, C_LEVEL, C_CAUSAL = 0, 128, 256, 256 + (LEVELS + 1) * 64
C_RESTART = C_CAUSAL + 128
C_SCAUSAL = C_RESTART + T
C_OWN = C_SCAUSAL + NS
N_CONST = C_OWN + B
G_FFN1, G_MIX, G_XA, G_MEM, G_FFN2, G_FIN, G_ML, G_GLA, G_BA, N_GAIN = 0, 8, 16, 24, 32, 40, 48, 52, 56, 58
UNIT = 1024
F32, F32R = mybir.dt.float32, mybir.dt.float32r
ALU, ACT, AX = mybir.AluOpType, mybir.ActivationFunctionType, mybir.AxisListType


def build(nc, a, o):
    ctx = ExitStack()
    with ctx:
        sems = {}

        def sem(name):
            if name not in sems:
                sems[name] = ctx.enter_context(nc.semaphore(name))
            return sems[name]

        base = (nc.sbuf_base + 63) // 64 * 64
        AT_X = base
        AT_XN = AT_X + ND * T * 4
        AT_H = AT_XN + 2 * ND * T * 4
        AT_W = AT_H + 2 * NF * T * 4
        AT_MISC = AT_W + 8 * UNIT * 4
        END = AT_MISC + 32000

        def at(name, shape, offset, dt=F32):
            size = 4
            for n in shape[1:]:
                size *= n
            assert offset + size <= END, name
            return nc.alloc_sbuf_tensor_at(name, shape, dt, offset=offset), (offset + size + 31) // 32 * 32

        x, _ = at("x", [128, ND, T], AT_X)
        xn_hi, p = at("xn_hi", [128, ND, T], AT_XN, F32R)
        xn_lo, _ = at("xn_lo", [128, ND, T], p, F32R)
        h_hi, p = at("h_hi", [128, NF, T], AT_H, F32R)
        h_lo, _ = at("h_lo", [128, NF, T], p, F32R)
        raw, w_hi, w_lo = [], [], []
        p = AT_W
        for n in range(4):
            t_, p = at(f"raw{n}", [128, UNIT], p)
            raw.append(t_)
        for n in range(2):
            t_, p = at(f"w_hi{n}", [128, UNIT], p, F32R)
            w_hi.append(t_)
            t_, p = at(f"w_lo{n}", [128, UNIT], p, F32R)
            w_lo.append(t_)
        p = AT_MISC
        const, p = at("const", [128, N_CONST], p)
        sel, p = at("sel", [H, H, 128], p)
        gains, p = at("gains", [128, N_GAIN], p)
        rinv, p = at("rinv", [128, T], p)
        acc, p = at("acc", [128, T], p)
        sq, sig, hf = [], [], []
        for n in range(2):
            t_, p = at(f"sq{n}", [128, T], p)
            sq.append(t_)
            t_, p = at(f"sig{n}", [128, T], p)
            sig.append(t_)
            t_, p = at(f"hf{n}", [128, T], p)
            hf.append(t_)
        mem_r, p = at("mem_r", [128, 2, 2], p)
        a2w, p = at("a2w", [RANK, H * GK], p)
        gate_b, p = at("gate_b", [64, 1], p)
        m0, p = at("m0", [H, B], p)
        p = AT_H
        mem_nat, p = at("mem_nat", [128, 2, D], p)
        xp_nat, p = at("xp_nat", [128, NC, D], p)
        xs_nat, p = at("xs_nat", [NS, D], p)
        gain_rows, p = at("gain_rows", [N_GAIN, 128], p)
        mem_f, p = at("mem_f", [128, ND, MEM], p)
        mem_hi, p = at("mem_hi", [128, ND, MEM], p, F32R)
        mem_lo, p = at("mem_lo", [128, ND, MEM], p, F32R)
        mem_sq, p = at("mem_sq", [128, D], p)
        kv_out = []
        for n in range(2):
            t_, p = at(f"kv_out{n}", [128, 2, 512], p)
            kv_out.append(t_)
        assert p <= AT_W
        z, p = at("z", [128, NZ, T], AT_H)
        rows, p = at("rows", [H, 8, T], p)
        R_U, R_W, R_B, R_M, R_WI, R_EM, R_WL, R_T = range(8)
        decay, p = at("decay", [128, 2, T], p)
        gla_a, p = at("gla_a", [128, NC, H, L], p)
        assert p <= AT_W
        p = AT_XN
        lv_e, p = at("lv_e", [128, 2, T], p)
        lv_q, lv_k = [], []
        for n in range(2):
            t_, p = at(f"lv_q{n}", [128, 2, T], p)
            lv_q.append(t_)
            t_, p = at(f"lv_k{n}", [128, 2, T], p)
            lv_k.append(t_)
        lv_acc, p = at("lv_acc", [128, NC, H, 64], p)
        lv_tmp, p = at("lv_tmp", [128, NC, H, 64], p)
        assert p <= AT_H
        p = AT_XN
        v_tok, p = at("v_tok", [128, H, DV], p)
        kw_tok, p = at("kw_tok", [128, H, DK], p)
        gk_tok, p = at("gk_tok", [128, 2, 128], p)
        gv_tok, p = at("gv_tok", [128, H, DV], p)
        ew, p = at("ew", [128, H, L], p)
        pw, p = at("pw", [128, H, L], p)
        q_in, p = at("q_in", [128, H, L], p)
        den, p = at("den", [128, H, L], p)
        ucol, p = at("ucol", [128, 2 * H], p)
        il, p = at("il", [128, H], p)
        ring = []
        for n in range(3):
            t_, p = at(f"ring{n}", [128, B, DV], p)
            ring.append(t_)
        s_ta = hf[1][0:NS, 0:12 * NS].rearrange("p (n r k t) -> p n r k t", n=3, r=2, k=2)
        s_a = hf[1][0:NS, 12 * NS:16 * NS].rearrange("p (h t) -> p h t", h=H)
        s_qn, p = at("s_qn", [128, H, NS], p)
        s_n, p = at("s_n", [128, B, H], p)
        s_n2, p = at("s_n2", [128, B, H], p)
        assert p <= AT_XN + 28672, p - AT_XN
        c_st, p = at("c_st", [128, H, DV], AT_XN + 28672)
        n_st, p = at("n_st", [128, H, 128], p)
        s_st, p = at("s_st", [128, H, DV], p)
        assert p <= AT_H
        p = AT_H + NZ * T * 4 + 8 * T * 4 + 2 * T * 4
        v_own = []
        for n in range(2):
            t_, p = at(f"v_own{n}", [NS, B, DV], p)
            v_own.append(t_)
        s_nrow, _ = at("s_nrow", [NS, DK], AT_H + NZ * T * 4 + 8 * T * 4)
        s_nrow2, _ = at("s_nrow2", [NS, DK], AT_H + NZ * T * 4 + 8 * T * 4 + 512)
        s_q, _ = at("s_q", [128, 2, 2, NS], AT_H + NZ * T * 4 + 8 * T * 4 + 1024)
        scan_in, p = at("scan_in", [H, 3, B, TS + 1], AT_XN)
        p = AT_H
        xq, p = at("xq", [128, ND, T], p)
        kv = []
        for n in range(3):
            t_, p = at(f"kv{n}", [128, 2, D], p)
            kv.append(t_)
        kT = []
        for n in range(2):
            t_, p = at(f"kT{n}", [128, ND, MEM], p)
            kT.append(t_)
        prob, probT = [], []
        for n in range(2):
            t_, p = at(f"prob{n}", [128, H, MEM], p)
            prob.append(t_)
            t_, p = at(f"probT{n}", [128, ND, 128], p)
            probT.append(t_)
        s_sc, p = at("s_sc", [128, 2, 128], p)
        xmx, p = at("xmx", [128, 3 * H], p)
        assert p <= AT_W
        yf, p = at("yf", [128, ND, T], AT_H)
        y_tok, p = at("y_tok", [128, NC + 1, D], p)
        assert p <= AT_W

        ps = ctx.enter_context(nc.psum_tensor("ps", [128, 8, 512], F32))
        ident = const[:, C_ID:C_ID + 128]
        ones = const[:, C_ONE:C_ONE + 128]
        causal = const[:, C_CAUSAL:C_CAUSAL + 128]
        restart = const[:, C_RESTART:C_RESTART + T]
        s_causal = const[0:NS, C_SCAUSAL:C_SCAUSAL + NS]
        own = const[0:NS, C_OWN:C_OWN + B]

        def level_mask(n):
            return const[:, C_LEVEL + 64 * n:C_LEVEL + 64 * n + 64]

        def pair(buf):
            q = 2 * (buf % 4)
            return ps[:, q:q + 2, 0:HT]

        def halves(t2d):
            return t2d.rearrange("p (h t) -> p h t", h=2)

        U_KV, B_KV = 0, 0
        B_N1 = 2
        U_UP1, B_UP1 = 16, 5
        U_DN1, B_DN1 = U_UP1 + 2 * NF, B_UP1 + 2 * NF
        B_N2 = B_DN1 + ND
        U_IN, B_IN = U_DN1 + 3 * ND, B_N2 + 1
        U_OUT, B_OUT = U_IN + NZ, B_IN + NZ
        B_N3 = B_OUT + ND
        U_XQ, B_XQ = U_OUT + ND, B_N3 + 1
        U_XO, B_XO = U_XQ + ND, B_XQ + ND
        B_N4 = B_XO + ND
        U_UP2, B_UP2 = U_XO + ND, B_N4 + 1
        U_DN2, B_DN2 = U_UP2 + 2 * NF, B_UP2 + 2 * NF
        B_N5 = B_DN2 + ND
        U_END = U_DN2 + 3 * ND

        def by_row(w):
            return w[0].rearrange("(kt p) c -> p kt c", p=128)

        wk, wv = by_row(a["xattn_w_k"]), by_row(a["xattn_w_v"])
        w_in, w_out = by_row(a["w_in"]), by_row(a["w_out"])
        wq, wo = by_row(a["xattn_w_q"]), by_row(a["xattn_w_o"])
        gate = [by_row(a["ffn1_w_gate"]), by_row(a["ffn2_w_gate"])]
        up = [by_row(a["ffn1_w_up"]), by_row(a["ffn2_w_up"])]
        down = [by_row(a["ffn1_w_down"]), by_row(a["ffn2_w_down"])]
        DN_K = [(0, 8), (8, 15), (15, 22)]
        mem_k_out = o["mem_k"][0, 0].rearrange("(mb p) h d -> p mb (h d)", p=128)
        mem_v_out = o["mem_v"][0, 0].rearrange("(mb p) h d -> p mb (h d)", p=128)

        block = ctx.enter_context(nc.Block())

        @block.sync
        def _(sp):
            raw_ready = [sem(f"raw_ready{n}") for n in range(4)]
            lo_done = sem("lo_done")

            sp.dma_start(const[:, :], a["consts"]).then_inc(sem("const_in"), 16)
            sp.dma_start(mem_nat[:, :, :], a["mem_prompt"][0].rearrange("(mb p) c -> p mb c", p=128))\
              .then_inc(sem("mem_in"), 16)

            def load(slot, src, free):
                if free is not None:
                    sp.wait_ge(lo_done, free)
                kts, cols = src.shape[1], src.shape[2]
                dst = raw[slot][:, 0:kts * cols].rearrange("p (k c) -> p k c", k=kts)
                sp.dma_start(dst, src).then_inc(raw_ready[slot], 16)

            for u in range(16):
                w, c, kt = (wk, wv)[u // 8], (u // 4) % 2, 2 * (u % 4)
                load(u % 4, w[:, kt:kt + 2, 512 * c:512 * c + 512], u - 3 if u >= 4 else None)
                if u == 3:
                    sp.dma_start(xp_nat[:, :, :], a["x_prompt"][0].rearrange("(c p) d -> p c d", p=128))\
                      .then_inc(sem("x_in"), 16)

            def load_up(n, u0):
                with sp.Fori(0, NF // 2) as i:
                    for k in range(4):
                        w = (gate, up)[k % 2][n]
                        load((u0 + k) % 4, w[:, :, bass.ds(i * 256 + 128 * (k // 2), 128)], i * 4 + (u0 + k - 3))

            def load_down(n, u0):
                with sp.Fori(0, 2) as i:
                    for k in range(12):
                        lo, hi = DN_K[k % 3]
                        load((u0 + k) % 4, down[n][:, lo:hi, bass.ds(i * 512 + 128 * (k // 3), 128)],
                             i * 12 + (u0 + k - 3))

            def load_blocks(w, u0, bodies, col, step=512):
                with sp.Fori(0, bodies) as i:
                    for k in range(4):
                        load((u0 + k) % 4, w[:, :, bass.ds(i * step + (col + 128 * k), 128)], i * 4 + (u0 + k - 3))

            load_up(0, U_UP1)
            load_down(0, U_DN1)
            load(U_IN % 4, w_in[:, :, COL_GA:COL_GA + 128], U_IN - 3)
            sp.wait_ge(lo_done, U_IN + 1 - 3)
            gate_unit = raw[(U_IN + 1) % 4][:, :].rearrange("p (k c) -> p k c", k=8)
            sp.dma_start(gate_unit[:, :, 0:H], w_in[:, :, COL_MI:COL_MI + H]).then_inc(sem("gate_i_in"), 16)
            sp.wait_ge(sem("gate_i_in"), 16)
            sp.dma_start(gate_unit[:, :, 32:32 + H], w_in[:, :, COL_MF:COL_MF + H])\
              .then_inc(raw_ready[(U_IN + 1) % 4], 16)
            load_blocks(w_in, U_IN + Z_GQ, 2, COL_GQ)
            load_blocks(w_in, U_IN + Z_MQ, 3, COL_MQ)
            load_blocks(w_in, U_IN + Z_MO, 2, COL_MO, COL_GG - COL_MO)
            load_blocks(w_out, U_OUT, 2, 0)
            load_blocks(wq, U_XQ, 2, 0)
            load_blocks(wo, U_XO, 2, 0)
            load_up(1, U_UP2)
            load_down(1, U_DN2)

        @block.gpsimd
        def _(pool):
            steps = [0]

            def link(ins):
                steps[0] += 1
                ins.then_inc(sem("pool_chain"), 1)
                pool.wait_ge(sem("pool_chain"), steps[0])

            pool.dma_start(xs_nat[:, :], a["x_sample"].rearrange("b t d -> (b t) d")).then_inc(sem("xs_in"), 16)
            rows_of = [("ffn1_norm_g", G_FFN1, 8), ("mix_norm_g", G_MIX, 8), ("xattn_norm_g", G_XA, 8),
                       ("mem_norm_g", G_MEM, 8), ("ffn2_norm_g", G_FFN2, 8), ("final_norm_g", G_FIN, 8),
                       ("mlstm_out_g", G_ML, 4), ("gla_out_g", G_GLA, 4), ("gla_b_a", G_BA, 2)]
            for name, g, n in rows_of:
                src = a[name] if name == "final_norm_g" else a[name][0]
                pool.dma_start(gain_rows[g:g + n, :], src.rearrange("(n p) -> n p", p=128))\
                    .then_inc(sem("gains_in"), 16)
            pool.dma_start(sel[:, :, :], a["sel"].rearrange("h (k p) -> h k p", k=H)).then_inc(sem("small_in"), 16)
            pool.dma_start(a2w[:, :], a["gla_w_a2"][0]).then_inc(sem("small_in"), 16)
            pool.dma_start(gate_b[0:H, :], a["mlstm_b_i"].rearrange("a h -> h a")).then_inc(sem("small_in"), 16)
            pool.dma_start(gate_b[32:32 + H, :], a["mlstm_b_f"].rearrange("a h -> h a")).then_inc(sem("small_in"), 16)
            pool.dma_start(m0[:, :], a["state_mlstm_m"][0].rearrange("b h -> h b"),
                           allow_slow_non_contiguous=True).then_inc(sem("small_in"), 16)

            for n in range(4):
                pool.wait_ge(sem("evac"), (1, 2, 4, 5)[n])
                dst = (mem_k_out, mem_v_out)[n // 2][:, :, 512 * (n % 2):512 * (n % 2) + 512]
                pool.dma_start(dst, kv_out[n % 2][:, :, :]).then_inc(sem(f"kv_stored{n % 2}"), 16)

            pool.wait_ge(sem("evac"), B_IN + NZ)
            link(pool.memset(gla_a[64:128, :, :, 0:64], 0.0))
            link(pool.memset(rows[:, R_WI, 0:L], 0.0))
            pool.memset(s_st[:, :, :], 0.0).then_inc(sem("zeros_set"), 1)
            for n in range(1, LEVELS):
                pool.wait_ge(sem("lv_masked"), n + 1)
                pool.tensor_tensor(lv_acc[:, :, :, :], lv_acc[:, :, :, :], lv_tmp[:, :, :, :], ALU.add)\
                    .then_inc(sem("lv_added"), 1)

            c_in = a["state_mlstm_c"][0].rearrange("b h k v -> h k b v")
            s_in = a["state_gla_s"][0].rearrange("b (p r) k v -> p (r k) b v", r=2)
            c_out = o["mlstm_c_s"][0].rearrange("b h k v -> h k b v")
            s_out = o["gla_s_s"][0].rearrange("b (p r) k v -> p (r k) b v", r=2)

            def load_state(n):
                src = c_in[n] if n < H else s_in[n - H]
                pool.dma_start(ring[n % 3][:, :, :], src).then_inc(sem(f"state_in{n % 3}"), 16)

            pool.wait_ge(sem("levels_done"), 1)
            pool.dma_start(s_nrow[:, :], a["state_mlstm_n"][0].rearrange("b h k -> (b h) k"))\
                .then_inc(sem("n_in"), 16)
            for n in range(3):
                load_state(n)

            for c in range(NC + 1):
                pool.wait_ge(sem("w_exp"), c + 1)
                if c < NC:
                    pool.tensor_tensor(ew[:, :, :], ew[:, :, :], causal.unsqueeze(1).broadcast_to([128, H, L]),
                                       ALU.mult).then_inc(sem("w_masked"), 1)
                else:
                    pool.tensor_tensor(ew[0:NS, :, 0:NS], ew[0:NS, :, 0:NS],
                                       s_causal.unsqueeze(1).broadcast_to([NS, H, NS]), ALU.mult)\
                        .then_inc(sem("w_masked"), 1)

            pool.wait_ge(sem("chunk_done"), NC)
            pool.wait_ge(sem("gla_out"), NC)
            pool.dma_start(o["mlstm_c_p"][0, 0].rearrange("h k v -> k h v"), c_st[:, :, :]).then_inc(sem("st_out"), 16)
            pool.dma_start(o["mlstm_n_p"][0, 0].rearrange("h k -> k h"), n_st[:, :, 0],
                           allow_slow_non_contiguous=True).then_inc(sem("st_out"), 16)
            pool.dma_start(o["mlstm_m_p"][0, 0].rearrange("(h a) -> h a", a=1), rows[:, R_M, TP - 1:TP])\
                .then_inc(sem("st_out"), 16)
            for h in range(H):
                r = 64 * (h % 2)
                pool.dma_start(o["gla_s_p"][0, 0, h], s_st[r:r + 64, h, :]).then_inc(sem("st_out"), 16)
            pool.dma_start(o["mlstm_m_s"][0].rearrange("b h -> h b"),
                           rows[:, R_M, TP + TS - 1:T:TS], allow_slow_non_contiguous=True)\
                .then_inc(sem("st_out"), 16)
            for n in range(H + 2):
                pool.wait_ge(sem("upd_free"), (1, 2, 3, 4, 6, 8)[n])
                dst = c_out[n] if n < H else s_out[n - H]
                pool.dma_start(dst, ring[n % 3][:, :, :]).then_inc(sem(f"state_out{n % 3}"), 16)
                if n + 3 < H + 2:
                    pool.wait_ge(sem(f"state_out{n % 3}"), 16 * (n // 3 + 1))
                    load_state(n + 3)
            pool.wait_ge(sem("n_new"), 1)
            pool.dma_start(o["mlstm_n_s"][0].rearrange("b h k -> (b h) k"), s_nrow2[:, :]).then_inc(sem("st_out"), 16)
            pool.wait_ge(sem("st_out"), 16 * 9)
            for n in range(3):
                pool.wait_ge(sem(f"state_out{n}"), 32)
            pool.sem_inc(sem("mixer_stored"), 1)

            for n in range(18):
                if n == 0:
                    pool.wait_ge(sem("ym_lo"), 8)
                    pool.wait_ge(sem("kv_stored0"), 32)
                    pool.wait_ge(sem("kv_stored1"), 32)
                if n >= 3:
                    was = n - 3
                    name, value = (("av_mm", NC) if was == 1 else ("kT_mm", max(was, 1)) if was < 10
                                   else ("sav_mm", was - 9))
                    pool.wait_ge(sem(name), value)
                if n < 2:
                    src = (mem_k_out, mem_v_out)[n]
                else:
                    src = (a["cache_mem_k"], a["cache_mem_v"])[n // 10][0, (n - 2) % 8]\
                        .rearrange("(mb p) h d -> p mb (h d)", p=128)
                pool.dma_start(kv[n % 3][:, :, :], src).then_inc(sem(f"kv_in{n % 3}"), 16)

            for c in range(NC):
                pool.wait_ge(sem("y_copied"), c + 1)
                pool.dma_start(o["y_prompt"][0, c * L:(c + 1) * L, :], y_tok[:, c, :]).then_inc(sem("y_out"), 16)
            pool.wait_ge(sem("y_copied"), NC + 1)
            pool.dma_start(o["y_sample"].rearrange("b t d -> (b t) d"), y_tok[0:NS, NC, :]).then_inc(sem("y_out"), 16)
            pool.wait_ge(sem("y_out"), 16 * (NC + 1))

        @block.scalar
        def _(act):
            raw_ready = [sem(f"raw_ready{n}") for n in range(4)]
            pe_unit, evac = sem("pe_unit"), sem("evac")
            steps = [0]

            def link(ins):
                steps[0] += 1
                ins.then_inc(sem("act_chain"), 1)
                act.wait_ge(sem("act_chain"), steps[0])

            def split(u0, i=0, per=0):
                act.wait_ge(raw_ready[u0 % 4], 16 * (u0 // 4 + 1) + i * (4 * per))
                if u0 >= 2:
                    act.wait_ge(pe_unit, i * per + (u0 - 1))
                act.activation(w_hi[u0 % 2][:, :], raw[u0 % 4][:, :], ACT.Copy).then_inc(sem("hi_done"), 1)

            def square(r, src, ready, value, i=0, per=0):
                act.wait_ge(ready, value)
                if r >= 2:
                    act.wait_ge(sem("acc_done"), i * per + (r - 1))
                act.activation(sq[r % 2][:, :], src, ACT.Square).then_inc(sem("sq_done"), 1)

            def norm_root(g, buf):
                act.wait_ge(sem("norm_mm"), g + 1)
                act.activation(halves(sig[0][:, :]), pair(buf), ACT.Sqrt, bias=EPS, scale=1.0 / D).then_inc(evac, 1)

            def norm_hi(g, d):
                act.wait_ge(sem("xf_done"), 8 * g + d + 1)
                act.activation(xn_hi[:, d, :], hf[d % 2][:, :], ACT.Copy).then_inc(sem("xnh_done"), 1)

            def norm(g, buf):
                norm_root(g, buf)
                for d in range(ND):
                    norm_hi(g, d)

            act.wait_ge(sem("mem_in"), 16)
            for mb in range(2):
                link(act.activation(mem_sq[:, :], mem_nat[:, mb, :], ACT.Square, accum_out=mem_r[:, 0, mb:mb + 1]))
            act.activation(mem_r[:, 1, :], mem_r[:, 0, :], ACT.Sqrt, bias=EPS, scale=1.0 / D)\
               .then_inc(sem("mem_root"), 1)
            act.wait_ge(sem("mem_f_done"), ND)
            act.activation(mem_hi[:, :, :], mem_f[:, :, :], ACT.Copy).then_inc(sem("mem_hi_done"), 1)
            split(0)
            split(1)
            for d in range(ND):
                square(d, x[:, d, :], sem("x_made"), d + 1)

            def kv_evac(n, buf, last_unit):
                act.wait_ge(pe_unit, last_unit + 1)
                if n >= 2:
                    act.wait_ge(sem(f"kv_stored{n % 2}"), 16)
                act.activation(kv_out[n % 2][:, 0, :], ps[:, 2 * (buf % 4), :], ACT.Copy, scale=mem_r[:, 0, 0:1])
                act.activation(kv_out[n % 2][:, 1, :], ps[:, 2 * (buf % 4) + 1, :], ACT.Copy,
                               scale=mem_r[:, 0, 1:2]).then_inc(evac, 1)

            act.wait_ge(sem("mem_r_done"), 1)
            for u in range(16):
                if u == 3:
                    kv_evac(0, 0, 3)
                if u == 7:
                    kv_evac(1, 1, 7)
                if u == 8:
                    norm_root(0, B_N1)
                if u == 11:
                    kv_evac(2, 3, 11)
                if u == 15:
                    kv_evac(3, 4, 15)
                split(u + 2)
                if u >= 8:
                    norm_hi(0, u - 8)

            def ffn_up(n, u0, b0):
                with act.Fori(0, NF // 2) as i:
                    for k in range(4):
                        j = k // 2
                        if k % 2 == 0:
                            act.wait_ge(pe_unit, i * 4 + (u0 + k + 1))
                            act.wait_ge(evac, i * 4 + (b0 + k - 2))
                            act.activation(halves(sig[j][:, :]), pair(b0 + k), ACT.Sigmoid)\
                               .then_inc(sem("sig_done"), 1)
                            split(u0 + k + 2, i, 4)
                        else:
                            split(u0 + k + 2, i, 4)
                            act.wait_ge(evac, i * 4 + (b0 + k + 1))
                            act.activation(h_hi[:, bass.ds(i * 2 + j, 1), :].rearrange("p a t -> p (a t)"),
                                           hf[j][:, :], ACT.Copy).then_inc(sem("hh_done"), 1)

            def ffn_down(u0, b0, r0, last):
                def body(i, splits):
                    for k in range(12):
                        if k % 3 == 2:
                            d = k // 3
                            square(r0 + d, x[:, bass.ds(i * 4 + d, 1), :].rearrange("p a t -> p (a t)"), evac,
                                   i * 4 + (b0 + d + 1), i, 4)
                        if k < splits:
                            split(u0 + k + 2, i, 12)
                if last:
                    body(0, 12)
                    for k in range(12):
                        if k % 3 == 2:
                            d = k // 3
                            square(r0 + 4 + d, x[:, 4 + d, :], evac, b0 + 4 + d + 1)
                        if k < 10:
                            split(u0 + 12 + k + 2)
                else:
                    with act.Fori(0, 2) as i:
                        body(i, 12)

            def residual(u0, b0, r0):
                with act.Fori(0, 2) as i:
                    for k in range(4):
                        square(r0 + k, x[:, bass.ds(i * 4 + k, 1), :].rearrange("p a t -> p (a t)"), evac,
                               i * 4 + (b0 + k + 1), i, 4)
                        split(u0 + k + 2, i, 4)

            ffn_up(0, U_UP1, B_UP1)
            ffn_down(U_DN1, B_DN1, 8, False)
            norm(1, B_N2)
            split(U_IN + 2)
            split(U_IN + 3)
            with act.Fori(0, 7) as i:
                for k in range(4):
                    split(U_IN + 2 + k + 2, i, 4)

            lv_t = lv_e
            act.wait_ge(sem("y_gates"), 1)
            link(act.activation(lv_t[:, :, :], decay[:, :, :], ACT.Abs))
            link(act.activation(rows[:, R_T, :], rows[:, R_W, :], ACT.Abs))
            link(act.activation(lv_t[:, :, :], lv_t[:, :, :], ACT.Exp, scale=-1.0))
            link(act.activation(rows[:, R_T, :], rows[:, R_T, :], ACT.Exp, scale=-1.0))
            link(act.activation(lv_t[:, :, :], lv_t[:, :, :], ACT.Ln, bias=1.0))
            act.activation(rows[:, R_T, :], rows[:, R_T, :], ACT.Ln, bias=1.0).then_inc(sem("log_done"), 1)
            act.wait_ge(sem("rows_made"), 1)
            act.activation(rows[:, R_WI, :], rows[:, R_WI, :], ACT.Exp).then_inc(sem("rows_exp"), 1)
            act.activation(rows[:, R_EM, :], rows[:, R_M, :], ACT.Exp, scale=-1.0).then_inc(sem("rows_exp"), 1)
            act.activation(rows[:, R_WL, :], rows[:, R_WL, :], ACT.Exp).then_inc(sem("rows_exp"), 1)
            for n in range(LEVELS + 1):
                act.wait_ge(sem("lv_diff"), n + 1)
                act.activation(lv_e[:, :, :], lv_e[:, :, :], ACT.Exp, scale=1.0 / TAU).then_inc(sem("lv_exp"), 1)
            for n in range(2):
                act.wait_ge(sem("in_diff"), n + 1)
                act.activation(lv_e[:, :, :], lv_e[:, :, :], ACT.Exp, scale=1.0 / TAU).then_inc(sem("in_exp"), 1)
            link(act.activation(z[:, Z_MO:Z_MO + 4, :], z[:, Z_MO:Z_MO + 4, :], ACT.Sigmoid))
            act.wait_ge(sem("levels_done"), 1)
            for j in range(4):
                if j >= 2:
                    act.wait_ge(sem("gg_done"), j - 1)
                act.activation(sig[j % 2][:, :], z[:, Z_GG + j, :], ACT.Sigmoid).then_inc(sem("gg_sig"), 1)

            def chunk(c, n):
                act.wait_ge(sem("w_arg"), c + 1)
                act.activation(ew[0:n, :, 0:n], ew[0:n, :, 0:n], ACT.Exp).then_inc(sem("w_exp"), 1)
                act.wait_ge(sem("pe_a"), 9 * c + 6)
                act.activation(v_tok[0:n, :, :], ps[0:n, 5, :].rearrange("p (h v) -> p h v", h=H), ACT.Copy)\
                   .then_inc(sem("tok_done"), 1)
                act.wait_ge(sem("pe_a"), 9 * c + 7)
                act.activation(gk_tok[0:n, :, :], ps[0:n, 6, 0:256].rearrange("p (h v) -> p h v", h=2), ACT.Copy)\
                   .then_inc(sem("tok_done"), 1)
                act.wait_ge(sem("pe_a"), 9 * c + 9)
                act.activation(gv_tok[0:n, :, :], ps[0:n, 7, :].rearrange("p (h v) -> p h v", h=H), ACT.Copy)\
                   .then_inc(sem("tok_done"), 1)
                act.wait_ge(sem("den_mm"), c + 1)
                act.activation(den[:, :, 0:n], ps[:, 3, 0:H * n].rearrange("p (h t) -> p h t", h=H), ACT.Abs)\
                   .then_inc(sem("den_abs"), 1)
                if c < NC:
                    act.wait_ge(sem("gla_mm"), c + 1)
                else:
                    act.wait_ge(sem("o_s"), H)
                act.activation(z[:, Z_GV:Z_GV + H, c * L:c * L + n],
                               ps[:, 7 if c < NC else 1, 0:H * n].rearrange("p (h t) -> p h t", h=H), ACT.Copy)\
                   .then_inc(sem("gla_out"), 1)

            for c in range(NC):
                chunk(c, L)
            chunk(NC, NS)

            for j in range(2 * H):
                src = z[:, Z_MQ + j, :] if j < H else z[:, Z_GV + j - H, :]
                if j == 0:
                    act.wait_ge(sem("chunk_done"), NC + 1)
                    act.wait_ge(sem("gla_out"), NC + 1)
                if j >= 2:
                    act.wait_ge(sem("hn_mm"), j - 1)
                act.activation(sq[j % 2][:, :], src, ACT.Square).then_inc(sem("hn_sq"), 1)
                if j >= 1:
                    act.wait_ge(sem("hn_mm"), j)
                    if j >= 3:
                        act.wait_ge(sem("hn_y"), j - 2)
                    act.activation(halves(sig[(j - 1) % 2][:, :]), pair(j - 1), ACT.Sqrt, bias=EPS, scale=1.0 / DV)\
                       .then_inc(sem("hn_root"), 1)
            act.wait_ge(sem("hn_mm"), 8)
            act.wait_ge(sem("hn_y"), 6)
            act.activation(halves(sig[1][:, :]), pair(7), ACT.Sqrt, bias=EPS, scale=1.0 / DV)\
               .then_inc(sem("hn_root"), 1)
            act.wait_ge(sem("mixer_stored"), 1)
            for j in range(2 * H):
                act.wait_ge(sem("hn_y"), j + 1)
                act.activation(xn_hi[:, j, :], z[:, Z_MQ + j, :] if j < H else z[:, Z_GV + j - H, :], ACT.Copy)\
                   .then_inc(sem("ym_hi"), 1)
            residual(U_OUT, B_OUT, 16)
            norm(2, B_N3)
            with act.Fori(0, 2) as i:
                for k in range(4):
                    split(U_XQ + k + 2, i, 4)

            def exp_rows(n_mx, heads, scores, dst):
                for h in range(heads):
                    ins = act.activation(dst(h), scores(h), ACT.Exp, bias=xmx[:, h:h + 1], scale=1.0 / 16,
                                         accum_out=xmx[:, 4 + h:5 + h])
                ins.then_inc(sem("x_exp"), 1)

            act.wait_ge(sem("kT_mm"), 1)
            act.activation(kT[0][:, 0:4, :], ps[:, 0:2, :].rearrange("p b (k m) -> p (b k) m", k=2), ACT.Copy)\
               .then_inc(sem("kT_act"), 1)
            for tb in range(NC):
                act.wait_ge(sem("x_max"), tb + 1)
                if tb >= 2:
                    act.wait_ge(sem("pT_mm"), tb - 1)
                sc = ps[:, 4 * (tb % 2):4 * (tb % 2) + 2, :].rearrange("p b (k m) -> p (b k) m", k=2)
                exp_rows(tb, H, lambda h: sc[:, h, :], lambda h: prob[tb % 2][:, h, :])
                act.wait_ge(sem("av_mm"), tb + 1)
                q = 4 * (tb % 2)
                act.activation(xn_hi[:, :, tb * 128:tb * 128 + 128],
                               ps[:, q:q + 2, :].rearrange("p b (k t) -> p (b k) t", k=4), ACT.Copy)\
                   .then_inc(sem("av_hi"), 1)
            for b in range(B):
                act.wait_ge(sem("kT_mm"), b + 2)
                act.activation(kT[(b + 1) % 2][:, 0:4, :], ps[:, 0:2, :].rearrange("p b (k m) -> p (b k) m", k=2),
                               ACT.Copy).then_inc(sem("kT_act"), 1)
            act.wait_ge(sem("x_max"), NC + 1)
            exp_rows(NC, 1, lambda h: ps[:, 6, 0:MEM], lambda h: prob[0][:, 0, :])
            act.wait_ge(sem("sav_mm"), B)
            act.activation(xn_hi[:, :, TP:T], ps[:, 5, 0:ND * NS].rearrange("p (k t) -> p k t", k=ND), ACT.Copy)\
               .then_inc(sem("av_hi"), 1)

            residual(U_XO, B_XO, 24)
            norm(3, B_N4)
            ffn_up(1, U_UP2, B_UP2)
            ffn_down(U_DN2, B_DN2, 32, True)
            norm_root(4, B_N5)
            for c in range(NC + 1):
                n = L if c < NC else NS
                act.wait_ge(sem("yT_mm"), c + 1)
                q = 2 * (c % 4)
                act.activation(y_tok[0:n, c, :].rearrange("p (b f) -> p b f", b=2), ps[0:n, q:q + 2, :], ACT.Copy)\
                   .then_inc(sem("y_copied"), 1)

        @block.vector
        def _(dve):
            pe_unit, evac = sem("pe_unit"), sem("evac")
            steps = [0]

            def link(ins):
                steps[0] += 1
                ins.then_inc(sem("dve_chain"), 1)
                dve.wait_ge(sem("dve_chain"), steps[0])

            def split(u0, i=0, per=0):
                dve.wait_ge(sem("hi_done"), i * per + (u0 + 1))
                dve.tensor_tensor(w_lo[u0 % 2][:, :], raw[u0 % 4][:, :], w_hi[u0 % 2][:, :].bitcast(F32),
                                  ALU.subtract).then_inc(sem("lo_done"), 1)

            def add_square(r, i=0, per=0):
                dve.wait_ge(sem("sq_done"), i * per + (r + 1))
                if not (r == 0):
                    dve.wait_ge(sem("acc_done"), i * per + r)
                dve.tensor_tensor(acc[:, :], acc[:, :], sq[r % 2][:, :], ALU.add).then_inc(sem("acc_done"), 1)

            def norm_begin(g, buf):
                dve.wait_ge(evac, buf + 1)
                dve.memset(acc[:, :], 0.0)
                link(dve.reciprocal(rinv[:, :], sig[0][:, :]))

            def norm_scale(g, gain, d):
                if d < ND:
                    if d >= 2:
                        dve.wait_ge(sem("xnl_done"), 8 * g + d - 1)
                    dve.scalar_tensor_tensor(out=hf[d % 2][:, :], in0=x[:, d, :],
                                             scalar=gains[:, gain + d:gain + d + 1], in1=rinv[:, :], op0=ALU.mult,
                                             op1=ALU.mult).then_inc(sem("xf_done"), 1)
                if d >= 1:
                    dve.wait_ge(sem("xnh_done"), 8 * g + d)
                    dve.tensor_tensor(xn_lo[:, d - 1, :], hf[(d - 1) % 2][:, :], xn_hi[:, d - 1, :].bitcast(F32),
                                      ALU.subtract).then_inc(sem("xnl_done"), 1)

            def norm(g, gain, buf):
                norm_begin(g, buf)
                for d in range(ND + 1):
                    norm_scale(g, gain, d)

            link(dve.memset(acc[:, :], 0.0))
            dve.wait_ge(sem("gain_mm"), 1)
            link(dve.tensor_copy(gains[:, :], ps[:, 7, 0:N_GAIN]))
            for d in range(ND):
                dve.wait_ge(sem("memT_mm"), 2 * (d // 2) + 2)
                dve.tensor_scalar(mem_f[:, d, :], ps[:, d // 2, MEM * (d % 2):MEM * (d % 2) + MEM],
                                  gains[:, G_MEM + d:G_MEM + d + 1], None, ALU.mult).then_inc(sem("mem_f_done"), 1)
            dve.wait_ge(sem("mem_root"), 1)
            dve.reciprocal(mem_r[:, 0, :], mem_r[:, 1, :]).then_inc(sem("mem_r_done"), 1)
            dve.wait_ge(sem("mem_hi_done"), 1)
            dve.tensor_tensor(mem_lo[:, :, :], mem_f[:, :, :], mem_hi[:, :, :].bitcast(F32), ALU.subtract)\
               .then_inc(sem("mem_lo_done"), 1)
            split(0)
            split(1)
            for d in range(ND):
                q = 4 + 2 * (d % 2)
                dve.wait_ge(sem("xT_mm"), d + 1)
                dve.tensor_copy(x[:, d, 0:TP], ps[:, q, :])
                dve.tensor_copy(x[:, d, TP:T], ps[:, q + 1, 0:NS]).then_inc(sem("x_made"), 1)
                if d >= 1:
                    add_square(d - 1)
            add_square(ND - 1)
            for u in range(16):
                if u == 8:
                    norm_begin(0, B_N1)
                split(u + 2)
                if u >= 8:
                    norm_scale(0, G_FFN1, u - 8)
            norm_scale(0, G_FFN1, ND)

            def ffn_up(n, u0, b0):
                p0 = NF * n
                with dve.Fori(0, NF // 2) as i:
                    for k in range(4):
                        j = k // 2
                        if k % 2 == 0:
                            dve.wait_ge(sem("sig_done"), i * 2 + (p0 + j + 1))
                            dve.tensor_tensor(halves(sig[j][:, :]), pair(b0 + k), halves(sig[j][:, :]), ALU.mult)\
                               .then_inc(evac, 1)
                            split(u0 + k + 2, i, 4)
                        else:
                            dve.wait_ge(pe_unit, i * 4 + (u0 + k + 1))
                            dve.wait_ge(evac, i * 4 + (b0 + k))
                            dve.tensor_tensor(halves(hf[j][:, :]), pair(b0 + k), halves(sig[j][:, :]), ALU.mult)\
                               .then_inc(evac, 1)
                            split(u0 + k + 2, i, 4)
                            dve.wait_ge(sem("hh_done"), i * 2 + (p0 + j + 1))
                            fb = bass.ds(i * 2 + j, 1)
                            dve.tensor_tensor(h_lo[:, fb, :].rearrange("p a t -> p (a t)"), hf[j][:, :],
                                              h_hi[:, fb, :].bitcast(F32).rearrange("p a t -> p (a t)"),
                                              ALU.subtract).then_inc(sem("hl_done"), 1)

            def add_block(d, buf, scale):
                dve.scalar_tensor_tensor(out=halves(x[:, d, :].rearrange("p a t -> p (a t)")), in0=pair(buf),
                                         scalar=scale, in1=halves(x[:, d, :].rearrange("p a t -> p (a t)")),
                                         op0=ALU.mult, op1=ALU.add).then_inc(evac, 1)

            def ffn_down(u0, b0, r0, last):
                def body(i, i0, splits):
                    for k in range(12):
                        if k % 3 == 2:
                            d = k // 3
                            dve.wait_ge(pe_unit, i * 12 + (u0 + 12 * i0 + k + 1))
                            at_d = bass.ds(i * 4 + (4 * i0 + d), 1) if not i0 else slice(4 * i0 + d, 4 * i0 + d + 1)
                            add_block(at_d, b0 + 4 * i0 + d, 0.5)
                        if k < splits:
                            split(u0 + 12 * i0 + k + 2, i, 12)
                        if k % 3 == 2:
                            add_square(r0 + 4 * i0 + k // 3, i, 4)
                if last:
                    body(0, 0, 12)
                    body(0, 1, 10)
                else:
                    with dve.Fori(0, 2) as i:
                        body(i, 0, 12)

            def residual(u0, b0, r0):
                with dve.Fori(0, 2) as i:
                    for k in range(4):
                        dve.wait_ge(pe_unit, i * 4 + (u0 + k + 1))
                        add_block(bass.ds(i * 4 + k, 1), b0 + k, 1.0)
                        split(u0 + k + 2, i, 4)
                        add_square(r0 + k, i, 4)

            ffn_up(0, U_UP1, B_UP1)
            ffn_down(U_DN1, B_DN1, 8, False)
            norm(1, G_MIX, B_N2)

            def z_block(k, i=0):
                dve.wait_ge(pe_unit, i * 4 + (U_IN + k + 1))
                dst = z[:, k:k + 1, :] if isinstance(i, int) else z[:, bass.ds(i * 4 + k, 1), :]
                dve.tensor_copy(halves(dst.rearrange("p a t -> p (a t)")), pair(B_IN + k)).then_inc(evac, 1)

            for k in range(2):
                z_block(k)
                split(U_IN + k + 2)
            with dve.Fori(0, 7) as i:
                for k in range(4):
                    z_block(2 + k, i)
                    split(U_IN + 2 + k + 2, i, 4)
            dve.wait_ge(evac, B_IN + NZ)

            def row(r, lo=0, hi=T):
                return rows[:, r, lo:hi]

            def by_chunk(r):
                return rows[:, r, 0:TP].rearrange("p (c t) -> p c t", c=NC)

            def by_seq(r):
                return rows[:, r, TP:T].rearrange("p (b t) -> p b t", b=B)

            dve.wait_ge(sem("small_in"), 16 * 5)
            dve.tensor_scalar(row(R_U), z[0:H, Z_GATE, :], gate_b[0:H, 0:1], None, ALU.add)
            dve.tensor_scalar(row(R_W), z[32:32 + H, Z_GATE, :], gate_b[32:32 + H, 0:1], None, ALU.add)
            dve.wait_ge(sem("a2_mm"), 1)
            dve.tensor_scalar(halves(decay[:, 0, :]), ps[:, 0:2, 0:HT], gains[:, G_BA:G_BA + 1], None, ALU.add)
            dve.tensor_scalar(halves(decay[:, 1, :]), ps[:, 2:4, 0:HT], gains[:, G_BA + 1:G_BA + 2], None, ALU.add)\
               .then_inc(sem("y_gates"), 1)
            dve.wait_ge(sem("log_done"), 1)
            link(dve.scalar_tensor_tensor(out=row(R_W), in0=row(R_W), scalar=0.0, in1=row(R_T), op0=ALU.min,
                                          op1=ALU.subtract))
            link(dve.scalar_tensor_tensor(out=lv_e[:, :, :], in0=decay[:, :, :], scalar=0.0, in1=lv_e[:, :, :],
                                          op0=ALU.min, op1=ALU.subtract))
            for n in range(2):
                dve.tensor_tensor_scan(decay[:, n, :], restart, lv_e[:, n, :], 0.0, ALU.mult, ALU.add)
            dve.tensor_tensor_scan(row(R_B), restart[0:H, :], row(R_W), 0.0, ALU.mult, ALU.add)
            link(dve.tensor_tensor_scan(row(R_M, 0, TP), row(R_W, 0, TP), row(R_U, 0, TP), 0.0, ALU.add, ALU.max))
            dve.memset(scan_in[:, 0, :, 0:1], -3.0e38)
            dve.tensor_copy(scan_in[:, 1, :, 0:1], m0[:, :].unsqueeze(2))
            dve.tensor_copy(scan_in[:, 0, :, 1:], by_seq(R_W))
            link(dve.tensor_copy(scan_in[:, 1, :, 1:], by_seq(R_U)))
            link(dve.tensor_tensor_scan(scan_in[:, 2, :, :].rearrange("p b t -> p (b t)"),
                                        scan_in[:, 0, :, :].rearrange("p b t -> p (b t)"),
                                        scan_in[:, 1, :, :].rearrange("p b t -> p (b t)"), 0.0, ALU.add, ALU.max))
            link(dve.tensor_copy(by_seq(R_M), scan_in[:, 2, :, 1:]))
            dve.wait_ge(sem("zeros_set"), 1)
            dve.tensor_tensor(row(R_U), row(R_U), row(R_B), ALU.subtract)
            dve.tensor_tensor(row(R_W), row(R_B), row(R_M), ALU.subtract)
            dve.tensor_copy(by_chunk(R_WI)[:, 1:NC, :],
                            by_chunk(R_M)[:, 0:NC - 1, L - 1:L].broadcast_to([H, NC - 1, L]))
            link(dve.tensor_copy(by_seq(R_WI), m0[:, :].unsqueeze(2).broadcast_to([H, B, TS])))
            dve.tensor_tensor(row(R_WI), row(R_WI), row(R_W), ALU.add)
            dve.tensor_tensor(by_chunk(R_WL), by_chunk(R_U), by_chunk(R_W)[:, :, L - 1:L].broadcast_to([H, NC, L]),
                              ALU.add)
            dve.tensor_tensor(by_seq(R_WL), by_seq(R_U), by_seq(R_W)[:, :, TS - 1:TS].broadcast_to([H, B, TS]),
                              ALU.add).then_inc(sem("rows_made"), 1)

            for n in range(LEVELS + 2):
                if n >= 2:
                    dve.wait_ge(sem("lv_mm"), n - 1)
                    dve.wait_ge(sem("lv_qk"), n - 1)
                if n >= 1:
                    half = 1 << (n - 1)
                    if half <= 16:
                        dst = lv_e[:, :, :].rearrange("p f t -> p (f t)").rearrange("p (b t) -> p b t", t=2 * half)
                        src = decay[:, :, :].rearrange("p f t -> p (f t)").rearrange("p (b t) -> p b t", t=2 * half)
                        link(dve.tensor_tensor(dst, src, src[:, :, half - 1:half].broadcast_to(list(src.shape)),
                                               ALU.subtract))
                    else:
                        dst = lv_e[:, :, 0:TP].rearrange("p f (b t) -> p f b t", t=2 * half)
                        src = decay[:, :, 0:TP].rearrange("p f (b t) -> p f b t", t=2 * half)
                        link(dve.tensor_tensor(dst, src, src[:, :, :, half - 1:half].broadcast_to(list(src.shape)),
                                               ALU.subtract))
                    dve.scalar_tensor_tensor(out=lv_e[:, :, :], in0=lv_e[:, :, :], scalar=-1.0,
                                             in1=lv_e[:, :, :], op0=ALU.mult, op1=ALU.min)\
                       .then_inc(sem("lv_diff"), 1)
                    dve.wait_ge(sem("lv_exp"), n)
                    dve.tensor_tensor(lv_q[n % 2][:, :, :], z[:, Z_GQ:Z_GQ + 2, :], lv_e[:, :, :], ALU.mult)
                    dve.tensor_tensor(lv_k[n % 2][:, :, :], z[:, Z_GK:Z_GK + 2, :], lv_e[:, :, :], ALU.mult)\
                       .then_inc(sem("lv_qk"), 1)
                m = n - 1
                if m < 0:
                    continue
                dve.wait_ge(sem("lv_mm"), m + 1)
                if m >= 2:
                    dve.wait_ge(sem("lv_added"), m - 1)
                for r in range(2):
                    dst = (lv_acc if m == 0 else lv_tmp)[:, :, r::2, :]
                    src = ps[:, 2 * (m % 2) + r, :].rearrange("p (c k t) -> p c k t", c=NC, k=2)
                    mask = level_mask(m).unsqueeze(1).unsqueeze(1).broadcast_to([128, NC, 2, 64])
                    ins = dve.tensor_tensor(dst, src, mask, ALU.mult)
                ins.then_inc(sem("lv_masked"), 1)
            dve.wait_ge(sem("lv_added"), LEVELS - 1)
            dve.wait_ge(sem("lv_masked"), LEVELS + 1)
            dve.wait_ge(sem("zeros_set"), 1)
            for lo in (0, 64):
                dve.tensor_tensor(gla_a[lo:lo + 64, :, :, lo:lo + 64], lv_acc[lo:lo + 64, :, :, :],
                                  lv_tmp[lo:lo + 64, :, :, :], ALU.add)
            dve.wait_ge(sem("lv_mm"), LEVELS + 2)
            m = LEVELS + 1
            for r in range(2):
                link(dve.tensor_scalar(gla_a[0:64, :, r::2, 64:128],
                                       ps[0:64, 2 * (m % 2) + r, :].rearrange("p (c k t) -> p c k t", c=NC, k=2),
                                       GK ** -0.5, None, ALU.mult))
            for r in range(2):
                dve.tensor_tensor(s_ta[:, :, r, :, :],
                                  ps[0:NS, 4 + r, 0:3 * 2 * NS].rearrange("p (n k t) -> p n k t", n=3, k=2),
                                  const[0:NS, C_LEVEL:C_LEVEL + 192].rearrange("p (n t) -> p n t", n=3)[:, :, 0:NS]
                                  .unsqueeze(2).broadcast_to([NS, 3, 2, NS]), ALU.mult)\
                   .then_inc(sem("s_ta_done"), 1)
            dve.wait_ge(sem("s_ta_done"), 2)
            s_a_v = s_a[:, :, :].rearrange("p (k r) t -> p r k t", r=2)
            link(dve.tensor_tensor(s_a_v, s_ta[:, 0, :, :, :], s_ta[:, 1, :, :, :], ALU.add))
            link(dve.tensor_tensor(s_a_v, s_a_v, s_ta[:, 2, :, :, :], ALU.add))
            dve.tensor_copy(lv_e[:, :, :], decay[:, :, :]).then_inc(sem("in_diff"), 1)
            dve.wait_ge(sem("in_exp"), 1)
            link(dve.scalar_tensor_tensor(out=z[:, Z_GQ:Z_GQ + 2, :], in0=z[:, Z_GQ:Z_GQ + 2, :],
                                          scalar=GK ** -0.5, in1=lv_e[:, :, :], op0=ALU.mult, op1=ALU.mult))
            e_last = hf[0][:, 0:2 * (NC + B)].rearrange("p (f n) -> p f n", f=2)
            dve.tensor_copy(e_last[:, :, 0:NC], lv_e[:, :, L - 1:TP:L])
            link(dve.tensor_copy(e_last[:, :, NC:NC + B], lv_e[:, :, TP + TS - 1:T:TS]))
            for n in range(2):
                src = decay[:, n, 0:TP].rearrange("p (c t) -> p c t", c=NC)
                dve.tensor_tensor(lv_e[:, n, 0:TP].rearrange("p (c t) -> p c t", c=NC),
                                  src[:, :, L - 1:L].broadcast_to([128, NC, L]), src, ALU.subtract)
                src = decay[:, n, TP:T].rearrange("p (b t) -> p b t", b=B)
                ins = dve.tensor_tensor(lv_e[:, n, TP:T].rearrange("p (b t) -> p b t", b=B),
                                        src[:, :, TS - 1:TS].broadcast_to([128, B, TS]), src, ALU.subtract)
            ins.then_inc(sem("in_diff"), 1)
            dve.wait_ge(sem("in_exp"), 2)
            dve.tensor_tensor(z[:, Z_GK:Z_GK + 2, :], z[:, Z_GK:Z_GK + 2, :], lv_e[:, :, :], ALU.mult)
            link(dve.memset(s_q[:, :, :, :], 0.0))
            for r in range(2):
                ins = dve.tensor_copy(s_q[64 * r:64 * r + 64, r, :, :], z[64 * r:64 * r + 64, Z_GQ:Z_GQ + 2, TP:T])
            ins.then_inc(sem("levels_done"), 1)
            for j in range(4):
                dve.wait_ge(sem("gg_sig"), j + 1)
                dve.tensor_tensor(z[:, Z_GG + j, :], z[:, Z_GG + j, :], sig[j % 2][:, :], ALU.mult)\
                   .then_inc(sem("gg_done"), 1)

            def chunk_weights(c, n):
                t0 = c * L
                dve.wait_ge(sem("pe_a"), 9 * c + 1)
                link(dve.tensor_copy(ucol[0:n, :], ps[0:n, 6, 256:256 + 2 * H]))
                dve.wait_ge(sem("pe_a"), 9 * c + 2)
                for h in range(H):
                    ins = dve.tensor_scalar(ew[0:n, h, 0:n], ps[0:n, 0, h * n:h * n + n], ucol[0:n, h:h + 1], 0.0,
                                            ALU.add, ALU.min)
                ins.then_inc(sem("w_arg"), 1)
                dve.wait_ge(sem("pe_a"), 9 * c + 3)
                wi = ps[:, 1, 0:H * n].rearrange("p (h t) -> p h t", h=H)
                dve.tensor_copy(il[:, :], wi[:, :, n - 1])
                dve.tensor_tensor(q_in[:, :, 0:n], wi, z[:, Z_MQ:Z_MQ + H, t0:t0 + n], ALU.mult)\
                   .then_inc(sem("q_in_done"), 1)
                dve.wait_ge(sem("pe_a"), 9 * c + 5)
                for h in range(H):
                    ins = dve.tensor_scalar(kw_tok[0:n, h, :], ps[0:n, 4, h * DK:(h + 1) * DK],
                                            ucol[0:n, H + h:H + h + 1], DK ** -0.5, ALU.mult, ALU.mult)
                ins.then_inc(sem("kw_done"), 1)
                dve.wait_ge(sem("w_masked"), c + 1)
                dve.wait_ge(sem("pe_a"), 9 * c + 4)
                dve.scalar_tensor_tensor(out=pw[0:n, :, 0:n], in0=ps[0:n, 3, 0:H * n]
                                         .rearrange("p (h t) -> p h t", h=H), scalar=DK ** -0.5,
                                         in1=ew[0:n, :, 0:n], op0=ALU.mult, op1=ALU.mult).then_inc(sem("p_done"), 1)

            def chunk_heads(c, n):
                t0 = c * L
                dve.wait_ge(sem("pe_a"), 9 * c + 8)
                dve.wait_ge(sem("den_abs"), c + 1)
                if c < NC:
                    dve.wait_ge(sem("num_mm"), c + 1)
                else:
                    dve.wait_ge(sem("num_s"), H)
                link(dve.tensor_tensor(den[:, :, 0:n], ps[:, 2, 0:H * n].rearrange("p (h t) -> p h t", h=H),
                                       den[:, :, 0:n], ALU.max))
                link(dve.reciprocal(den[:, :, 0:n], den[:, :, 0:n]))
                dve.tensor_tensor(z[:, Z_MQ:Z_MQ + H, t0:t0 + n],
                                  ps[:, 0, 0:H * n].rearrange("p (h t) -> p h t", h=H), den[:, :, 0:n], ALU.mult)

            for c in range(NC):
                chunk_weights(c, L)
                chunk_heads(c, L)
                dve.wait_ge(sem("state_mm"), c + 1)
                if c == 0:
                    dve.tensor_copy(c_st[:, :, :], ps[:, 4, :].rearrange("p (h v) -> p h v", h=H))
                    dve.tensor_copy(n_st[:, :, :], ps[:, 5, :].rearrange("p (h v) -> p h v", h=H))
                    for h in range(H):
                        r = 64 * (h % 2)
                        ins = dve.tensor_copy(s_st[r:r + 64, h, :], ps[r:r + 64, 6, h * DV:(h + 1) * DV])
                else:
                    for h in range(H):
                        dve.scalar_tensor_tensor(out=c_st[:, h, :], in0=c_st[:, h, :], scalar=il[:, h:h + 1],
                                                 in1=ps[:, 4, h * DV:(h + 1) * DV], op0=ALU.mult, op1=ALU.add)
                        dve.scalar_tensor_tensor(out=n_st[:, h, :], in0=n_st[:, h, :], scalar=il[:, h:h + 1],
                                                 in1=ps[:, 5, h * 128:(h + 1) * 128], op0=ALU.mult, op1=ALU.add)
                        r = 64 * (h % 2)
                        ins = dve.scalar_tensor_tensor(out=s_st[r:r + 64, h, :], in0=s_st[r:r + 64, h, :],
                                                 scalar=e_last[r:r + 64, h // 2, c:c + 1],
                                                 in1=ps[r:r + 64, 6, h * DV:(h + 1) * DV], op0=ALU.mult, op1=ALU.add)
                ins.then_inc(sem("chunk_done"), 1)
                dve.wait_ge(sem("chunk_done"), c + 1)

            c, n = NC, NS
            chunk_weights(c, n)
            dve.wait_ge(sem("n_mm"), 1)
            link(dve.tensor_copy(s_n[:, :, :], ps[:, 6, 300:300 + NS].rearrange("p (b h) -> p b h", b=B)))
            dve.tensor_tensor(s_qn[:, :, :].rearrange("p h (b t) -> p h b t", b=B),
                              q_in[:, :, 0:NS].rearrange("p h (b t) -> p h b t", b=B),
                              s_n[:, :, :].rearrange("p b h -> p h b").unsqueeze(3).broadcast_to([128, H, B, TS]),
                              ALU.mult).then_inc(sem("qn_done"), 1)
            il_s = rinv[:, 0:H * B].rearrange("p (h b) -> p h b", h=H)
            dve.tensor_copy(il_s, ps[:, 1, 0:H * n].rearrange("p (h b t) -> p h b t", h=H, b=B)[:, :, :, TS - 1])\
               .then_inc(sem("il_s_done"), 1)
            dve.wait_ge(sem("il_s_done"), 1)

            def own_values(u):
                if u >= 2:
                    dve.wait_ge(sem("upd_mm"), u - 1)
                src = (v_tok if u < H else gv_tok)[0:NS, u % H, :]
                dve.tensor_tensor(v_own[u % 2][:, :, :], src.unsqueeze(1).broadcast_to([NS, B, DV]),
                                  own.unsqueeze(2).broadcast_to([NS, B, DV]), ALU.mult).then_inc(sem("v_own"), 1)

            def in_banks(t3d):
                return t3d.rearrange("p b v -> p (b v)").rearrange("p (k f) -> p k f", k=2)

            dve.wait_ge(sem("tok_done"), 3 * c + 3)
            for h in range(H):
                own_values(h)
                st = ring[h % 3]
                dve.wait_ge(sem(f"state_in{h % 3}"), 16 * (h // 3 + 1))
                dve.wait_ge(sem("num_s"), h + 1)
                link(dve.tensor_tensor(st[:, :, :], st[:, :, :], il_s[:, h, :].unsqueeze(2).broadcast_to([128, B, DV]),
                                       ALU.mult))
                dve.wait_ge(sem("upd_mm"), h + 1)
                q = 4 + 2 * (h % 2)
                dve.tensor_tensor(in_banks(st[:, :, :]), ps[:, q:q + 2, :], in_banks(st[:, :, :]), ALU.add)\
                   .then_inc(sem("upd_free"), 1)
            dve.wait_ge(sem("nnew_mm"), 1)
            link(dve.tensor_tensor(s_n2[:, :, :], s_n[:, :, :], il_s.rearrange("p h b -> p b h"), ALU.mult))
            dve.tensor_tensor(s_n2[:, :, :].rearrange("p b h -> p h b"),
                              ps[:, 3, 256:256 + H * B].rearrange("p (h b) -> p h b", h=H),
                              s_n2[:, :, :].rearrange("p b h -> p h b"), ALU.add).then_inc(sem("n2_done"), 1)
            dve.wait_ge(sem("n2_mm"), 1)
            dve.tensor_copy(s_nrow2[:, :], ps[0:NS, 3, 384:384 + DK]).then_inc(sem("n_new"), 1)
            chunk_heads(c, n)
            for h in range(H):
                u, r, st = H + h, 64 * (h % 2), ring[(H + h // 2) % 3]
                own_values(u)
                dve.wait_ge(sem(f"state_in{(H + h // 2) % 3}"), 32)
                dve.wait_ge(sem("o_s"), 2 * (h // 2) + 2)
                link(dve.tensor_tensor(st[r:r + 64, :, :], st[r:r + 64, :, :],
                                       e_last[r:r + 64, h // 2, NC:NC + B].unsqueeze(2).broadcast_to([64, B, DV]),
                                       ALU.mult))
                dve.wait_ge(sem("upd_mm"), u + 1)
                q = 4 + 2 * (u % 2)
                dve.tensor_tensor(in_banks(st[r:r + 64, :, :]), ps[r:r + 64, q:q + 2, :],
                                  in_banks(st[r:r + 64, :, :]), ALU.add).then_inc(sem("upd_free"), 1)
            dve.wait_ge(sem("upd_free"), 2 * H)
            dve.sem_inc(sem("chunk_done"), 1)

            for j in range(2 * H):
                hz = z[:, Z_MQ + j, :] if j < H else z[:, Z_GV + j - H, :]
                og = z[:, Z_MO + j, :] if j < H else z[:, Z_GG + j - H, :]
                gc = G_ML + j if j < H else G_GLA + j - H
                dve.wait_ge(sem("hn_root"), j + 1)
                link(dve.reciprocal(hf[j % 2][:, :], sig[j % 2][:, :]))
                link(dve.scalar_tensor_tensor(out=hf[j % 2][:, :], in0=hf[j % 2][:, :], scalar=gains[:, gc:gc + 1],
                                              in1=og, op0=ALU.mult, op1=ALU.mult))
                dve.tensor_tensor(hz, hz, hf[j % 2][:, :], ALU.mult).then_inc(sem("hn_y"), 1)
            for j in range(2 * H):
                hz = z[:, Z_MQ + j, :] if j < H else z[:, Z_GV + j - H, :]
                dve.wait_ge(sem("ym_hi"), j + 1)
                dve.tensor_tensor(xn_lo[:, j, :], hz, xn_hi[:, j, :].bitcast(F32), ALU.subtract)\
                   .then_inc(sem("ym_lo"), 1)
            residual(U_OUT, B_OUT, 16)
            norm(2, G_XA, B_N3)
            with dve.Fori(0, 2) as i:
                for k in range(4):
                    dve.wait_ge(pe_unit, i * 4 + (U_XQ + k + 1))
                    dve.tensor_copy(halves(xq[:, bass.ds(i * 4 + k, 1), :].rearrange("p a t -> p (a t)")),
                                    pair(B_XQ + k)).then_inc(evac, 1)
                    split(U_XQ + k + 2, i, 4)

            def softmax_max(scores, heads):
                link(dve.tensor_reduce(xmx[:, 8:8 + heads], scores, AX.X, ALU.max))
                dve.tensor_scalar(xmx[:, 0:heads], xmx[:, 8:8 + heads], -1.0 / 16, None, ALU.mult)\
                   .then_inc(sem("x_max"), 1)

            def softmax_scale(k, pr, heads):
                dve.wait_ge(sem("x_exp"), k + 1)
                link(dve.reciprocal(xmx[:, 8:8 + heads], xmx[:, 4:4 + heads]))
                for h in range(heads):
                    ins = dve.tensor_scalar(pr[:, h, :], pr[:, h, :], xmx[:, 8 + h:9 + h], None, ALU.mult)
                ins.then_inc(sem("p_ready"), 1)

            dve.wait_ge(sem("kT_mm"), 1)
            dve.tensor_copy(kT[0][:, 4:8, :], ps[:, 2:4, :].rearrange("p b (k m) -> p (b k) m", k=2))\
               .then_inc(sem("kT_dve"), 1)
            for tb in range(NC):
                q = 4 * (tb % 2)
                dve.wait_ge(sem("sc_mm"), tb + 1)
                sc = ps[:, q:q + 2, :].rearrange("p b (k m) -> p (b k) m", k=2)
                softmax_max(sc, H)
                softmax_scale(tb, prob[tb % 2], H)
                dve.wait_ge(sem("pT_mm"), tb + 1)
                dve.tensor_copy(probT[tb % 2][:, :, :], ps[:, q + 2:q + 4, :].rearrange("p b (k t) -> p (b k) t", k=4))\
                   .then_inc(sem("pT_copied"), 1)
                dve.wait_ge(sem("av_hi"), tb + 1)
                dve.tensor_tensor(xn_lo[:, :, tb * 128:tb * 128 + 128],
                                  ps[:, q:q + 2, :].rearrange("p b (k t) -> p (b k) t", k=4),
                                  xn_hi[:, :, tb * 128:tb * 128 + 128].bitcast(F32), ALU.subtract)\
                   .then_inc(sem("av_lo"), 1)
            for b in range(B):
                dve.wait_ge(sem("kT_mm"), b + 2)
                dve.tensor_copy(kT[(b + 1) % 2][:, 4:8, :], ps[:, 2:4, :].rearrange("p b (k m) -> p (b k) m", k=2))\
                   .then_inc(sem("kT_dve"), 1)
            dve.wait_ge(sem("ssc_mm"), 1)
            dve.tensor_copy(s_sc[:, :, :], ps[:, 4, 0:MEM].rearrange("p (m t) -> p m t", m=2))\
               .then_inc(sem("ssc_copied"), 1)
            dve.wait_ge(sem("sc_mm"), NC + 1)
            softmax_max(ps[:, 6, 0:MEM].unsqueeze(1), 1)
            softmax_scale(NC, prob[0], 1)
            dve.wait_ge(sem("pT_mm"), NC + 1)
            dve.tensor_copy(probT[0][:, 0:2, :], ps[:, 7, 0:MEM].rearrange("p (m t) -> p m t", m=2))\
               .then_inc(sem("pT_copied"), 1)
            dve.wait_ge(sem("av_hi"), NC + 1)
            dve.tensor_tensor(xn_lo[:, :, TP:T], ps[:, 5, 0:ND * NS].rearrange("p (k t) -> p k t", k=ND),
                              xn_hi[:, :, TP:T].bitcast(F32), ALU.subtract).then_inc(sem("av_lo"), 1)

            residual(U_XO, B_XO, 24)
            norm(3, G_FFN2, B_N4)
            ffn_up(1, U_UP2, B_UP2)
            ffn_down(U_DN2, B_DN2, 32, True)
            norm_begin(4, B_N5)
            for d in range(ND):
                dve.scalar_tensor_tensor(out=yf[:, d, :], in0=x[:, d, :], scalar=gains[:, G_FIN + d:G_FIN + d + 1],
                                         in1=rinv[:, :], op0=ALU.mult, op1=ALU.mult).then_inc(sem("yf_done"), 1)

        @block.tensor
        def _(pe):
            pe_unit, evac, lo_done = sem("pe_unit"), sem("evac"), sem("lo_done")

            def mm(out, lhsT, rhs, start=True, stop=True):
                return pe.matmul(out, lhsT, rhs, start=start, stop=stop)

            pe.wait_ge(sem("const_in"), 16)
            pe.wait_ge(sem("gains_in"), 16 * 9)
            pe.transpose(ps[:, 7, 0:N_GAIN], gain_rows[:, :], const[0:N_GAIN, 0:N_GAIN]).then_inc(sem("gain_mm"), 1)
            pe.wait_ge(sem("mem_in"), 16)
            for d in range(ND):
                for mb in range(2):
                    c = MEM * (d % 2) + 128 * mb
                    ins = pe.transpose(ps[:, d // 2, c:c + 128], mem_nat[:, mb, d * 128:d * 128 + 128], ident)
                ins.then_inc(sem("memT_mm"), 1)
            pe.wait_ge(sem("x_in"), 16)
            pe.wait_ge(sem("xs_in"), 16)
            for d in range(ND):
                q = 4 + 2 * (d % 2)
                if d == 1:
                    pe.wait_ge(sem("mem_f_done"), 1)
                if d >= 2:
                    pe.wait_ge(sem("x_made"), d - 1)
                for c in range(NC):
                    pe.transpose(ps[:, q, c * L:(c + 1) * L], xp_nat[:, c, d * 128:d * 128 + 128], ident)
                pe.transpose(ps[:, q + 1, 0:NS], xs_nat[:, d * 128:d * 128 + 128], const[0:NS, 0:NS])\
                  .then_inc(sem("xT_mm"), 1)

            def norm(g, buf):
                pe.wait_ge(sem("acc_done"), 8 * (g + 1))
                if buf >= 4:
                    pe.wait_ge(evac, buf - 3)
                mm(pair(buf)[:, 0, :], ones, acc[:, 0:HT])
                mm(pair(buf)[:, 1, :], ones, acc[:, HT:T]).then_inc(sem("norm_mm"), 1)

            pe.wait_ge(sem("mem_lo_done"), 1)
            pe.wait_ge(sem("x_made"), ND)
            for u in range(16):
                if u == 8:
                    norm(0, B_N1)
                pe.wait_ge(lo_done, u + 1)
                buf = (0, 1, 3, 4)[u // 4]
                if u == 12:
                    pe.wait_ge(evac, 1)
                for kt in range(2):
                    k = 2 * (u % 4) + kt
                    cols = slice(512 * kt, 512 * kt + 512)
                    for mb in range(2):
                        dst, toks = ps[:, 2 * (buf % 4) + mb, :], slice(128 * mb, 128 * mb + 128)
                        mm(dst, mem_hi[:, k, toks], w_hi[u % 2][:, cols], k == 0, False)
                        mm(dst, mem_hi[:, k, toks], w_lo[u % 2][:, cols], False, False)
                        ins = mm(dst, mem_lo[:, k, toks], w_hi[u % 2][:, cols], False, k == 7)
                ins.then_inc(pe_unit, 1)

            def unit(u, buf, hi, lo, k0, nk, first, last):
                for j in range(nk):
                    wh = w_hi[u % 2][:, 128 * j:128 * j + 128]
                    wl = w_lo[u % 2][:, 128 * j:128 * j + 128]
                    for n, (w, m) in enumerate(((wh, hi), (wh, lo), (wl, hi))):
                        for half in range(2):
                            ins = mm(ps[:, 2 * (buf % 4) + half, 0:HT], w, m[:, k0 + j, half * HT:(half + 1) * HT],
                                     first and j == 0 and n == 0, last and j == nk - 1 and n == 2)
                ins.then_inc(pe_unit, 1)

            def blocks(u0, b0, bodies):
                with pe.Fori(0, bodies) as i:
                    for k in range(4):
                        pe.wait_ge(lo_done, i * 4 + (u0 + k + 1))
                        pe.wait_ge(evac, i * 4 + (b0 + k - 3))
                        unit(u0 + k, b0 + k, xn_hi, xn_lo, 0, 8, True, True)

            def ffn_down(n, u0, b0):
                pe.wait_ge(sem("hl_done"), NF * (n + 1))
                with pe.Fori(0, 2) as i:
                    for k in range(12):
                        pe.wait_ge(lo_done, i * 12 + (u0 + k + 1))
                        if k % 3 == 0:
                            pe.wait_ge(evac, i * 4 + (b0 + k // 3 - 3))
                        lo, hi = DN_K[k % 3]
                        unit(u0 + k, b0 + k // 3, h_hi, h_lo, lo, hi - lo, k % 3 == 0, k % 3 == 2)

            pe.wait_ge(sem("xnl_done"), 8)
            pe.wait_ge(sem("kv_stored0"), 32)
            pe.wait_ge(sem("kv_stored1"), 32)
            blocks(U_UP1, B_UP1, NF // 2)
            ffn_down(0, U_DN1, B_DN1)
            norm(1, B_N2)
            pe.wait_ge(sem("xnl_done"), 16)
            for k in range(2):
                pe.wait_ge(lo_done, U_IN + k + 1)
                pe.wait_ge(evac, B_IN + k - 3)
                unit(U_IN + k, B_IN + k, xn_hi, xn_lo, 0, 8, True, True)
            blocks(U_IN + 2, B_IN + 2, 7)

            pe.wait_ge(evac, B_IN + NZ)
            pe.wait_ge(sem("small_in"), 16 * 5)
            for n in range(2):
                for half in range(2):
                    ins = mm(ps[:, 2 * n + half, 0:HT], a2w[:, 128 * n:128 * n + 128],
                             z[0:RANK, Z_GA, half * HT:(half + 1) * HT])
            ins.then_inc(sem("a2_mm"), 1)

            for n in range(LEVELS + 2):
                if n == 0:
                    q_, k_ = z[:, Z_GQ:Z_GQ + 2, :], z[:, Z_GK:Z_GK + 2, :]
                    pe.wait_ge(sem("y_gates"), 1)
                else:
                    q_, k_ = lv_q[n % 2][:, :, :], lv_k[n % 2][:, :, :]
                    pe.wait_ge(sem("lv_qk"), n)
                if n >= 2:
                    pe.wait_ge(sem("lv_masked"), n - 1)
                for r in range(2):
                    rr = slice(64 * r, 64 * r + 64)
                    bank = 2 * (n % 2) + r
                    for c in range(NC):
                        for pr in range(2):
                            at_ = (c * 2 + pr) * 64
                            if n <= LEVELS:
                                for j in range(2):
                                    tt = slice(c * L + 64 * j, c * L + 64 * j + 64)
                                    ins = mm(ps[64 * j:64 * j + 64, bank, at_:at_ + 64], k_[rr, pr, tt],
                                             q_[rr, pr, tt])
                            else:
                                ins = mm(ps[0:64, bank, at_:at_ + 64], k_[rr, pr, c * L:c * L + 64],
                                         q_[rr, pr, c * L + 64:c * L + 128])
                    if n <= 2:
                        for pr in range(2):
                            at_ = (n * 2 + pr) * NS
                            ins = mm(ps[0:NS, 4 + r, at_:at_ + NS], k_[rr, pr, TP:T], q_[rr, pr, TP:T])
                ins.then_inc(sem("lv_mm"), 1)

            def chunk_first(c, n):
                t0 = c * L
                tt = slice(t0, t0 + n)
                if c == 0:
                    pe.wait_ge(sem("levels_done"), 1)
                    pe.wait_ge(sem("rows_exp"), 3)
                else:
                    pe.wait_ge(sem("chunk_done"), c)
                    pe.wait_ge(sem("gla_out"), c)

                def spread(bank, r):
                    for h in range(H):
                        ins = mm(ps[:, bank, h * n:h * n + n], sel[:, h, :], rows[:, r, tt])
                    ins.then_inc(sem("pe_a"), 1)

                pe.transpose(ps[0:n, 6, 256:256 + H], rows[:, R_U, tt], const[0:H, 0:H])
                pe.transpose(ps[0:n, 6, 256 + H:256 + 2 * H], rows[:, R_WL, tt], const[0:H, 0:H])\
                  .then_inc(sem("pe_a"), 1)
                spread(0, R_W)
                spread(1, R_WI)
                for h in range(H):
                    ins = mm(ps[0:n, 3, h * n:h * n + n], z[:, Z_MK + h, tt], z[:, Z_MQ + h, tt])
                ins.then_inc(sem("pe_a"), 1)

                def to_tokens(bank, zb, blocks_):
                    for h in range(blocks_):
                        ins = pe.transpose(ps[0:n, bank, h * 128:h * 128 + 128], z[:, zb + h, tt], ident)
                    ins.then_inc(sem("pe_a"), 1)

                to_tokens(4, Z_MK, 4)
                to_tokens(5, Z_MV, 4)
                pe.wait_ge(sem("w_arg"), c + 1)
                to_tokens(6, Z_GK, 2)
                spread(2, R_EM)
                to_tokens(7, Z_GV, 4)

            for c in range(NC):
                chunk_first(c, L)
                tt = slice(c * L, c * L + L)
                pe.wait_ge(sem("q_in_done"), c + 1)
                pe.wait_ge(sem("kw_done"), c + 1)
                pe.wait_ge(sem("p_done"), c + 1)
                pe.wait_ge(sem("tok_done"), 3 * c + 3)
                for h in range(H):
                    hh = slice(h * L, h * L + L)
                    ins = mm(ps[:, 3, hh], ones, pw[:, h, :], True, c == 0)
                    if c:
                        ins = mm(ps[:, 3, hh], n_st[:, h, :], q_in[:, h, :], False, True)
                ins.then_inc(sem("den_mm"), 1)
                for h in range(H):
                    hh = slice(h * L, h * L + L)
                    ins = mm(ps[:, 0, hh], v_tok[:, h, :], pw[:, h, :], True, c == 0)
                    if c:
                        ins = mm(ps[:, 0, hh], c_st[:, h, :], q_in[:, h, :], False, True)
                ins.then_inc(sem("num_mm"), 1)
                for h in range(H):
                    hh = slice(h * L, h * L + L)
                    ins = mm(ps[:, 7, hh], gv_tok[:, h, :], gla_a[:, c, h, :], True, c == 0)
                    if c:
                        ins = mm(ps[:, 7, hh], s_st[:, h, :], z[:, Z_GQ + h // 2, tt], False, True)
                ins.then_inc(sem("gla_mm"), 1)
                for h in range(H):
                    mm(ps[:, 4, h * DV:(h + 1) * DV], kw_tok[:, h, :], v_tok[:, h, :])
                    mm(ps[:, 5, h * 128:(h + 1) * 128], kw_tok[:, h, :], ones)
                for pr in range(2):
                    ins = mm(ps[:, 6, 256 * pr:256 * pr + 256], gk_tok[:, pr, :],
                             gv_tok[:, 2 * pr:2 * pr + 2, :].rearrange("p h v -> p (h v)"))
                ins.then_inc(sem("state_mm"), 1)

            c, n = NC, NS
            chunk_first(c, n)
            pe.wait_ge(sem("n_in"), 16)
            pe.wait_ge(sem("tok_done"), 3 * c + 3)
            pe.transpose(ps[:, 6, 300:300 + NS], s_nrow[:, :], const[0:NS, 0:NS]).then_inc(sem("n_mm"), 1)
            pe.wait_ge(sem("kw_done"), c + 1)
            pe.wait_ge(sem("p_done"), c + 1)
            pe.wait_ge(sem("qn_done"), 1)
            for h in range(H):
                mm(ps[:, 3, h * n:h * n + n], const[0:NS, C_ONE:C_ONE + 128], pw[0:n, h, 0:n], True, False)
                ins = mm(ps[:, 3, h * n:h * n + n], ones, s_qn[:, h, :], False, True)
            ins.then_inc(sem("den_mm"), 1)

            def update(u, keys):
                pe.wait_ge(sem("v_own"), u + 1)
                if u >= 2:
                    pe.wait_ge(sem("upd_free"), u - 1)
                q = 4 + 2 * (u % 2)
                vo = v_own[u % 2][:, :, :].rearrange("p b v -> p (b v)")
                mm(ps[:, q, :], keys, vo[:, 0:512])
                mm(ps[:, q + 1, :], keys, vo[:, 512:1024]).then_inc(sem("upd_mm"), 1)

            for h in range(H):
                pe.wait_ge(sem(f"state_in{h % 3}"), 16 * (h // 3 + 1))
                mm(ps[:, 0, h * n:h * n + n], v_tok[0:n, h, :], pw[0:n, h, 0:n], True, False)
                for b in range(B):
                    s = h * n + TS * b
                    ins = mm(ps[:, 0, s:s + TS], ring[h % 3][:, b, :], q_in[:, h, TS * b:TS * b + TS], False,
                             b == B - 1)
                ins.then_inc(sem("num_s"), 1)
                update(h, kw_tok[0:n, h, :])
            pe.wait_ge(sem("den_abs"), c + 1)
            for h in range(H):
                ins = mm(ps[:, 3, 256 + h * B:256 + h * B + B], kw_tok[0:n, h, :], own)
            ins.then_inc(sem("nnew_mm"), 1)
            pe.wait_ge(sem("n2_done"), 1)
            pe.transpose(ps[0:NS, 3, 384:384 + DK], s_n2[:, :, :].rearrange("p b h -> p (b h)"), ident)\
              .then_inc(sem("n2_mm"), 1)
            pe.wait_ge(sem("il_s_done"), 1)
            for pr in range(2):
                slot = (H + pr) % 3
                pe.wait_ge(sem(f"state_in{slot}"), 32)
                for r in range(2):
                    h = 2 * pr + r
                    mm(ps[:, 1, h * n:h * n + n], gv_tok[0:n, h, :], s_a[:, h, :], True, False)
                    for b in range(B):
                        s = h * n + TS * b
                        ins = mm(ps[:, 1, s:s + TS], ring[slot][:, b, :], s_q[:, r, pr, TS * b:TS * b + TS], False,
                                 b == B - 1)
                    ins.then_inc(sem("o_s"), 1)
                for r in range(2):
                    update(H + 2 * pr + r, gk_tok[0:n, pr, :])

            pe.wait_ge(sem("chunk_done"), NC + 1)
            pe.wait_ge(sem("gla_out"), NC + 1)
            for j in range(2 * H):
                pe.wait_ge(sem("hn_sq"), j + 1)
                if j >= 4:
                    pe.wait_ge(sem("hn_root"), j - 3)
                for half in range(2):
                    ins = mm(pair(j)[:, half, :], ones, sq[j % 2][:, half * HT:(half + 1) * HT])
                ins.then_inc(sem("hn_mm"), 1)
            pe.wait_ge(sem("hn_root"), 2 * H)
            pe.wait_ge(sem("ym_lo"), 8)
            blocks(U_OUT, B_OUT, 2)
            norm(2, B_N3)
            pe.wait_ge(sem("xnl_done"), 24)
            blocks(U_XQ, B_XQ, 2)

            def transpose_k(n, buf):
                pe.wait_ge(sem(f"kv_in{buf % 3}"), 16 * (buf // 3 + 1))
                for k in range(ND):
                    for mb in range(2):
                        col = MEM * (k % 2) + 128 * mb
                        ins = pe.transpose(ps[:, k // 2, col:col + 128], kv[buf % 3][:, mb, k * 128:k * 128 + 128],
                                           ident)
                ins.then_inc(sem("kT_mm"), 1)

            def k_ready(n):
                pe.wait_ge(sem("kT_act"), n)
                pe.wait_ge(sem("kT_dve"), n)

            pe.wait_ge(evac, B_XQ + ND)
            transpose_k(0, 0)
            k_ready(1)

            def scores(tb):
                q = 4 * (tb % 2)
                if tb >= 2:
                    pe.wait_ge(sem("av_lo"), tb - 1)
                for h in range(H):
                    for dd in range(2):
                        ins = mm(ps[:, q + h // 2, MEM * (h % 2):MEM * (h % 2) + MEM],
                                 xq[:, 2 * h + dd, tb * 128:tb * 128 + 128], kT[0][:, 2 * h + dd, :], dd == 0, dd == 1)
                ins.then_inc(sem("sc_mm"), 1)

            scores(0)
            pe.wait_ge(sem("kv_in1"), 16)
            for tb in range(NC):
                if tb + 1 < NC:
                    scores(tb + 1)
                q = 4 * (tb % 2)
                pe.wait_ge(sem("p_ready"), tb + 1)
                for k in range(ND):
                    ins = pe.transpose(ps[:, q + 2 + k // 4, 128 * (k % 4):128 * (k % 4) + 128],
                                       prob[tb % 2][:, k // 2, 128 * (k % 2):128 * (k % 2) + 128], ident)
                ins.then_inc(sem("pT_mm"), 1)
                pe.wait_ge(sem("pT_copied"), tb + 1)
                for k in range(ND):
                    for mb in range(2):
                        ins = mm(ps[:, q + k // 4, 128 * (k % 4):128 * (k % 4) + 128],
                                 kv[1][:, mb, k * 128:k * 128 + 128], probT[tb % 2][:, 2 * (k // 2) + mb, :],
                                 mb == 0, mb == 1)
                ins.then_inc(sem("av_mm"), 1)
            pe.wait_ge(sem("av_lo"), NC)
            for b in range(B):
                transpose_k(b + 1, b + 2)
                k_ready(b + 2)
                kt = kT[(b + 1) % 2]
                for h in range(H):
                    for mb in range(2):
                        col = 128 * mb + TS * (H * b + h)
                        for dd in range(2):
                            ins = mm(ps[:, 4, col:col + TS], kt[:, 2 * h + dd, 128 * mb:128 * mb + 128],
                                     xq[:, 2 * h + dd, TP + TS * b:TP + TS * b + TS], dd == 0, dd == 1)
            ins.then_inc(sem("ssc_mm"), 1)
            pe.wait_ge(sem("ssc_copied"), 1)
            for mb in range(2):
                ins = pe.transpose(ps[:, 6, 128 * mb:128 * mb + 128], s_sc[:, mb, :], ident)
            ins.then_inc(sem("sc_mm"), 1)
            pe.wait_ge(sem("p_ready"), NC + 1)
            for mb in range(2):
                ins = pe.transpose(ps[:, 7, 128 * mb:128 * mb + 128], prob[0][:, 0, 128 * mb:128 * mb + 128], ident)
            ins.then_inc(sem("pT_mm"), 1)
            pe.wait_ge(sem("pT_copied"), NC + 1)
            for b in range(B):
                n = 10 + b
                pe.wait_ge(sem(f"kv_in{n % 3}"), 16 * (n // 3 + 1))
                for k in range(ND):
                    for mb in range(2):
                        col, row = NS * k + TS * b, TS * (H * b + k // 2)
                        ins = mm(ps[:, 5, col:col + TS], kv[n % 3][:, mb, k * 128:k * 128 + 128],
                                 probT[0][:, mb, row:row + TS], mb == 0, mb == 1)
                ins.then_inc(sem("sav_mm"), 1)

            pe.wait_ge(sem("av_lo"), NC + 1)
            blocks(U_XO, B_XO, 2)
            norm(3, B_N4)
            pe.wait_ge(sem("xnl_done"), 32)
            blocks(U_UP2, B_UP2, NF // 2)
            ffn_down(1, U_DN2, B_DN2)
            norm(4, B_N5)
            pe.wait_ge(evac, B_N5 + 1)
            for c in range(NC + 1):
                n = L if c < NC else NS
                if c == 4:
                    pe.wait_ge(sem("y_copied"), 1)
                for d in range(ND):
                    if c == 0:
                        pe.wait_ge(sem("yf_done"), d + 1)
                    ins = pe.transpose(ps[0:n, 2 * (c % 4) + d // 4, 128 * (d % 4):128 * (d % 4) + 128],
                                       yf[:, d, c * L:c * L + n], ident)
                ins.then_inc(sem("yT_mm"), 1)


_INS = ["x_prompt", "x_sample", "mem_prompt", "cache_mem_k", "cache_mem_v", "state_mlstm_c", "state_mlstm_n",
        "state_mlstm_m", "state_gla_s", "ffn1_norm_g", "ffn1_w_gate", "ffn1_w_up", "ffn1_w_down", "mix_norm_g",
        "w_in", "mlstm_b_i", "mlstm_b_f", "mlstm_out_g", "gla_w_a2", "gla_b_a", "gla_out_g", "w_out",
        "xattn_norm_g", "mem_norm_g", "xattn_w_q", "xattn_w_k", "xattn_w_v", "xattn_w_o", "ffn2_norm_g",
        "ffn2_w_gate", "ffn2_w_up", "ffn2_w_down", "final_norm_g"]
_OUTS = [("y_prompt", (1, TP, D)), ("y_sample", (B, TS, D)), ("mem_k", (1, 1, MEM, H, D // H)),
         ("mem_v", (1, 1, MEM, H, D // H)), ("mlstm_c_p", (1, 1, H, DK, DV)), ("mlstm_n_p", (1, 1, H, DK)),
         ("mlstm_m_p", (1, 1, H)), ("gla_s_p", (1, 1, H, GK, DV)), ("mlstm_c_s", (1, B, H, DK, DV)),
         ("mlstm_n_s", (1, B, H, DK)), ("mlstm_m_s", (1, B, H)), ("gla_s_s", (1, B, H, GK, DV))]


def _constants(np):
    c = np.zeros((128, N_CONST), np.float32)
    c[:, C_ID:C_ID + 128] = np.eye(128)
    c[:, C_ONE:C_ONE + 128] = 1.0
    s, t = np.arange(128)[:, None] % 64, np.arange(64)[None, :]
    for n in range(LEVELS + 1):
        if n == 0:
            mask = s == t
        else:
            half = 1 << (n - 1)
            mask = (s // (2 * half) == t // (2 * half)) & (s % (2 * half) < half) & (t % (2 * half) >= half)
        c[:, C_LEVEL + 64 * n:C_LEVEL + 64 * n + 64] = mask * GK ** -0.5
    s, t = np.arange(128)[:, None], np.arange(128)[None, :]
    c[:, C_CAUSAL:C_CAUSAL + 128] = s <= t
    t = np.arange(T)
    c[:, C_RESTART:C_RESTART + T] = np.where(t < TP, t % L != 0, t % TS != 0)
    s, t = np.arange(NS)[:, None], np.arange(NS)[None, :]
    c[0:NS, C_SCAUSAL:C_SCAUSAL + NS] = (s <= t) & (s // TS == t // TS)
    c[0:NS, C_OWN:C_OWN + B] = s // TS == np.arange(B)[None, :]
    sel = np.zeros((H, H * 128), np.float32)
    for h in range(H):
        sel[h, h * 128:(h + 1) * 128] = 1.0
    return c, sel


def kernel(**inputs):
    import numpy as _np
    import concourse.bacc as _bacc
    from concourse import mybir as _mybir
    from concourse.bass_utils import run_bass_kernel_spmd as _run

    nc = _bacc.Bacc("TRN2", target_bir_lowering=False, num_devices=1)
    given = {name: _np.ascontiguousarray(inputs[name]) for name in _INS}
    given["consts"], given["sel"] = _constants(_np)
    arrays, a, o = {}, {}, {}
    for name, value in given.items():
        arrays[f"in_{name}"] = value
        a[name] = nc.dram_tensor(f"in_{name}", value.shape, _mybir.dt.from_np(value.dtype), kind="ExternalInput").ap()
    for name, shape in _OUTS:
        o[name] = nc.dram_tensor(f"out_{name}", shape, _mybir.dt.float32, kind="ExternalOutput").ap()
    build(nc, a, o)
    r = _run(nc, [arrays], core_ids=[0])
    return tuple(r.results[0][f"out_{name}"] for name, _ in _OUTS)
```

```python
import concourse.bass as bass
from concourse import mybir
from contextlib import ExitStack

D = 1024
ND = D // 128
TP, B, TS = 512, 8, 4
NS = B * TS
T = TP + NS
HT = T // 2
FF = 2816
NF = FF // 128
H, DK, DV, GK = 4, 128, 128, 64
L = 128
NC = TP // L
MEM = 256
EPS = 1e-6
RANK = 16
LEVELS = 6
TAU = 16.0
Z_GA, Z_GATE, Z_GQ, Z_GK, Z_GV, Z_MQ, Z_MK, Z_MV, Z_MO, Z_GG, NZ = 0, 1, 2, 4, 6, 10, 14, 18, 22, 26, 30
COL_MQ, COL_MI, COL_MF, COL_MO, COL_GQ, COL_GA, COL_GG = 0, 1536, 1540, 1544, 2056, 3080, 3096
C_ID, C_ONE, C_LEVEL, C_CAUSAL = 0, 128, 256, 256 + (LEVELS + 1) * 64
C_RESTART = C_CAUSAL + 128
C_SCAUSAL = C_RESTART + T
C_OWN = C_SCAUSAL + NS
N_CONST = C_OWN + B
G_FFN1, G_MIX, G_XA, G_MEM, G_FFN2, G_FIN, G_ML, G_GLA, G_BA, N_GAIN = 0, 8, 16, 24, 32, 40, 48, 52, 56, 58
KV_RING = 5
UNIT = 1024
F32, F32R = mybir.dt.float32, mybir.dt.float32r
ALU, ACT, AX = mybir.AluOpType, mybir.ActivationFunctionType, mybir.AxisListType


def build(nc, a, o):
    ctx = ExitStack()
    with ctx:
        sems = {}

        def sem(name):
            if name not in sems:
                sems[name] = ctx.enter_context(nc.semaphore(name))
            return sems[name]

        base = (nc.sbuf_base + 63) // 64 * 64
        AT_X = base
        AT_XN = AT_X + ND * T * 4
        AT_H = AT_XN + 2 * ND * T * 4
        AT_W = AT_H + 2 * NF * T * 4
        AT_MISC = AT_W + 8 * UNIT * 4
        END = AT_MISC + 32000

        def at(name, shape, offset, dt=F32):
            size = 4
            for n in shape[1:]:
                size *= n
            assert offset + size <= END, name
            return nc.alloc_sbuf_tensor_at(name, shape, dt, offset=offset), (offset + size + 31) // 32 * 32

        x, _ = at("x", [128, ND, T], AT_X)
        xn_hi, p = at("xn_hi", [128, ND, T], AT_XN, F32R)
        xn_lo, _ = at("xn_lo", [128, ND, T], p, F32R)
        h_hi, p = at("h_hi", [128, NF, T], AT_H, F32R)
        h_lo, _ = at("h_lo", [128, NF, T], p, F32R)
        raw, w_hi, w_lo = [], [], []
        p = AT_W
        for n in range(4):
            t_, p = at(f"raw{n}", [128, UNIT], p)
            raw.append(t_)
        for n in range(2):
            t_, p = at(f"w_hi{n}", [128, UNIT], p, F32R)
            w_hi.append(t_)
            t_, p = at(f"w_lo{n}", [128, UNIT], p, F32R)
            w_lo.append(t_)
        p = AT_MISC
        const, p = at("const", [128, N_CONST], p)
        sel, p = at("sel", [H, H, 128], p)
        gains, p = at("gains", [128, N_GAIN], p)
        rinv, p = at("rinv", [128, T], p)
        acc, p = at("acc", [128, T], p)
        sq, sig, hf = [], [], []
        AT_SQ = p
        for n in range(2):
            t_, p = at(f"sq{n}", [128, T], p)
            sq.append(t_)
            t_, p = at(f"sig{n}", [128, T], p)
            sig.append(t_)
            t_, p = at(f"hf{n}", [128, T], p)
            hf.append(t_)
        mem_r, p = at("mem_r", [128, 2, 2], p)
        a2w, p = at("a2w", [RANK, H * GK], p)
        gate_b, p = at("gate_b", [64, 1], p)
        m0, p = at("m0", [H, B], p)
        scan_in, p = at("scan_in", [H, 3, B, TS + 1], p)
        s_lv, p = at("s_lv", [128, 2, 2, 2, NS], p)
        p = AT_H
        mem_nat, p = at("mem_nat", [128, 2, D], p)
        xp_nat, p = at("xp_nat", [128, NC, D], p)
        xs_nat, p = at("xs_nat", [NS, D], p)
        gain_rows, p = at("gain_rows", [N_GAIN, 128], p)
        mem_gain, p = at("mem_gain", [ND, 128], p)
        mem_f, p = at("mem_f", [128, ND, MEM], p)
        mem_hi, p = at("mem_hi", [128, ND, MEM], p, F32R)
        mem_lo, p = at("mem_lo", [128, ND, MEM], p, F32R)
        mem_sq, p = at("mem_sq", [128, D], p)
        kv_out = []
        for n in range(2):
            t_, p = at(f"kv_out{n}", [128, 2, 512], p)
            kv_out.append(t_)
        assert p <= AT_W
        z, p = at("z", [128, NZ, T], AT_H)
        rows, p = at("rows", [H, 8, T], p)
        R_U, R_W, R_B, R_M, R_WI, R_EM, R_WL, R_T = range(8)
        decay, p = at("decay", [128, 2, T], p)
        gla_a, p = at("gla_a", [128, NC, H, L], p)
        assert p <= AT_W
        lv_q, lv_k = [], []
        p = AT_H + NZ * T * 4
        for n in range(2):
            t_, p = at(f"lv_q{n}", [128, 2, T], p)
            lv_q.append(t_)
            t_, p = at(f"lv_k{n}", [128, 2, T], p)
            lv_k.append(t_)
        assert p <= AT_H + NZ * T * 4 + 8 * T * 4
        lv_e, p = at("lv_e", [128, 2, T], AT_SQ)
        lv_acc, p = at("lv_acc", [128, NC, H, 64], p)
        lv_tmp, p = at("lv_tmp", [128, NC, H, 64], p)
        assert p <= AT_SQ + 6 * T * 4
        p = AT_XN
        v_tok, p = at("v_tok", [128, H, DV], p)
        kw_tok, p = at("kw_tok", [128, H, DK], p)
        gk_tok, p = at("gk_tok", [128, 2, 128], p)
        gv_tok, p = at("gv_tok", [128, H, DV], p)
        ew, p = at("ew", [128, H, L], p)
        pw, p = at("pw", [128, H, L], p)
        q_in, p = at("q_in", [128, H, L], p)
        den, p = at("den", [128, H, L], p)
        ucol, p = at("ucol", [128, 2 * H], p)
        il, p = at("il", [128, H], p)
        ring = []
        for n in range(3):
            t_, p = at(f"ring{n}", [128, B, DV], p)
            ring.append(t_)
        s_ta = hf[1][0:NS, 0:12 * NS].rearrange("p (n r k t) -> p n r k t", n=3, r=2, k=2)
        s_a = hf[1][0:NS, 12 * NS:16 * NS].rearrange("p (h t) -> p h t", h=H)
        s_qn, p = at("s_qn", [128, H, NS], p)
        s_n, p = at("s_n", [128, B, H], p)
        s_n2, p = at("s_n2", [128, B, H], p)
        assert p <= AT_XN + 28672, p - AT_XN
        c_st, p = at("c_st", [128, H, DV], AT_XN + 28672)
        n_st, p = at("n_st", [128, H, 128], p)
        s_st, p = at("s_st", [128, H, DV], p)
        assert p <= AT_H
        p = AT_H + NZ * T * 4 + 8 * T * 4 + 2 * T * 4
        v_own = []
        for n in range(2):
            t_, p = at(f"v_own{n}", [NS, B, DV], p)
            v_own.append(t_)
        s_nrow, _ = at("s_nrow", [NS, DK], AT_H + NZ * T * 4 + 8 * T * 4)
        s_nrow2, _ = at("s_nrow2", [NS, DK], AT_H + NZ * T * 4 + 8 * T * 4 + 512)
        s_q, _ = at("s_q", [128, 2, 2, NS], AT_H + NZ * T * 4 + 8 * T * 4 + 1024)
        p = AT_H
        xq, p = at("xq", [128, ND, T], p)
        kv = []
        for n in range(KV_RING):
            t_, p = at(f"kv{n}", [128, 2, D], p)
            kv.append(t_)
        kT = []
        for n in range(2):
            t_, p = at(f"kT{n}", [128, ND, MEM], p)
            kT.append(t_)
        prob, probT = [], []
        for n in range(2):
            t_, p = at(f"prob{n}", [128, H, MEM], p)
            prob.append(t_)
            t_, p = at(f"probT{n}", [128, ND, 128], p)
            probT.append(t_)
        q_pad, _ = at("q_pad", [128, ND, B, 32], AT_SQ)
        p_pad, _ = at("p_pad", [128, 2, H, B, NS], AT_H + (ND * T + KV_RING * 2 * D + 2 * ND * MEM + H * MEM) * 4)
        s_av = probT[1]
        xmx, p = at("xmx", [128, 3 * H], p)
        assert p <= AT_W
        yf, p = at("yf", [128, ND, T], AT_H)
        y_tok, p = at("y_tok", [128, NC + 1, D], p)
        assert p <= AT_W

        ps = ctx.enter_context(nc.psum_tensor("ps", [128, 8, 512], F32))
        gg_sig = [sq[0], sig[0], sq[1], sig[1]]
        S_DECAY = 7
        S_DIFF = [9 + 2 * n for n in range(LEVELS + 1)]
        S_QK = [k + 1 for k in S_DIFF]
        S_SCORES = [9] + [k + 2 for k in S_DIFF]
        S_SUM = S_SCORES[-1] + 1
        S_IN, S_GATE, S_ROWS = S_SUM + 1, S_SUM + 2, S_SUM + 3
        ident = const[:, C_ID:C_ID + 128]
        ones = const[:, C_ONE:C_ONE + 128]
        causal = const[:, C_CAUSAL:C_CAUSAL + 128]
        restart = const[:, C_RESTART:C_RESTART + T]
        s_causal = const[0:NS, C_SCAUSAL:C_SCAUSAL + NS]
        own = const[0:NS, C_OWN:C_OWN + B]

        def level_mask(n):
            return const[:, C_LEVEL + 64 * n:C_LEVEL + 64 * n + 64]

        def pair(buf):
            q = 2 * (buf % 4)
            return ps[:, q:q + 2, 0:HT]

        def k_banks(n):
            q = (0, 2, 5)[n % 3]
            return ps[:, q:q + 2, :].rearrange("p b (k m) -> p (b k) m", k=2)

        def halves(t2d):
            return t2d.rearrange("p (h t) -> p h t", h=2)

        U_KV, B_KV = 0, 0
        B_N1 = 2
        U_UP1, B_UP1 = 16, 5
        U_DN1, B_DN1 = U_UP1 + 2 * NF, B_UP1 + 2 * NF
        B_N2 = B_DN1 + ND
        U_IN, B_IN = U_DN1 + 3 * ND, B_N2 + 1
        U_OUT, B_OUT = U_IN + NZ, B_IN + NZ
        B_N3 = B_OUT + ND
        assert B_IN % 4 == 2
        U_XQ, B_XQ = U_OUT + ND, B_N3 + 1
        U_XO, B_XO = U_XQ + ND, B_XQ + ND
        B_N4 = B_XO + ND
        U_UP2, B_UP2 = U_XO + ND, B_N4 + 1
        U_DN2, B_DN2 = U_UP2 + 2 * NF, B_UP2 + 2 * NF
        B_N5 = B_DN2 + ND
        U_END = U_DN2 + 3 * ND

        def by_row(w):
            return w[0].rearrange("(kt p) c -> p kt c", p=128)

        wk, wv = by_row(a["xattn_w_k"]), by_row(a["xattn_w_v"])
        w_in, w_out = by_row(a["w_in"]), by_row(a["w_out"])
        wq, wo = by_row(a["xattn_w_q"]), by_row(a["xattn_w_o"])
        gate = [by_row(a["ffn1_w_gate"]), by_row(a["ffn2_w_gate"])]
        up = [by_row(a["ffn1_w_up"]), by_row(a["ffn2_w_up"])]
        down = [by_row(a["ffn1_w_down"]), by_row(a["ffn2_w_down"])]
        DN_K = [(0, 8), (8, 15), (15, 22)]
        mem_k_out = o["mem_k"][0, 0].rearrange("(mb p) h d -> p mb (h d)", p=128)
        mem_v_out = o["mem_v"][0, 0].rearrange("(mb p) h d -> p mb (h d)", p=128)

        block = ctx.enter_context(nc.Block())

        @block.sync
        def _(sp):
            raw_ready = [sem(f"raw_ready{n}") for n in range(4)]
            lo_done = sem("lo_done")

            sp.dma_start(const[:, 0:C_LEVEL], a["consts"][:, 0:C_LEVEL]).then_inc(sem("const_in"), 16)
            sp.dma_start(mem_nat[:, :, :], a["mem_prompt"][0].rearrange("(mb p) c -> p mb c", p=128))\
              .then_inc(sem("mem_in"), 16)

            def load(slot, src, free):
                if free is not None:
                    sp.wait_ge(lo_done, free)
                kts, cols = src.shape[1], src.shape[2]
                dst = raw[slot][:, 0:kts * cols].rearrange("p (k c) -> p k c", k=kts)
                sp.dma_start(dst, src).then_inc(raw_ready[slot], 16)

            for u in range(16):
                w, c, kt = (wk, wv)[u // 8], (u // 4) % 2, 2 * (u % 4)
                load(u % 4, w[:, kt:kt + 2, 512 * c:512 * c + 512], u - 3 if u >= 4 else None)
                if u == 3:
                    sp.dma_start(xp_nat[:, :, :], a["x_prompt"][0].rearrange("(c p) d -> p c d", p=128))\
                      .then_inc(sem("x_in"), 16)

            def load_up(n, u0):
                with sp.Fori(0, NF // 2) as i:
                    for k in range(4):
                        w = (gate, up)[k % 2][n]
                        load((u0 + k) % 4, w[:, :, bass.ds(i * 256 + 128 * (k // 2), 128)], i * 4 + (u0 + k - 3))

            def load_down(n, u0):
                with sp.Fori(0, 2) as i:
                    for k in range(12):
                        lo, hi = DN_K[k % 3]
                        load((u0 + k) % 4, down[n][:, lo:hi, bass.ds(i * 512 + 128 * (k // 3), 128)],
                             i * 12 + (u0 + k - 3))

            def load_blocks(w, u0, bodies, col, step=512):
                with sp.Fori(0, bodies) as i:
                    for k in range(4):
                        load((u0 + k) % 4, w[:, :, bass.ds(i * step + (col + 128 * k), 128)], i * 4 + (u0 + k - 3))

            load_up(0, U_UP1)
            load_down(0, U_DN1)
            load(U_IN % 4, w_in[:, :, COL_GA:COL_GA + 128], U_IN - 3)
            sp.wait_ge(lo_done, U_IN + 1 - 3)
            gate_unit = raw[(U_IN + 1) % 4][:, :].rearrange("p (k c) -> p k c", k=8)
            sp.dma_start(gate_unit[:, :, 0:H], w_in[:, :, COL_MI:COL_MI + H]).then_inc(sem("gate_i_in"), 16)
            sp.wait_ge(sem("gate_i_in"), 16)
            sp.dma_start(gate_unit[:, :, 32:32 + H], w_in[:, :, COL_MF:COL_MF + H])\
              .then_inc(raw_ready[(U_IN + 1) % 4], 16)
            load_blocks(w_in, U_IN + Z_GQ, 2, COL_GQ)
            load_blocks(w_in, U_IN + Z_MQ, 3, COL_MQ)
            load_blocks(w_in, U_IN + Z_MO, 2, COL_MO, COL_GG - COL_MO)
            load_blocks(w_out, U_OUT, 2, 0)
            load_blocks(wq, U_XQ, 2, 0)
            load_blocks(wo, U_XO, 2, 0)
            load_up(1, U_UP2)
            load_down(1, U_DN2)

        @block.gpsimd
        def _(pool):
            steps = [0]

            def link(ins):
                steps[0] += 1
                ins.then_inc(sem("pool_chain"), 1)
                pool.wait_ge(sem("pool_chain"), steps[0])

            pool.dma_start(xs_nat[:, :], a["x_sample"].rearrange("b t d -> (b t) d")).then_inc(sem("xs_in"), 16)
            pool.dma_start(const[:, C_LEVEL:], a["consts"][:, C_LEVEL:]).then_inc(sem("small_in"), 16)
            pool.dma_start(sel[:, :, :], a["sel"].rearrange("h (k p) -> h k p", k=H)).then_inc(sem("small_in"), 16)
            pool.dma_start(a2w[:, :], a["gla_w_a2"][0]).then_inc(sem("small_in"), 16)
            pool.dma_start(gate_b[0:H, :], a["mlstm_b_i"].rearrange("a h -> h a")).then_inc(sem("small_in"), 16)
            pool.dma_start(gate_b[32:32 + H, :], a["mlstm_b_f"].rearrange("a h -> h a")).then_inc(sem("small_in"), 16)
            pool.dma_start(m0[:, :], a["state_mlstm_m"][0].rearrange("b h -> h b"),
                           allow_slow_non_contiguous=True).then_inc(sem("small_in"), 16)

            for n in range(4):
                pool.wait_ge(sem("evac"), (1, 2, 4, 5)[n])
                dst = (mem_k_out, mem_v_out)[n // 2][:, :, 512 * (n % 2):512 * (n % 2) + 512]
                pool.dma_start(dst, kv_out[n % 2][:, :, :]).then_inc(sem(f"kv_stored{n % 2}"), 16)

            pool.wait_ge(sem("evac"), B_IN)
            pool.memset(gla_a[64:128, :, :, 0:64], 0.0).then_inc(sem("zeros_set"), 1)
            pool.wait_ge(sem("zeros_set"), 1)
            for n in range(1, LEVELS):
                pool.wait_ge(sem("lv_masked"), n + 1)
                pool.tensor_tensor(lv_acc[:, :, :, :], lv_acc[:, :, :, :], lv_tmp[:, :, :, :], ALU.add)\
                    .then_inc(sem("lv_added"), 1)

            c_in = a["state_mlstm_c"][0].rearrange("b h k v -> h k b v")
            s_in = a["state_gla_s"][0].rearrange("b (p r) k v -> p (r k) b v", r=2)
            c_out = o["mlstm_c_s"][0].rearrange("b h k v -> h k b v")
            s_out = o["gla_s_s"][0].rearrange("b (p r) k v -> p (r k) b v", r=2)

            def load_state(n):
                src = c_in[n] if n < H else s_in[n - H]
                pool.dma_start(ring[n % 3][:, :, :], src).then_inc(sem(f"state_in{n % 3}"), 16)

            pool.wait_ge(sem("pe_unit"), U_IN + NZ)
            pool.memset(s_st[:, :, :], 0.0).then_inc(sem("zeros_set"), 1)
            pool.wait_ge(sem("zeros_set"), 2)
            pool.wait_ge(sem("levels_done"), 1)
            pool.dma_start(s_nrow[:, :], a["state_mlstm_n"][0].rearrange("b h k -> (b h) k"))\
                .then_inc(sem("n_in"), 16)
            for n in range(3):
                load_state(n)

            for c in range(NC + 1):
                pool.wait_ge(sem("w_exp"), c + 1)
                if c < NC:
                    pool.tensor_tensor(ew[:, :, :], ew[:, :, :], causal.unsqueeze(1).broadcast_to([128, H, L]),
                                       ALU.mult).then_inc(sem("w_masked"), 1)
                else:
                    pool.tensor_tensor(ew[0:NS, :, 0:NS], ew[0:NS, :, 0:NS],
                                       s_causal.unsqueeze(1).broadcast_to([NS, H, NS]), ALU.mult)\
                        .then_inc(sem("w_masked"), 1)

            pool.wait_ge(sem("chunk_done"), NC)
            pool.wait_ge(sem("gla_out"), NC)
            pool.dma_start(o["mlstm_c_p"][0, 0].rearrange("h k v -> k h v"), c_st[:, :, :]).then_inc(sem("st_out"), 16)
            pool.dma_start(o["mlstm_n_p"][0, 0].rearrange("h k -> k h"), n_st[:, :, 0],
                           allow_slow_non_contiguous=True).then_inc(sem("st_out"), 16)
            pool.dma_start(o["mlstm_m_p"][0, 0].rearrange("(h a) -> h a", a=1), rows[:, R_M, TP - 1:TP])\
                .then_inc(sem("st_out"), 16)
            for h in range(H):
                r = 64 * (h % 2)
                pool.dma_start(o["gla_s_p"][0, 0, h], s_st[r:r + 64, h, :]).then_inc(sem("st_out"), 16)
            pool.dma_start(o["mlstm_m_s"][0].rearrange("b h -> h b"),
                           rows[:, R_M, TP + TS - 1:T:TS], allow_slow_non_contiguous=True)\
                .then_inc(sem("st_out"), 16)
            for n in range(H + 2):
                pool.wait_ge(sem("upd_free"), (1, 2, 3, 4, 6, 8)[n])
                dst = c_out[n] if n < H else s_out[n - H]
                pool.dma_start(dst, ring[n % 3][:, :, :]).then_inc(sem(f"state_out{n % 3}"), 16)
                if n + 3 < H + 2:
                    pool.wait_ge(sem(f"state_out{n % 3}"), 16 * (n // 3 + 1))
                    load_state(n + 3)
            pool.wait_ge(sem("n_new"), 1)
            pool.dma_start(o["mlstm_n_s"][0].rearrange("b h k -> (b h) k"), s_nrow2[:, :]).then_inc(sem("st_out"), 16)
            pool.wait_ge(sem("st_out"), 16 * 9)
            for n in range(3):
                pool.wait_ge(sem(f"state_out{n}"), 32)
            pool.sem_inc(sem("mixer_stored"), 1)

            for n in range(18):
                if n == 0:
                    pool.wait_ge(sem("ym_lo"), 8)
                    pool.wait_ge(sem("kv_stored0"), 32)
                    pool.wait_ge(sem("kv_stored1"), 32)
                if n >= KV_RING:
                    was = n - KV_RING
                    name, value = (("av_mm", NC) if was == 1 else ("kT_mm", 1 + 2 * max(was - 1, 0)) if was < 10
                                   else ("sav_mm", was - 9))
                    pool.wait_ge(sem(name), value)
                if n < 2:
                    src = (mem_k_out, mem_v_out)[n]
                else:
                    src = (a["cache_mem_k"], a["cache_mem_v"])[n // 10][0, (n - 2) % 8]\
                        .rearrange("(mb p) h d -> p mb (h d)", p=128)
                pool.dma_start(kv[n % KV_RING][:, :, :], src).then_inc(sem(f"kv_in{n % KV_RING}"), 16)

            for c in range(NC):
                pool.wait_ge(sem("y_copied"), c + 1)
                pool.dma_start(o["y_prompt"][0, c * L:(c + 1) * L, :], y_tok[:, c, :]).then_inc(sem("y_out"), 16)
            pool.wait_ge(sem("y_copied"), NC + 1)
            pool.dma_start(o["y_sample"].rearrange("b t d -> (b t) d"), y_tok[0:NS, NC, :]).then_inc(sem("y_out"), 16)
            pool.wait_ge(sem("y_out"), 16 * (NC + 1))

        @block.scalar
        def _(act):
            raw_ready = [sem(f"raw_ready{n}") for n in range(4)]
            pe_unit, evac = sem("pe_unit"), sem("evac")
            steps = [0]

            def link(ins):
                steps[0] += 1
                ins.then_inc(sem("act_chain"), 1)
                act.wait_ge(sem("act_chain"), steps[0])

            def split(u0, i=0, per=0):
                act.wait_ge(raw_ready[u0 % 4], 16 * (u0 // 4 + 1) + i * (4 * per))
                if u0 >= 2:
                    act.wait_ge(pe_unit, i * per + (u0 - 1))
                act.activation(w_hi[u0 % 2][:, :], raw[u0 % 4][:, :], ACT.Copy).then_inc(sem("hi_done"), 1)

            def square(r, src, ready, value, i=0, per=0):
                act.wait_ge(ready, value)
                if r >= 2:
                    act.wait_ge(sem("acc_done"), i * per + (r - 1))
                act.activation(sq[r % 2][:, :], src, ACT.Square).then_inc(sem("sq_done"), 1)

            def norm_inverse(g, buf):
                act.wait_ge(sem("norm_mm"), g + 1)
                act.activation(halves(sig[0][:, :]), pair(buf), ACT.Ln, bias=EPS, scale=1.0 / D).then_inc(evac, 1)
                act.wait_ge(evac, buf + 1)
                act.activation(rinv[:, :], sig[0][:, :], ACT.Exp, scale=-0.5).then_inc(sem("norm_inv"), 1)

            def norm_hi(g, d):
                act.wait_ge(sem("xf_done"), 8 * g + d + 1)
                act.activation(xn_hi[:, d, :], hf[d % 2][:, :], ACT.Copy).then_inc(sem("xnh_done"), 1)

            def norm(g, buf):
                norm_inverse(g, buf)
                for d in range(ND):
                    norm_hi(g, d)

            act.dma_start(mem_gain[:, :], a["mem_norm_g"][0].rearrange("(n p) -> n p", p=128))\
               .then_inc(sem("mem_gain_in"), 16)
            rows_of = [("ffn1_norm_g", G_FFN1, 8), ("mix_norm_g", G_MIX, 8), ("xattn_norm_g", G_XA, 8),
                       ("ffn2_norm_g", G_FFN2, 8), ("final_norm_g", G_FIN, 8),
                       ("mem_norm_g", G_MEM, 8), ("mlstm_out_g", G_ML, 4), ("gla_out_g", G_GLA, 4), ("gla_b_a", G_BA, 2)]
            for name, g, n in rows_of:
                src = a[name] if name == "final_norm_g" else a[name][0]
                act.dma_start(gain_rows[g:g + n, :], src.rearrange("(n p) -> n p", p=128))\
                    .then_inc(sem("gains_in"), 16)
            act.wait_ge(sem("mem_in"), 16)
            for mb in range(2):
                link(act.activation(mem_sq[:, :], mem_nat[:, mb, :], ACT.Square, accum_out=mem_r[:, 0, mb:mb + 1]))
            act.activation(mem_r[:, 1, :], mem_r[:, 0, :], ACT.Sqrt, bias=EPS, scale=1.0 / D)\
               .then_inc(sem("mem_root"), 1)
            act.wait_ge(sem("mem_f_done"), ND)
            act.activation(mem_hi[:, :, :], mem_f[:, :, :], ACT.Copy).then_inc(sem("mem_hi_done"), 1)
            split(0)
            split(1)
            def kv_evac(n, buf, last_unit):
                act.wait_ge(pe_unit, last_unit + 1)
                if n >= 2:
                    act.wait_ge(sem(f"kv_stored{n % 2}"), 16)
                act.activation(kv_out[n % 2][:, 0, :], ps[:, 2 * (buf % 4), :], ACT.Copy, scale=mem_r[:, 0, 0:1])
                act.activation(kv_out[n % 2][:, 1, :], ps[:, 2 * (buf % 4) + 1, :], ACT.Copy,
                               scale=mem_r[:, 0, 1:2]).then_inc(evac, 1)

            act.wait_ge(sem("mem_r_done"), 1)
            for u in range(16):
                if u == 3:
                    kv_evac(0, 0, 3)
                if u == 7:
                    kv_evac(1, 1, 7)
                if u == 9:
                    norm_inverse(0, B_N1)
                if u == 11:
                    kv_evac(2, 3, 11)
                if u == 15:
                    kv_evac(3, 4, 15)
                split(u + 2)
                if u < ND:
                    square(u, x[:, u, :], sem("x_made"), u + 1)
                if u >= 9:
                    norm_hi(0, u - 9)
            norm_hi(0, ND - 1)

            def ffn_up(n, u0, b0):
                with act.Fori(0, NF // 2) as i:
                    for k in range(4):
                        j = k // 2
                        if k % 2 == 0:
                            act.wait_ge(pe_unit, i * 4 + (u0 + k + 1))
                            act.wait_ge(evac, i * 4 + (b0 + k - 2))
                            act.activation(halves(sig[j][:, :]), pair(b0 + k), ACT.Sigmoid)\
                               .then_inc(sem("sig_done"), 1)
                            split(u0 + k + 2, i, 4)
                        else:
                            split(u0 + k + 2, i, 4)
                            act.wait_ge(evac, i * 4 + (b0 + k + 1))
                            act.activation(h_hi[:, bass.ds(i * 2 + j, 1), :].rearrange("p a t -> p (a t)"),
                                           hf[j][:, :], ACT.Copy).then_inc(sem("hh_done"), 1)

            def ffn_down(u0, b0, r0, last):
                def body(i, splits):
                    for k in range(12):
                        if k % 3 == 2:
                            d = k // 3
                            square(r0 + d, x[:, bass.ds(i * 4 + d, 1), :].rearrange("p a t -> p (a t)"), evac,
                                   i * 4 + (b0 + d + 1), i, 4)
                        if k < splits:
                            split(u0 + k + 2, i, 12)
                if last:
                    body(0, 12)
                    for k in range(12):
                        if k % 3 == 2:
                            d = k // 3
                            square(r0 + 4 + d, x[:, 4 + d, :], evac, b0 + 4 + d + 1)
                        if k < 10:
                            split(u0 + 12 + k + 2)
                else:
                    with act.Fori(0, 2) as i:
                        body(i, 12)

            def residual(u0, b0, r0):
                with act.Fori(0, 2) as i:
                    for k in range(4):
                        square(r0 + k, x[:, bass.ds(i * 4 + k, 1), :].rearrange("p a t -> p (a t)"), evac,
                               i * 4 + (b0 + k + 1), i, 4)
                        split(u0 + k + 2, i, 4)

            act.wait_ge(sem("kv_stored0"), 32)
            act.wait_ge(sem("kv_stored1"), 32)
            ffn_up(0, U_UP1, B_UP1)
            ffn_down(U_DN1, B_DN1, 8, False)
            norm(1, B_N2)
            def level_exp(n):
                act.wait_ge(sem("lv_diff"), n)
                link(act.activation(lv_e[:, :, :], lv_e[:, :, :], ACT.Abs))
                act.activation(lv_e[:, :, :], lv_e[:, :, :], ACT.Exp, scale=-1.0 / TAU).then_inc(sem("lv_exp"), 1)

            for k in range(NZ):
                split(U_IN + k + 2)
                if k == S_DECAY:
                    act.wait_ge(sem("y_decay"), 1)
                    link(act.activation(lv_e[:, :, :], decay[:, :, :], ACT.Abs))
                    link(act.activation(lv_e[:, :, :], lv_e[:, :, :], ACT.Exp, scale=-1.0))
                    act.activation(lv_e[:, :, :], lv_e[:, :, :], ACT.Ln, bias=1.0).then_inc(sem("log_decay"), 1)
                if k in S_DIFF:
                    level_exp(S_DIFF.index(k) + 1)
                if k == S_SUM:
                    act.wait_ge(sem("lv_qk"), LEVELS + 1)
                    act.activation(lv_e[:, :, :], decay[:, :, :], ACT.Exp, scale=1.0 / TAU).then_inc(sem("in_exp"), 1)
                if k == S_IN:
                    act.wait_ge(sem("in_diff"), 1)
                    act.activation(lv_e[:, :, :], lv_e[:, :, :], ACT.Exp, scale=1.0 / TAU).then_inc(sem("in_exp"), 1)
                if k == S_GATE:
                    act.wait_ge(sem("y_rows"), 1)
                    link(act.activation(rows[:, R_T, :], rows[:, R_W, :], ACT.Abs))
                    link(act.activation(rows[:, R_T, :], rows[:, R_T, :], ACT.Exp, scale=-1.0))
                    act.activation(rows[:, R_T, :], rows[:, R_T, :], ACT.Ln, bias=1.0).then_inc(sem("log_rows"), 1)
                if k == S_ROWS + 1:
                    act.wait_ge(sem("rows_made"), 1)
                    for dst, src, scale in ((R_WI, R_WI, 1.0), (R_EM, R_M, -1.0), (R_WL, R_WL, 1.0)):
                        act.activation(rows[:, dst, :], rows[:, src, :], ACT.Exp, scale=scale)\
                           .then_inc(sem("rows_exp"), 1)
            act.wait_ge(evac, B_IN + NZ)
            act.activation(z[:, Z_MO:Z_MO + 4, :], z[:, Z_MO:Z_MO + 4, :], ACT.Sigmoid)
            act.wait_ge(sem("levels_done"), 1)
            for j in range(4):
                act.activation(gg_sig[j][:, :], z[:, Z_GG + j, :], ACT.Sigmoid).then_inc(sem("gg_sig"), 1)

            def chunk(c, n):
                act.wait_ge(sem("w_arg"), c + 1)
                act.activation(ew[0:n, :, 0:n], ew[0:n, :, 0:n], ACT.Exp).then_inc(sem("w_exp"), 1)
                act.wait_ge(sem("pe_a"), 9 * c + 7)
                act.activation(v_tok[0:n, :, :], ps[0:n, 5, :].rearrange("p (h v) -> p h v", h=H), ACT.Copy)\
                   .then_inc(sem("tok_done"), 1)
                act.wait_ge(sem("pe_a"), 9 * c + 8)
                act.activation(gk_tok[0:n, :, :], ps[0:n, 6, 0:256].rearrange("p (h v) -> p h v", h=2), ACT.Copy)\
                   .then_inc(sem("tok_done"), 1)
                act.wait_ge(sem("pe_a"), 9 * c + 9)
                act.activation(gv_tok[0:n, :, :], ps[0:n, 7, :].rearrange("p (h v) -> p h v", h=H), ACT.Copy)\
                   .then_inc(sem("tok_done"), 1)
                act.wait_ge(sem("den_mm"), c + 1)
                act.activation(den[:, :, 0:n], ps[:, 3, 0:H * n].rearrange("p (h t) -> p h t", h=H), ACT.Abs)\
                   .then_inc(sem("den_abs"), 1)
                if c < NC:
                    act.wait_ge(sem("gla_mm"), c + 1)
                else:
                    act.wait_ge(sem("o_s"), H)
                act.activation(z[:, Z_GV:Z_GV + H, c * L:c * L + n],
                               ps[:, 7 if c < NC else 1, 0:H * n].rearrange("p (h t) -> p h t", h=H), ACT.Copy)\
                   .then_inc(sem("gla_out"), 1)

            for c in range(NC):
                chunk(c, L)
            chunk(NC, NS)

            act.wait_ge(sem("chunk_done"), NC + 1)
            act.wait_ge(sem("gla_out"), NC + 1)

            def head(j):
                return z[:, Z_MQ + j, :] if j < H else z[:, Z_GV + j - H, :]

            def head_square(j):
                if j >= 2:
                    act.wait_ge(sem("hn_mm"), j - 1)
                act.activation(sq[j % 2][:, :], head(j), ACT.Square).then_inc(sem("hn_sq"), 1)

            head_square(0)
            for j in range(2 * H):
                if j + 1 < 2 * H:
                    head_square(j + 1)
                act.wait_ge(sem("hn_mm"), j + 1)
                if j >= 2:
                    act.wait_ge(sem("hn_y"), j - 1)
                act.activation(halves(sig[j % 2][:, :]), pair(j), ACT.Ln, bias=EPS, scale=1.0 / DV)\
                   .then_inc(sem("hn_root"), 1)
                act.wait_ge(sem("hn_root"), j + 1)
                act.activation(sig[j % 2][:, :], sig[j % 2][:, :], ACT.Exp, scale=-0.5).then_inc(sem("hn_inv"), 1)
                if j == 1:
                    act.wait_ge(sem("mixer_stored"), 1)
                if j >= 1:
                    act.wait_ge(sem("hn_y"), j)
                    act.activation(xn_hi[:, j - 1, :], head(j - 1), ACT.Copy).then_inc(sem("ym_hi"), 1)
            act.wait_ge(sem("hn_y"), 2 * H)
            act.activation(xn_hi[:, 7, :], head(7), ACT.Copy).then_inc(sem("ym_hi"), 1)
            residual(U_OUT, B_OUT, 16)
            norm(2, B_N3)
            with act.Fori(0, 2) as i:
                for k in range(4):
                    split(U_XQ + k + 2, i, 4)

            def exp_rows(n_mx, heads, scores, dst):
                for h in range(heads):
                    ins = act.activation(dst(h), scores(h), ACT.Exp, bias=xmx[:, h:h + 1], scale=1.0 / 16,
                                         accum_out=xmx[:, 4 + h:5 + h])
                ins.then_inc(sem("x_exp"), 1)

            act.wait_ge(sem("kT_mm"), 1)
            act.activation(kT[0][:, 0:4, :], ps[:, 0:2, :].rearrange("p b (k m) -> p (b k) m", k=2), ACT.Copy)\
               .then_inc(sem("kT_act"), 1)
            for tb in range(NC):
                act.wait_ge(sem("x_max"), tb + 1)
                if tb >= 2:
                    act.wait_ge(sem("pT_mm"), tb - 1)
                sc = ps[:, 4 * (tb % 2):4 * (tb % 2) + 2, :].rearrange("p b (k m) -> p (b k) m", k=2)
                exp_rows(tb, H, lambda h: sc[:, h, :], lambda h: prob[tb % 2][:, h, :])
                act.wait_ge(sem("av_mm"), tb + 1)
                q = 4 * (tb % 2)
                act.activation(xn_hi[:, :, tb * 128:tb * 128 + 128],
                               ps[:, q:q + 2, :].rearrange("p b (k t) -> p (b k) t", k=4), ACT.Copy)\
                   .then_inc(sem("av_hi"), 1)
            for b in range(B):
                act.wait_ge(sem("kT_mm"), 2 * b + 2)
                if b >= 2:
                    act.wait_ge(sem("ssc_mm"), b - 1)
                act.activation(kT[(b + 1) % 2][:, 0:4, :], k_banks(2 * b), ACT.Copy).then_inc(sem("kT_act"), 1)
            act.wait_ge(sem("x_max"), NC + 1)
            exp_rows(NC, 1, lambda h: ps[:, 4, 0:MEM], lambda h: prob[0][:, 0, :])
            act.wait_ge(sem("savT_mm"), 1)
            act.activation(xn_hi[:, :, TP:T], ps[:, 5, 0:ND * NS].rearrange("p (k t) -> p k t", k=ND), ACT.Copy)\
               .then_inc(sem("av_hi"), 1)

            residual(U_XO, B_XO, 24)
            norm(3, B_N4)
            ffn_up(1, U_UP2, B_UP2)
            ffn_down(U_DN2, B_DN2, 32, True)
            norm_inverse(4, B_N5)
            for c in range(NC + 1):
                n = L if c < NC else NS
                act.wait_ge(sem("yT_mm"), c + 1)
                q = 2 * (c % 4)
                act.activation(y_tok[0:n, c, :].rearrange("p (b f) -> p b f", b=2), ps[0:n, q:q + 2, :], ACT.Copy)\
                   .then_inc(sem("y_copied"), 1)

        @block.vector
        def _(dve):
            pe_unit, evac = sem("pe_unit"), sem("evac")
            steps = [0]

            def link(ins):
                steps[0] += 1
                ins.then_inc(sem("dve_chain"), 1)
                dve.wait_ge(sem("dve_chain"), steps[0])

            def split(u0, i=0, per=0):
                dve.wait_ge(sem("hi_done"), i * per + (u0 + 1))
                dve.tensor_tensor(w_lo[u0 % 2][:, :], raw[u0 % 4][:, :], w_hi[u0 % 2][:, :].bitcast(F32),
                                  ALU.subtract).then_inc(sem("lo_done"), 1)

            def add_square(r, i=0, per=0):
                dve.wait_ge(sem("sq_done"), i * per + (r + 1))
                if not (r == 0):
                    dve.wait_ge(sem("acc_done"), i * per + r)
                dve.tensor_tensor(acc[:, :], acc[:, :], sq[r % 2][:, :], ALU.add).then_inc(sem("acc_done"), 1)


            def norm_scale(g, gain, d):
                if d == 0:
                    dve.wait_ge(sem("norm_inv"), g + 1)
                if d == 2:
                    dve.memset(acc[:, :], 0.0)
                if d < ND:
                    if d >= 2:
                        dve.wait_ge(sem("xnl_done"), 8 * g + d - 1)
                    dve.scalar_tensor_tensor(out=hf[d % 2][:, :], in0=x[:, d, :],
                                             scalar=gains[:, gain + d:gain + d + 1], in1=rinv[:, :], op0=ALU.mult,
                                             op1=ALU.mult).then_inc(sem("xf_done"), 1)
                if d >= 1:
                    dve.wait_ge(sem("xnh_done"), 8 * g + d)
                    dve.tensor_tensor(xn_lo[:, d - 1, :], hf[(d - 1) % 2][:, :], xn_hi[:, d - 1, :].bitcast(F32),
                                      ALU.subtract).then_inc(sem("xnl_done"), 1)

            def norm(g, gain):
                for d in range(ND + 1):
                    norm_scale(g, gain, d)

            link(dve.memset(acc[:, :], 0.0))
            dve.wait_ge(sem("gain_mm"), 1)
            link(dve.tensor_copy(gains[:, G_MEM:G_MEM + 8], ps[:, 7, 0:8]))
            for d in range(ND):
                dve.wait_ge(sem("memT_mm"), 2 * (d // 2) + 2)
                dve.tensor_scalar(mem_f[:, d, :], ps[:, d // 2, MEM * (d % 2):MEM * (d % 2) + MEM],
                                  gains[:, G_MEM + d:G_MEM + d + 1], None, ALU.mult).then_inc(sem("mem_f_done"), 1)
            dve.wait_ge(sem("mem_root"), 1)
            dve.reciprocal(mem_r[:, 0, :], mem_r[:, 1, :]).then_inc(sem("mem_r_done"), 1)
            dve.wait_ge(sem("mem_hi_done"), 1)
            dve.tensor_tensor(mem_lo[:, :, :], mem_f[:, :, :], mem_hi[:, :, :].bitcast(F32), ALU.subtract)\
               .then_inc(sem("mem_lo_done"), 1)
            split(0)
            split(1)
            for u in range(16):
                split(u + 2)
                if u < ND:
                    q = 4 + 2 * (u % 2)
                    dve.wait_ge(sem("xT_mm"), u + 1)
                    dve.tensor_copy(x[:, u, 0:TP], ps[:, q, :])
                    dve.tensor_copy(x[:, u, TP:T], ps[:, q + 1, 0:NS]).then_inc(sem("x_made"), 1)
                    if u >= 1:
                        add_square(u - 1)
                if u == ND - 1:
                    add_square(u)
                    dve.wait_ge(sem("gain_mm"), 2)
                    dve.tensor_copy(gains[:, :], ps[:, 5, 256:256 + N_GAIN]).then_inc(sem("gains_made"), 1)
                    dve.wait_ge(sem("gains_made"), 1)
                if u >= 9:
                    norm_scale(0, G_FFN1, u - 9)
            norm_scale(0, G_FFN1, ND - 1)
            norm_scale(0, G_FFN1, ND)

            def ffn_up(n, u0, b0):
                p0 = NF * n
                with dve.Fori(0, NF // 2) as i:
                    for k in range(4):
                        j = k // 2
                        if k % 2 == 0:
                            dve.wait_ge(sem("sig_done"), i * 2 + (p0 + j + 1))
                            dve.tensor_tensor(halves(sig[j][:, :]), pair(b0 + k), halves(sig[j][:, :]), ALU.mult)\
                               .then_inc(evac, 1)
                            split(u0 + k + 2, i, 4)
                        else:
                            dve.wait_ge(pe_unit, i * 4 + (u0 + k + 1))
                            dve.wait_ge(evac, i * 4 + (b0 + k))
                            dve.tensor_tensor(halves(hf[j][:, :]), pair(b0 + k), halves(sig[j][:, :]), ALU.mult)\
                               .then_inc(evac, 1)
                            split(u0 + k + 2, i, 4)
                            dve.wait_ge(sem("hh_done"), i * 2 + (p0 + j + 1))
                            fb = bass.ds(i * 2 + j, 1)
                            dve.tensor_tensor(h_lo[:, fb, :].rearrange("p a t -> p (a t)"), hf[j][:, :],
                                              h_hi[:, fb, :].bitcast(F32).rearrange("p a t -> p (a t)"),
                                              ALU.subtract).then_inc(sem("hl_done"), 1)

            def add_block(d, buf, scale):
                dve.scalar_tensor_tensor(out=halves(x[:, d, :].rearrange("p a t -> p (a t)")), in0=pair(buf),
                                         scalar=scale, in1=halves(x[:, d, :].rearrange("p a t -> p (a t)")),
                                         op0=ALU.mult, op1=ALU.add).then_inc(evac, 1)

            def ffn_down(u0, b0, r0, last):
                def body(i, i0, splits):
                    for k in range(12):
                        if k % 3 == 2:
                            d = k // 3
                            dve.wait_ge(pe_unit, i * 12 + (u0 + 12 * i0 + k + 1))
                            at_d = bass.ds(i * 4 + (4 * i0 + d), 1) if not i0 else slice(4 * i0 + d, 4 * i0 + d + 1)
                            add_block(at_d, b0 + 4 * i0 + d, 0.5)
                        if k < splits:
                            split(u0 + 12 * i0 + k + 2, i, 12)
                        if k % 3 == 2:
                            add_square(r0 + 4 * i0 + k // 3, i, 4)
                if last:
                    body(0, 0, 12)
                    body(0, 1, 10)
                else:
                    with dve.Fori(0, 2) as i:
                        body(i, 0, 12)

            def residual(u0, b0, r0):
                with dve.Fori(0, 2) as i:
                    for k in range(4):
                        dve.wait_ge(pe_unit, i * 4 + (u0 + k + 1))
                        add_block(bass.ds(i * 4 + k, 1), b0 + k, 1.0)
                        split(u0 + k + 2, i, 4)
                        add_square(r0 + k, i, 4)

            dve.wait_ge(sem("kv_stored0"), 32)
            dve.wait_ge(sem("kv_stored1"), 32)
            ffn_up(0, U_UP1, B_UP1)
            ffn_down(U_DN1, B_DN1, 8, False)
            norm(1, G_MIX)

            def row(r, lo=0, hi=T):
                return rows[:, r, lo:hi]

            def by_chunk(r):
                return rows[:, r, 0:TP].rearrange("p (c t) -> p c t", c=NC)

            def by_seq(r):
                return rows[:, r, TP:T].rearrange("p (b t) -> p b t", b=B)

            def make_decay():
                dve.wait_ge(sem("log_decay"), 1)
                link(dve.scalar_tensor_tensor(out=lv_e[:, :, :], in0=decay[:, :, :], scalar=0.0, in1=lv_e[:, :, :],
                                              op0=ALU.min, op1=ALU.subtract))
                for n in range(2):
                    ins = dve.tensor_tensor_scan(decay[:, n, :], restart, lv_e[:, n, :], 0.0, ALU.mult, ALU.add)
                link(ins)

            def level_diff(n):
                half = 1 << (n - 1)
                if n >= 2:
                    dve.wait_ge(sem("lv_qk"), n - 1)
                if half <= 16:
                    dst = lv_e[:, :, :].rearrange("p f t -> p (f t)").rearrange("p (b t) -> p b t", t=2 * half)
                    src = decay[:, :, :].rearrange("p f t -> p (f t)").rearrange("p (b t) -> p b t", t=2 * half)
                    dve.tensor_tensor(dst, src, src[:, :, half - 1:half].broadcast_to(list(src.shape)),
                                      ALU.subtract).then_inc(sem("lv_diff"), 1)
                else:
                    dst = lv_e[:, :, 0:TP].rearrange("p f (b t) -> p f b t", t=2 * half)
                    src = decay[:, :, 0:TP].rearrange("p f (b t) -> p f b t", t=2 * half)
                    dve.tensor_tensor(dst, src, src[:, :, :, half - 1:half].broadcast_to(list(src.shape)),
                                      ALU.subtract).then_inc(sem("lv_diff"), 1)

            def level_qk(n):
                if n >= 3:
                    dve.wait_ge(sem("lv_mm"), n - 1)
                dve.wait_ge(sem("lv_exp"), n)
                if n <= 2:
                    dve.tensor_tensor(s_lv[:, n - 1, 0, :, :], z[:, Z_GQ:Z_GQ + 2, TP:T], lv_e[:, :, TP:T], ALU.mult)
                    dve.tensor_tensor(s_lv[:, n - 1, 1, :, :], z[:, Z_GK:Z_GK + 2, TP:T], lv_e[:, :, TP:T], ALU.mult)
                dve.tensor_tensor(lv_q[n % 2][:, :, 0:TP], z[:, Z_GQ:Z_GQ + 2, 0:TP], lv_e[:, :, 0:TP], ALU.mult)
                dve.tensor_tensor(lv_k[n % 2][:, :, 0:TP], z[:, Z_GK:Z_GK + 2, 0:TP], lv_e[:, :, 0:TP], ALU.mult)\
                   .then_inc(sem("lv_qk"), 1)

            def level_masked(m):
                dve.wait_ge(sem("lv_mm"), m + 1)
                if m >= 2:
                    dve.wait_ge(sem("lv_added"), m - 1)
                for r in range(2):
                    dst = (lv_acc if m == 0 else lv_tmp)[:, :, r::2, :]
                    src = ps[:, 4 + 2 * (m % 2) + r, :].rearrange("p (c k t) -> p c k t", c=NC, k=2)
                    mask = level_mask(m).unsqueeze(1).unsqueeze(1).broadcast_to([128, NC, 2, 64])
                    ins = dve.tensor_tensor(dst, src, mask, ALU.mult)
                ins.then_inc(sem("lv_masked"), 1)

            def level_sum():
                dve.wait_ge(sem("lv_added"), LEVELS - 1)
                dve.wait_ge(sem("lv_masked"), LEVELS + 1)
                dve.wait_ge(sem("zeros_set"), 1)
                for lo in (0, 64):
                    dve.tensor_tensor(gla_a[lo:lo + 64, :, :, lo:lo + 64], lv_acc[lo:lo + 64, :, :, :],
                                      lv_tmp[lo:lo + 64, :, :, :], ALU.add)
                dve.wait_ge(sem("lv_mm"), LEVELS + 2)
                m = LEVELS + 1
                for r in range(2):
                    ins = dve.tensor_scalar(gla_a[0:64, :, r::2, 64:128],
                                            ps[0:64, 4 + 2 * (m % 2) + r, :].rearrange("p (c k t) -> p c k t", c=NC, k=2),
                                            GK ** -0.5, None, ALU.mult)
                link(ins)
                for r in range(2):
                    ins = dve.tensor_tensor(s_ta[:, :, r, :, :],
                                            ps[0:NS, 4 + r, 0:3 * 2 * NS].rearrange("p (n k t) -> p n k t", n=3, k=2),
                                            const[0:NS, C_LEVEL:C_LEVEL + 192].rearrange("p (n t) -> p n t", n=3)
                                            [:, :, 0:NS].unsqueeze(2).broadcast_to([NS, 3, 2, NS]), ALU.mult)
                link(ins)
                s_a_v = s_a[:, :, :].rearrange("p (k r) t -> p r k t", r=2)
                link(dve.tensor_tensor(s_a_v, s_ta[:, 0, :, :, :], s_ta[:, 1, :, :, :], ALU.add))
                link(dve.tensor_tensor(s_a_v, s_a_v, s_ta[:, 2, :, :, :], ALU.add))

            e_last = hf[0][:, 0:2 * (NC + B)].rearrange("p (f n) -> p f n", f=2)

            def into_chunk():
                dve.wait_ge(sem("in_exp"), 1)
                dve.scalar_tensor_tensor(out=z[:, Z_GQ:Z_GQ + 2, :], in0=z[:, Z_GQ:Z_GQ + 2, :],
                                         scalar=GK ** -0.5, in1=lv_e[:, :, :], op0=ALU.mult, op1=ALU.mult)
                dve.tensor_copy(e_last[:, :, 0:NC], lv_e[:, :, L - 1:TP:L])
                link(dve.tensor_copy(e_last[:, :, NC:NC + B], lv_e[:, :, TP + TS - 1:T:TS]))
                for n in range(2):
                    src = decay[:, n, 0:TP].rearrange("p (c t) -> p c t", c=NC)
                    dve.tensor_tensor(lv_e[:, n, 0:TP].rearrange("p (c t) -> p c t", c=NC),
                                      src[:, :, L - 1:L].broadcast_to([128, NC, L]), src, ALU.subtract)
                    src = decay[:, n, TP:T].rearrange("p (b t) -> p b t", b=B)
                    ins = dve.tensor_tensor(lv_e[:, n, TP:T].rearrange("p (b t) -> p b t", b=B),
                                            src[:, :, TS - 1:TS].broadcast_to([128, B, TS]), src, ALU.subtract)
                ins.then_inc(sem("in_diff"), 1)

            def out_of_chunk():
                dve.wait_ge(sem("in_exp"), 2)
                dve.tensor_tensor(z[:, Z_GK:Z_GK + 2, :], z[:, Z_GK:Z_GK + 2, :], lv_e[:, :, :], ALU.mult)
                link(dve.memset(s_q[:, :, :, :], 0.0))
                for r in range(2):
                    ins = dve.tensor_copy(s_q[64 * r:64 * r + 64, r, :, :], z[64 * r:64 * r + 64, Z_GQ:Z_GQ + 2, TP:T])
                ins.then_inc(sem("levels_done"), 1)

            def make_rows():
                dve.wait_ge(sem("log_rows"), 1)
                link(dve.scalar_tensor_tensor(out=row(R_W), in0=row(R_W), scalar=0.0, in1=row(R_T), op0=ALU.min,
                                              op1=ALU.subtract))
                dve.tensor_tensor_scan(row(R_B), restart[0:H, :], row(R_W), 0.0, ALU.mult, ALU.add)
                dve.tensor_tensor_scan(row(R_M, 0, TP), row(R_W, 0, TP), row(R_U, 0, TP), 0.0, ALU.add, ALU.max)
                dve.memset(scan_in[:, 0, :, 0:1], -3.0e38)
                dve.tensor_copy(scan_in[:, 1, :, 0:1], m0[:, :].unsqueeze(2))
                dve.tensor_copy(scan_in[:, 0, :, 1:], by_seq(R_W))
                dve.memset(row(R_WI, 0, L), 0.0)
                link(dve.tensor_copy(scan_in[:, 1, :, 1:], by_seq(R_U)))
                link(dve.tensor_tensor_scan(scan_in[:, 2, :, :].rearrange("p b t -> p (b t)"),
                                            scan_in[:, 0, :, :].rearrange("p b t -> p (b t)"),
                                            scan_in[:, 1, :, :].rearrange("p b t -> p (b t)"), 0.0, ALU.add, ALU.max))
                link(dve.tensor_copy(by_seq(R_M), scan_in[:, 2, :, 1:]))

            def make_weight_rows():
                dve.tensor_tensor(row(R_U), row(R_U), row(R_B), ALU.subtract)
                dve.tensor_tensor(row(R_W), row(R_B), row(R_M), ALU.subtract)
                dve.tensor_copy(by_chunk(R_WI)[:, 1:NC, :],
                                by_chunk(R_M)[:, 0:NC - 1, L - 1:L].broadcast_to([H, NC - 1, L]))
                link(dve.tensor_copy(by_seq(R_WI), m0[:, :].unsqueeze(2).broadcast_to([H, B, TS])))
                dve.tensor_tensor(row(R_WI), row(R_WI), row(R_W), ALU.add)
                dve.tensor_tensor(by_chunk(R_WL), by_chunk(R_U), by_chunk(R_W)[:, :, L - 1:L].broadcast_to([H, NC, L]),
                                  ALU.add)
                dve.tensor_tensor(by_seq(R_WL), by_seq(R_U), by_seq(R_W)[:, :, TS - 1:TS].broadcast_to([H, B, TS]),
                                  ALU.add).then_inc(sem("rows_made"), 1)

            for k in range(NZ):
                dve.wait_ge(pe_unit, U_IN + k + 1)
                dve.tensor_copy(halves(z[:, k, :]), pair(B_IN + k if k < Z_GV else k % 2)).then_inc(evac, 1)
                split(U_IN + k + 2)
                if k == S_DECAY:
                    dve.wait_ge(sem("small_in"), 16 * 6)
                    dve.wait_ge(sem("a2_mm"), 1)
                    for n in range(2):
                        ins = dve.tensor_scalar(halves(decay[:, n, :]), ps[:, 4 + 2 * n:6 + 2 * n, 0:HT],
                                                gains[:, G_BA + n:G_BA + n + 1], None, ALU.add)
                    ins.then_inc(sem("y_decay"), 1)
                if k == S_DECAY + 1:
                    make_decay()
                if k in S_DIFF:
                    level_diff(S_DIFF.index(k) + 1)
                if k in S_QK:
                    level_masked(S_QK.index(k))
                    level_qk(S_QK.index(k) + 1)
                if k == S_SUM:
                    level_sum()
                if k == S_IN:
                    into_chunk()
                if k == S_GATE:
                    out_of_chunk()
                    dve.tensor_scalar(row(R_U), z[0:H, Z_GATE, :], gate_b[0:H, 0:1], None, ALU.add)
                    dve.tensor_scalar(row(R_W), z[32:32 + H, Z_GATE, :], gate_b[32:32 + H, 0:1], None, ALU.add)\
                       .then_inc(sem("y_rows"), 1)
                if k == S_ROWS:
                    make_rows()
                if k == S_ROWS + 1:
                    make_weight_rows()

            def gla_gate(j):
                dve.wait_ge(sem("gg_sig"), j + 1)
                dve.tensor_tensor(z[:, Z_GG + j, :], z[:, Z_GG + j, :], gg_sig[j][:, :], ALU.mult)

            def chunk_weights(c, n):
                t0 = c * L
                dve.wait_ge(sem("pe_a"), 9 * c + 1)
                link(dve.tensor_copy(ucol[0:n, :], ps[0:n, 7, 0:2 * H]))
                dve.wait_ge(sem("pe_a"), 9 * c + 2)
                for h in range(H):
                    ins = dve.tensor_scalar(ew[0:n, h, 0:n], ps[0:n, 0, h * n:h * n + n], ucol[0:n, h:h + 1], 0.0,
                                            ALU.add, ALU.min)
                ins.then_inc(sem("w_arg"), 1)
                dve.wait_ge(sem("pe_a"), 9 * c + 3)
                wi = ps[:, 1, 0:H * n].rearrange("p (h t) -> p h t", h=H)
                dve.tensor_copy(il[:, :], wi[:, :, n - 1])
                dve.tensor_tensor(q_in[:, :, 0:n], wi, z[:, Z_MQ:Z_MQ + H, t0:t0 + n], ALU.mult)\
                   .then_inc(sem("q_in_done"), 1)
                dve.wait_ge(sem("pe_a"), 9 * c + 6)
                for h in range(H):
                    ins = dve.tensor_scalar(kw_tok[0:n, h, :], ps[0:n, 4, h * DK:(h + 1) * DK],
                                            ucol[0:n, H + h:H + h + 1], DK ** -0.5, ALU.mult, ALU.mult)
                ins.then_inc(sem("kw_done"), 1)
                dve.wait_ge(sem("w_masked"), c + 1)
                dve.wait_ge(sem("pe_a"), 9 * c + 4)
                dve.scalar_tensor_tensor(out=pw[0:n, :, 0:n], in0=ps[0:n, 3, 0:H * n]
                                         .rearrange("p (h t) -> p h t", h=H), scalar=DK ** -0.5,
                                         in1=ew[0:n, :, 0:n], op0=ALU.mult, op1=ALU.mult).then_inc(sem("p_done"), 1)

            def chunk_heads(c, n):
                t0 = c * L
                dve.wait_ge(sem("pe_a"), 9 * c + 5)
                dve.wait_ge(sem("den_abs"), c + 1)
                if c < NC:
                    dve.wait_ge(sem("num_mm"), c + 1)
                else:
                    dve.wait_ge(sem("num_s"), H)
                link(dve.tensor_tensor(den[:, :, 0:n], ps[:, 2, 0:H * n].rearrange("p (h t) -> p h t", h=H),
                                       den[:, :, 0:n], ALU.max))
                link(dve.reciprocal(den[:, :, 0:n], den[:, :, 0:n]))
                dve.tensor_tensor(z[:, Z_MQ:Z_MQ + H, t0:t0 + n],
                                  ps[:, 0, 0:H * n].rearrange("p (h t) -> p h t", h=H), den[:, :, 0:n], ALU.mult)\
                   .then_inc(sem("heads_done"), 1)

            for c in range(NC):
                chunk_weights(c, L)
                gla_gate(c)
                chunk_heads(c, L)
                dve.wait_ge(sem("state_mm"), c + 1)
                if c == 0:
                    dve.wait_ge(sem("zeros_set"), 2)
                    dve.tensor_copy(c_st[:, :, :], ps[:, 4, :].rearrange("p (h v) -> p h v", h=H))
                    dve.tensor_copy(n_st[:, :, :], ps[:, 5, :].rearrange("p (h v) -> p h v", h=H))
                    for h in range(H):
                        r = 64 * (h % 2)
                        ins = dve.tensor_copy(s_st[r:r + 64, h, :], ps[r:r + 64, 6, h * DV:(h + 1) * DV])
                else:
                    for h in range(H):
                        dve.scalar_tensor_tensor(out=c_st[:, h, :], in0=c_st[:, h, :], scalar=il[:, h:h + 1],
                                                 in1=ps[:, 4, h * DV:(h + 1) * DV], op0=ALU.mult, op1=ALU.add)
                        dve.scalar_tensor_tensor(out=n_st[:, h, :], in0=n_st[:, h, :], scalar=il[:, h:h + 1],
                                                 in1=ps[:, 5, h * 128:(h + 1) * 128], op0=ALU.mult, op1=ALU.add)
                        r = 64 * (h % 2)
                        ins = dve.scalar_tensor_tensor(out=s_st[r:r + 64, h, :], in0=s_st[r:r + 64, h, :],
                                                 scalar=e_last[r:r + 64, h // 2, c:c + 1],
                                                 in1=ps[r:r + 64, 6, h * DV:(h + 1) * DV], op0=ALU.mult, op1=ALU.add)
                ins.then_inc(sem("chunk_done"), 1)
                dve.wait_ge(sem("chunk_done"), c + 1)

            c, n = NC, NS
            chunk_weights(c, n)
            dve.wait_ge(sem("n_mm"), 1)
            link(dve.tensor_copy(s_n[:, :, :], ps[:, 6, 300:300 + NS].rearrange("p (b h) -> p b h", b=B)))
            dve.tensor_tensor(s_qn[:, :, :].rearrange("p h (b t) -> p h b t", b=B),
                              q_in[:, :, 0:NS].rearrange("p h (b t) -> p h b t", b=B),
                              s_n[:, :, :].rearrange("p b h -> p h b").unsqueeze(3).broadcast_to([128, H, B, TS]),
                              ALU.mult).then_inc(sem("qn_done"), 1)
            il_s = rinv[:, 0:H * B].rearrange("p (h b) -> p h b", h=H)
            dve.tensor_copy(il_s, ps[:, 1, 0:H * n].rearrange("p (h b t) -> p h b t", h=H, b=B)[:, :, :, TS - 1])\
               .then_inc(sem("il_s_done"), 1)
            dve.wait_ge(sem("il_s_done"), 1)

            def own_values(u):
                if u >= 2:
                    dve.wait_ge(sem("upd_mm"), u - 1)
                src = (v_tok if u < H else gv_tok)[0:NS, u % H, :]
                dve.tensor_tensor(v_own[u % 2][:, :, :], src.unsqueeze(1).broadcast_to([NS, B, DV]),
                                  own.unsqueeze(2).broadcast_to([NS, B, DV]), ALU.mult).then_inc(sem("v_own"), 1)

            def in_banks(t3d):
                return t3d.rearrange("p b v -> p (b v)").rearrange("p (k f) -> p k f", k=2)

            dve.wait_ge(sem("tok_done"), 3 * c + 3)
            for h in range(H):
                own_values(h)
                st = ring[h % 3]
                dve.wait_ge(sem(f"state_in{h % 3}"), 16 * (h // 3 + 1))
                dve.wait_ge(sem("num_s"), h + 1)
                link(dve.tensor_tensor(st[:, :, :], st[:, :, :], il_s[:, h, :].unsqueeze(2).broadcast_to([128, B, DV]),
                                       ALU.mult))
                dve.wait_ge(sem("upd_mm"), h + 1)
                q = 4 + 2 * (h % 2)
                dve.tensor_tensor(in_banks(st[:, :, :]), ps[:, q:q + 2, :], in_banks(st[:, :, :]), ALU.add)\
                   .then_inc(sem("upd_free"), 1)
            dve.wait_ge(sem("nnew_mm"), 1)
            link(dve.tensor_tensor(s_n2[:, :, :], s_n[:, :, :], il_s.rearrange("p h b -> p b h"), ALU.mult))
            dve.tensor_tensor(s_n2[:, :, :].rearrange("p b h -> p h b"),
                              ps[:, 3, 256:256 + H * B].rearrange("p (h b) -> p h b", h=H),
                              s_n2[:, :, :].rearrange("p b h -> p h b"), ALU.add).then_inc(sem("n2_done"), 1)
            dve.wait_ge(sem("n2_mm"), 1)
            dve.tensor_copy(s_nrow2[:, :], ps[0:NS, 3, 384:384 + DK]).then_inc(sem("n_new"), 1)
            chunk_heads(c, n)
            for h in range(H):
                u, r, st = H + h, 64 * (h % 2), ring[(H + h // 2) % 3]
                own_values(u)
                dve.wait_ge(sem(f"state_in{(H + h // 2) % 3}"), 32)
                dve.wait_ge(sem("o_s"), 2 * (h // 2) + 2)
                link(dve.tensor_tensor(st[r:r + 64, :, :], st[r:r + 64, :, :],
                                       e_last[r:r + 64, h // 2, NC:NC + B].unsqueeze(2).broadcast_to([64, B, DV]),
                                       ALU.mult))
                dve.wait_ge(sem("upd_mm"), u + 1)
                q = 4 + 2 * (u % 2)
                dve.tensor_tensor(in_banks(st[r:r + 64, :, :]), ps[r:r + 64, q:q + 2, :],
                                  in_banks(st[r:r + 64, :, :]), ALU.add).then_inc(sem("upd_free"), 1)
            dve.wait_ge(sem("upd_free"), 2 * H)
            dve.sem_inc(sem("chunk_done"), 1)

            def head(j):
                return z[:, Z_MQ + j, :] if j < H else z[:, Z_GV + j - H, :]

            for j in range(2 * H + 1):
                if j < 2 * H:
                    og = z[:, Z_MO + j, :] if j < H else z[:, Z_GG + j - H, :]
                    gc = G_ML + j if j < H else G_GLA + j - H
                    dve.wait_ge(sem("hn_sq"), j + 1)
                    link(dve.scalar_tensor_tensor(out=head(j), in0=head(j), scalar=gains[:, gc:gc + 1], in1=og,
                                                  op0=ALU.mult, op1=ALU.mult))
                    dve.wait_ge(sem("hn_inv"), j + 1)
                    dve.tensor_tensor(head(j), head(j), sig[j % 2][:, :], ALU.mult).then_inc(sem("hn_y"), 1)
                if j >= 1:
                    dve.wait_ge(sem("ym_hi"), j)
                    dve.tensor_tensor(xn_lo[:, j - 1, :], head(j - 1), xn_hi[:, j - 1, :].bitcast(F32), ALU.subtract)\
                       .then_inc(sem("ym_lo"), 1)
            residual(U_OUT, B_OUT, 16)
            norm(2, G_XA)
            with dve.Fori(0, 2) as i:
                for k in range(4):
                    dve.wait_ge(pe_unit, i * 4 + (U_XQ + k + 1))
                    dve.tensor_copy(halves(xq[:, bass.ds(i * 4 + k, 1), :].rearrange("p a t -> p (a t)")),
                                    pair(B_XQ + k)).then_inc(evac, 1)
                    split(U_XQ + k + 2, i, 4)

            def softmax_max(scores, heads):
                link(dve.tensor_reduce(xmx[:, 8:8 + heads], scores, AX.X, ALU.max))
                dve.tensor_scalar(xmx[:, 0:heads], xmx[:, 8:8 + heads], -1.0 / 16, None, ALU.mult)\
                   .then_inc(sem("x_max"), 1)

            def softmax_scale(k, pr, heads):
                dve.wait_ge(sem("x_exp"), k + 1)
                link(dve.reciprocal(xmx[:, 8:8 + heads], xmx[:, 4:4 + heads]))
                for h in range(heads):
                    ins = dve.tensor_scalar(pr[:, h, :], pr[:, h, :], xmx[:, 8 + h:9 + h], None, ALU.mult)
                ins.then_inc(sem("p_ready"), 1)

            dve.wait_ge(sem("kT_mm"), 1)
            dve.tensor_copy(kT[0][:, 4:8, :], ps[:, 2:4, :].rearrange("p b (k m) -> p (b k) m", k=2))\
               .then_inc(sem("kT_dve"), 1)
            link(dve.memset(q_pad[:, :, :, :], 0.0))
            for h in range(H):
                for par in range(2):
                    row = 16 * par + TS * h
                    ins = dve.tensor_copy(q_pad[:, 2 * h:2 * h + 2, par::2, row:row + TS],
                                          xq[:, 2 * h:2 * h + 2, TP:T].rearrange("p k (b t) -> p k b t", b=B)
                                          [:, :, par::2, :])
            ins.then_inc(sem("q_padded"), 1)
            for tb in range(NC):
                q = 4 * (tb % 2)
                dve.wait_ge(sem("sc_mm"), tb + 1)
                sc = ps[:, q:q + 2, :].rearrange("p b (k m) -> p (b k) m", k=2)
                softmax_max(sc, H)
                softmax_scale(tb, prob[tb % 2], H)
                dve.wait_ge(sem("pT_mm"), tb + 1)
                dve.tensor_copy(probT[tb % 2][:, :, :], ps[:, q + 2:q + 4, :].rearrange("p b (k t) -> p (b k) t", k=4))\
                   .then_inc(sem("pT_copied"), 1)
                dve.wait_ge(sem("av_hi"), tb + 1)
                dve.tensor_tensor(xn_lo[:, :, tb * 128:tb * 128 + 128],
                                  ps[:, q:q + 2, :].rearrange("p b (k t) -> p (b k) t", k=4),
                                  xn_hi[:, :, tb * 128:tb * 128 + 128].bitcast(F32), ALU.subtract)\
                   .then_inc(sem("av_lo"), 1)
            for b in range(B):
                dve.wait_ge(sem("kT_mm"), 2 * b + 3)
                if b >= 2:
                    dve.wait_ge(sem("ssc_mm"), b - 1)
                dve.tensor_copy(kT[(b + 1) % 2][:, 4:8, :], k_banks(2 * b + 1)).then_inc(sem("kT_dve"), 1)
            dve.memset(p_pad[:, :, :, :, :], 0.0)
            dve.wait_ge(sem("ssc_mm"), B)
            softmax_max(ps[:, 4, 0:MEM].unsqueeze(1), 1)
            softmax_scale(NC, prob[0], 1)
            dve.wait_ge(sem("pT_mm"), NC + 1)
            p_rows = ps[:, 7, 0:MEM].rearrange("p (m b h t) -> p m h b t", m=2, b=B, h=H)
            for b in range(B):
                ins = dve.tensor_copy(p_pad[:, :, :, b, TS * b:TS * b + TS], p_rows[:, :, :, b, :])
            ins.then_inc(sem("pT_copied"), 1)
            dve.wait_ge(sem("sav_mm"), B)
            dve.tensor_copy(s_av[0:NS, :, :].rearrange("p (h e) f -> p h (e f)", h=H), ps[0:NS, 0:H, 0:256])\
               .then_inc(sem("sav_copied"), 1)
            dve.wait_ge(sem("av_hi"), NC + 1)
            dve.tensor_tensor(xn_lo[:, :, TP:T], ps[:, 5, 0:ND * NS].rearrange("p (k t) -> p k t", k=ND),
                              xn_hi[:, :, TP:T].bitcast(F32), ALU.subtract).then_inc(sem("av_lo"), 1)

            residual(U_XO, B_XO, 24)
            norm(3, G_FFN2)
            ffn_up(1, U_UP2, B_UP2)
            ffn_down(U_DN2, B_DN2, 32, True)
            dve.wait_ge(sem("norm_inv"), 5)
            for d in range(ND):
                dve.scalar_tensor_tensor(out=yf[:, d, :], in0=x[:, d, :], scalar=gains[:, G_FIN + d:G_FIN + d + 1],
                                         in1=rinv[:, :], op0=ALU.mult, op1=ALU.mult).then_inc(sem("yf_done"), 1)

        @block.tensor
        def _(pe):
            pe_unit, evac, lo_done = sem("pe_unit"), sem("evac"), sem("lo_done")

            def mm(out, lhsT, rhs, start=True, stop=True):
                return pe.matmul(out, lhsT, rhs, start=start, stop=stop)

            pe.wait_ge(sem("const_in"), 16)
            pe.wait_ge(sem("mem_gain_in"), 16)
            pe.transpose(ps[:, 7, 0:ND], mem_gain[:, :], const[0:ND, 0:ND]).then_inc(sem("gain_mm"), 1)
            pe.wait_ge(sem("mem_in"), 16)
            for d in range(ND):
                for mb in range(2):
                    c = MEM * (d % 2) + 128 * mb
                    ins = pe.transpose(ps[:, d // 2, c:c + 128], mem_nat[:, mb, d * 128:d * 128 + 128], ident)
                ins.then_inc(sem("memT_mm"), 1)

            def transpose_x(d):
                q = 4 + 2 * (d % 2)
                if d == 0:
                    pe.wait_ge(sem("x_in"), 16)
                    pe.wait_ge(sem("xs_in"), 16)
                if d >= 2:
                    pe.wait_ge(sem("x_made"), d - 1)
                for c in range(NC):
                    pe.transpose(ps[:, q, c * L:(c + 1) * L], xp_nat[:, c, d * 128:d * 128 + 128], ident)
                pe.transpose(ps[:, q + 1, 0:NS], xs_nat[:, d * 128:d * 128 + 128], const[0:NS, 0:NS])\
                  .then_inc(sem("xT_mm"), 1)
                if d == ND - 1:
                    pe.wait_ge(sem("x_made"), d)
                    pe.wait_ge(sem("gains_in"), 16 * 9)
                    pe.transpose(ps[:, 5, 256:256 + N_GAIN], gain_rows[:, :], const[0:N_GAIN, 0:N_GAIN])\
                      .then_inc(sem("gain_mm"), 1)

            def norm(g, buf):
                pe.wait_ge(sem("acc_done"), 8 * (g + 1))
                if buf >= 4:
                    pe.wait_ge(evac, buf - 3)
                mm(pair(buf)[:, 0, :], ones, acc[:, 0:HT])
                mm(pair(buf)[:, 1, :], ones, acc[:, HT:T]).then_inc(sem("norm_mm"), 1)

            pe.wait_ge(sem("mem_lo_done"), 1)
            for u in range(16):
                if u == 8:
                    pe.wait_ge(sem("x_made"), ND)
                if u == 9:
                    pe.wait_ge(sem("gains_made"), 1)
                    norm(0, B_N1)
                pe.wait_ge(lo_done, u + 1)
                buf = (0, 1, 3, 4)[u // 4]
                if u == 12:
                    pe.wait_ge(evac, 1)
                for kt in range(2):
                    k = 2 * (u % 4) + kt
                    cols = slice(512 * kt, 512 * kt + 512)
                    for mb in range(2):
                        dst, toks = ps[:, 2 * (buf % 4) + mb, :], slice(128 * mb, 128 * mb + 128)
                        mm(dst, mem_hi[:, k, toks], w_hi[u % 2][:, cols], k == 0, False)
                        mm(dst, mem_hi[:, k, toks], w_lo[u % 2][:, cols], False, False)
                        ins = mm(dst, mem_lo[:, k, toks], w_hi[u % 2][:, cols], False, k == 7)
                ins.then_inc(pe_unit, 1)
                if u < ND:
                    transpose_x(u)

            def unit(u, buf, hi, lo, k0, nk, first, last, only=None):
                for j in (range(nk) if only is None else (only,)):
                    wh = w_hi[u % 2][:, 128 * j:128 * j + 128]
                    wl = w_lo[u % 2][:, 128 * j:128 * j + 128]
                    for n, (w, m) in enumerate(((wh, hi), (wh, lo), (wl, hi))):
                        for half in range(2):
                            ins = mm(ps[:, 2 * (buf % 4) + half, 0:HT], w, m[:, k0 + j, half * HT:(half + 1) * HT],
                                     first and j == 0 and n == 0, last and j == nk - 1 and n == 2)
                if only is None or only == nk - 1:
                    ins.then_inc(pe_unit, 1)

            LAG = 2

            def first_two(u0, b0, made, base_):
                pe.wait_ge(lo_done, u0 + 2)
                pe.wait_ge(evac, b0)
                for d in range(ND + LAG):
                    if d < ND:
                        pe.wait_ge(made, base_ + d + 1)
                        unit(u0, b0, xn_hi, xn_lo, 0, 8, True, True, d)
                    if d >= LAG:
                        unit(u0 + 1, b0 + 1, xn_hi, xn_lo, 0, 8, True, True, d - LAG)

            def blocks(u0, b0, bodies, made=None, base_=0):
                def step(k, i=0):
                    pe.wait_ge(lo_done, i * 4 + (u0 + k + 1))
                    pe.wait_ge(evac, i * 4 + (b0 + k - 3))
                    unit(u0 + k, b0 + k, xn_hi, xn_lo, 0, 8, True, True)

                if made is not None:
                    first_two(u0, b0, made, base_)
                    for k in (2, 3):
                        step(k)
                    bodies, u0, b0 = bodies - 1, u0 + 4, b0 + 4
                with pe.Fori(0, bodies) as i:
                    for k in range(4):
                        step(k, i)

            def ffn_down(n, u0, b0):
                pe.wait_ge(sem("hl_done"), NF * (n + 1))
                with pe.Fori(0, 2) as i:
                    for k in range(12):
                        pe.wait_ge(lo_done, i * 12 + (u0 + k + 1))
                        if k % 3 == 0:
                            pe.wait_ge(evac, i * 4 + (b0 + k // 3 - 3))
                        lo, hi = DN_K[k % 3]
                        unit(u0 + k, b0 + k // 3, h_hi, h_lo, lo, hi - lo, k % 3 == 0, k % 3 == 2)

            blocks(U_UP1, B_UP1, NF // 2, sem("xnl_done"), 0)
            ffn_down(0, U_DN1, B_DN1)
            norm(1, B_N2)
            first_two(U_IN, B_IN, sem("xnl_done"), 8)

            def decay_product():
                pe.wait_ge(evac, B_IN + Z_GV)
                pe.wait_ge(sem("small_in"), 16 * 6)
                for n in range(2):
                    for half in range(2):
                        ins = mm(ps[:, 4 + 2 * n + half, 0:HT], a2w[:, 128 * n:128 * n + 128],
                                 z[0:RANK, Z_GA, half * HT:(half + 1) * HT])
                ins.then_inc(sem("a2_mm"), 1)

            def level_scores(n):
                if n == 0:
                    q_, k_ = z[:, Z_GQ:Z_GQ + 2, :], z[:, Z_GK:Z_GK + 2, :]
                    pe.wait_ge(evac, B_IN + Z_GV)
                    pe.wait_ge(sem("y_decay"), 1)
                else:
                    q_, k_ = lv_q[n % 2][:, :, :], lv_k[n % 2][:, :, :]
                    pe.wait_ge(sem("lv_qk"), n)
                if n >= 2:
                    pe.wait_ge(sem("lv_masked"), n - 1)
                for r in range(2):
                    rr = slice(64 * r, 64 * r + 64)
                    bank = 4 + 2 * (n % 2) + r
                    for c in range(NC):
                        for pr in range(2):
                            at_ = (c * 2 + pr) * 64
                            if n <= LEVELS:
                                for j in range(2):
                                    tt = slice(c * L + 64 * j, c * L + 64 * j + 64)
                                    ins = mm(ps[64 * j:64 * j + 64, bank, at_:at_ + 64], k_[rr, pr, tt],
                                             q_[rr, pr, tt])
                            else:
                                ins = mm(ps[0:64, bank, at_:at_ + 64], k_[rr, pr, c * L:c * L + 64],
                                         q_[rr, pr, c * L + 64:c * L + 128])
                if n == LEVELS + 1:
                    pe.wait_ge(sem("lv_masked"), n)
                    for m in range(3):
                        for r in range(2):
                            rr = slice(64 * r, 64 * r + 64)
                            for pr in range(2):
                                at_ = (m * 2 + pr) * NS
                                k_ = s_lv[rr, m - 1, 1, pr, :] if m else z[rr, Z_GK + pr, TP:T]
                                q_ = s_lv[rr, m - 1, 0, pr, :] if m else z[rr, Z_GQ + pr, TP:T]
                                ins = mm(ps[0:NS, 4 + r, at_:at_ + NS], k_, q_)
                ins.then_inc(sem("lv_mm"), 1)

            for k in range(2, NZ):
                pe.wait_ge(lo_done, U_IN + k + 1)
                pe.wait_ge(evac, B_IN + k - (3 if k < Z_GV else 1))
                unit(U_IN + k, B_IN + k if k < Z_GV else k % 2, xn_hi, xn_lo, 0, 8, True, True)
                if k == S_DECAY - 1:
                    decay_product()
                if k in S_SCORES:
                    level_scores(S_SCORES.index(k))

            def chunk_first(c, n):
                t0 = c * L
                tt = slice(t0, t0 + n)
                if c == 0:
                    pe.wait_ge(sem("levels_done"), 1)
                    pe.wait_ge(sem("rows_exp"), 3)
                    pe.wait_ge(evac, B_IN + NZ)
                else:
                    pe.wait_ge(sem("heads_done"), c)
                    pe.wait_ge(sem("gla_out"), c)

                def spread(bank, r):
                    for h in range(H):
                        ins = mm(ps[:, bank, h * n:h * n + n], sel[:, h, :], rows[:, r, tt])
                    ins.then_inc(sem("pe_a"), 1)

                pe.transpose(ps[0:n, 7, 0:H], rows[:, R_U, tt], const[0:H, 0:H])
                pe.transpose(ps[0:n, 7, H:2 * H], rows[:, R_WL, tt], const[0:H, 0:H])\
                  .then_inc(sem("pe_a"), 1)
                spread(0, R_W)
                spread(1, R_WI)
                for h in range(H):
                    ins = mm(ps[0:n, 3, h * n:h * n + n], z[:, Z_MK + h, tt], z[:, Z_MQ + h, tt])
                ins.then_inc(sem("pe_a"), 1)
                spread(2, R_EM)
                if c:
                    pe.wait_ge(sem("chunk_done"), c)

                def to_tokens(bank, zb, blocks_):
                    for h in range(blocks_):
                        ins = pe.transpose(ps[0:n, bank, h * 128:h * 128 + 128], z[:, zb + h, tt], ident)
                    ins.then_inc(sem("pe_a"), 1)

                to_tokens(4, Z_MK, 4)
                to_tokens(5, Z_MV, 4)
                to_tokens(6, Z_GK, 2)
                pe.wait_ge(sem("w_arg"), c + 1)
                to_tokens(7, Z_GV, 4)

            for c in range(NC):
                chunk_first(c, L)
                tt = slice(c * L, c * L + L)
                pe.wait_ge(sem("q_in_done"), c + 1)
                pe.wait_ge(sem("kw_done"), c + 1)
                pe.wait_ge(sem("p_done"), c + 1)
                pe.wait_ge(sem("tok_done"), 3 * c + 3)
                for h in range(H):
                    hh = slice(h * L, h * L + L)
                    ins = mm(ps[:, 3, hh], ones, pw[:, h, :], True, c == 0)
                    if c:
                        ins = mm(ps[:, 3, hh], n_st[:, h, :], q_in[:, h, :], False, True)
                ins.then_inc(sem("den_mm"), 1)
                for h in range(H):
                    hh = slice(h * L, h * L + L)
                    ins = mm(ps[:, 0, hh], v_tok[:, h, :], pw[:, h, :], True, c == 0)
                    if c:
                        ins = mm(ps[:, 0, hh], c_st[:, h, :], q_in[:, h, :], False, True)
                ins.then_inc(sem("num_mm"), 1)
                for h in range(H):
                    hh = slice(h * L, h * L + L)
                    ins = mm(ps[:, 7, hh], gv_tok[:, h, :], gla_a[:, c, h, :], True, c == 0)
                    if c:
                        ins = mm(ps[:, 7, hh], s_st[:, h, :], z[:, Z_GQ + h // 2, tt], False, True)
                ins.then_inc(sem("gla_mm"), 1)
                for h in range(H):
                    mm(ps[:, 4, h * DV:(h + 1) * DV], kw_tok[:, h, :], v_tok[:, h, :])
                    mm(ps[:, 5, h * 128:(h + 1) * 128], kw_tok[:, h, :], ones)
                for pr in range(2):
                    ins = mm(ps[:, 6, 256 * pr:256 * pr + 256], gk_tok[:, pr, :],
                             gv_tok[:, 2 * pr:2 * pr + 2, :].rearrange("p h v -> p (h v)"))
                ins.then_inc(sem("state_mm"), 1)

            c, n = NC, NS
            chunk_first(c, n)
            pe.wait_ge(sem("n_in"), 16)
            pe.wait_ge(sem("tok_done"), 3 * c + 3)
            pe.transpose(ps[:, 6, 300:300 + NS], s_nrow[:, :], const[0:NS, 0:NS]).then_inc(sem("n_mm"), 1)
            pe.wait_ge(sem("kw_done"), c + 1)
            pe.wait_ge(sem("p_done"), c + 1)
            pe.wait_ge(sem("qn_done"), 1)
            for h in range(H):
                mm(ps[:, 3, h * n:h * n + n], const[0:NS, C_ONE:C_ONE + 128], pw[0:n, h, 0:n], True, False)
                ins = mm(ps[:, 3, h * n:h * n + n], ones, s_qn[:, h, :], False, True)
            ins.then_inc(sem("den_mm"), 1)

            def update(u, keys):
                pe.wait_ge(sem("v_own"), u + 1)
                if u >= 2:
                    pe.wait_ge(sem("upd_free"), u - 1)
                q = 4 + 2 * (u % 2)
                vo = v_own[u % 2][:, :, :].rearrange("p b v -> p (b v)")
                mm(ps[:, q, :], keys, vo[:, 0:512])
                mm(ps[:, q + 1, :], keys, vo[:, 512:1024]).then_inc(sem("upd_mm"), 1)

            for h in range(H):
                pe.wait_ge(sem(f"state_in{h % 3}"), 16 * (h // 3 + 1))
                mm(ps[:, 0, h * n:h * n + n], v_tok[0:n, h, :], pw[0:n, h, 0:n], True, False)
                for b in range(B):
                    s = h * n + TS * b
                    ins = mm(ps[:, 0, s:s + TS], ring[h % 3][:, b, :], q_in[:, h, TS * b:TS * b + TS], False,
                             b == B - 1)
                ins.then_inc(sem("num_s"), 1)
                update(h, kw_tok[0:n, h, :])
            pe.wait_ge(sem("den_abs"), c + 1)
            for h in range(H):
                ins = mm(ps[:, 3, 256 + h * B:256 + h * B + B], kw_tok[0:n, h, :], own)
            ins.then_inc(sem("nnew_mm"), 1)
            pe.wait_ge(sem("n2_done"), 1)
            pe.transpose(ps[0:NS, 3, 384:384 + DK], s_n2[:, :, :].rearrange("p b h -> p (b h)"), ident)\
              .then_inc(sem("n2_mm"), 1)
            pe.wait_ge(sem("il_s_done"), 1)
            for pr in range(2):
                slot = (H + pr) % 3
                pe.wait_ge(sem(f"state_in{slot}"), 32)
                for r in range(2):
                    h = 2 * pr + r
                    mm(ps[:, 1, h * n:h * n + n], gv_tok[0:n, h, :], s_a[:, h, :], True, False)
                    for b in range(B):
                        s = h * n + TS * b
                        ins = mm(ps[:, 1, s:s + TS], ring[slot][:, b, :], s_q[:, r, pr, TS * b:TS * b + TS], False,
                                 b == B - 1)
                    ins.then_inc(sem("o_s"), 1)
                for r in range(2):
                    update(H + 2 * pr + r, gk_tok[0:n, pr, :])

            pe.wait_ge(sem("chunk_done"), NC + 1)
            pe.wait_ge(sem("gla_out"), NC + 1)
            for j in range(2 * H):
                pe.wait_ge(sem("hn_sq"), j + 1)
                if j >= 4:
                    pe.wait_ge(sem("hn_root"), j - 3)
                for half in range(2):
                    ins = mm(pair(j)[:, half, :], ones, sq[j % 2][:, half * HT:(half + 1) * HT])
                ins.then_inc(sem("hn_mm"), 1)
            pe.wait_ge(sem("hn_root"), 2 * H)
            blocks(U_OUT, B_OUT, 2, sem("ym_lo"), 0)
            norm(2, B_N3)
            blocks(U_XQ, B_XQ, 2, sem("xnl_done"), 16)

            def k_ready(n):
                pe.wait_ge(sem("kT_act"), n)
                pe.wait_ge(sem("kT_dve"), n)

            pe.wait_ge(evac, B_XQ + ND)
            pe.wait_ge(sem("kv_in0"), 16)
            for k in range(ND):
                for mb in range(2):
                    col = MEM * (k % 2) + 128 * mb
                    ins = pe.transpose(ps[:, k // 2, col:col + 128], kv[0][:, mb, k * 128:k * 128 + 128], ident)
            ins.then_inc(sem("kT_mm"), 1)
            k_ready(1)

            def scores(tb):
                q = 4 * (tb % 2)
                if tb >= 2:
                    pe.wait_ge(sem("av_lo"), tb - 1)
                for h in range(H):
                    for dd in range(2):
                        ins = mm(ps[:, q + h // 2, MEM * (h % 2):MEM * (h % 2) + MEM],
                                 xq[:, 2 * h + dd, tb * 128:tb * 128 + 128], kT[0][:, 2 * h + dd, :], dd == 0, dd == 1)
                ins.then_inc(sem("sc_mm"), 1)

            scores(0)
            pe.wait_ge(sem("kv_in1"), 16)
            for tb in range(NC):
                if tb + 1 < NC:
                    scores(tb + 1)
                q = 4 * (tb % 2)
                pe.wait_ge(sem("p_ready"), tb + 1)
                for k in range(ND):
                    ins = pe.transpose(ps[:, q + 2 + k // 4, 128 * (k % 4):128 * (k % 4) + 128],
                                       prob[tb % 2][:, k // 2, 128 * (k % 2):128 * (k % 2) + 128], ident)
                ins.then_inc(sem("pT_mm"), 1)
                pe.wait_ge(sem("pT_copied"), tb + 1)
                for k in range(ND):
                    for mb in range(2):
                        ins = mm(ps[:, q + k // 4, 128 * (k % 4):128 * (k % 4) + 128],
                                 kv[1][:, mb, k * 128:k * 128 + 128], probT[tb % 2][:, 2 * (k // 2) + mb, :],
                                 mb == 0, mb == 1)
                ins.then_inc(sem("av_mm"), 1)
            pe.wait_ge(sem("av_lo"), NC)

            def transpose_sample_k(b):
                buf = b + 2
                pe.wait_ge(sem(f"kv_in{buf % KV_RING}"), 16 * (buf // KV_RING + 1))
                for half in range(2):
                    n = 2 * b + half
                    if n >= 3:
                        pe.wait_ge(sem("kT_dve" if half == 0 else "kT_act"), (n - 3) // 2 + 2)
                    for k in range(4 * half, 4 * half + 4):
                        for mb in range(2):
                            ins = pe.transpose(k_banks(n)[:, k % 4, 128 * mb:128 * mb + 128],
                                               kv[buf % KV_RING][:, mb, k * 128:k * 128 + 128], ident)
                    ins.then_inc(sem("kT_mm"), 1)

            pe.wait_ge(sem("q_padded"), 1)
            transpose_sample_k(0)
            for b in range(B):
                if b + 1 < B:
                    transpose_sample_k(b + 1)
                k_ready(b + 2)
                kt = kT[(b + 1) % 2]
                rows_ = slice(32 * (b // 2), 32 * (b // 2) + 32)
                for k in range(ND):
                    ins = mm(ps[rows_, 4, 0:MEM], q_pad[:, k, b, :], kt[:, k, :], b % 2 == 0 and k == 0,
                             b % 2 == 1 and k == ND - 1)
                ins.then_inc(sem("ssc_mm"), 1)
            pe.wait_ge(sem("p_ready"), NC + 1)
            for mb in range(2):
                ins = pe.transpose(ps[:, 7, 128 * mb:128 * mb + 128], prob[0][:, 0, 128 * mb:128 * mb + 128], ident)
            ins.then_inc(sem("pT_mm"), 1)
            pe.wait_ge(sem("pT_copied"), NC + 1)
            for b in range(B):
                n = 10 + b
                pe.wait_ge(sem(f"kv_in{n % KV_RING}"), 16 * (n // KV_RING + 1))
                for h in range(H):
                    for mb in range(2):
                        ins = mm(ps[0:NS, h, 0:256], p_pad[:, mb, h, b, :], kv[n % KV_RING][:, mb, 256 * h:256 * h + 256],
                                 b == 0 and mb == 0, b == B - 1 and mb == 1)
                ins.then_inc(sem("sav_mm"), 1)
            pe.wait_ge(sem("sav_copied"), 1)
            for k in range(ND):
                ins = pe.transpose(ps[:, 5, NS * k:NS * k + NS], s_av[0:NS, k, :], const[0:NS, 0:NS])
            ins.then_inc(sem("savT_mm"), 1)

            pe.wait_ge(sem("av_lo"), NC + 1)
            blocks(U_XO, B_XO, 2)
            norm(3, B_N4)
            blocks(U_UP2, B_UP2, NF // 2, sem("xnl_done"), 24)
            ffn_down(1, U_DN2, B_DN2)
            norm(4, B_N5)
            pe.wait_ge(evac, B_N5 + 1)
            for c in range(NC + 1):
                n = L if c < NC else NS
                if c == 4:
                    pe.wait_ge(sem("y_copied"), 1)
                for d in range(ND):
                    if c == 0:
                        pe.wait_ge(sem("yf_done"), d + 1)
                    ins = pe.transpose(ps[0:n, 2 * (c % 4) + d // 4, 128 * (d % 4):128 * (d % 4) + 128],
                                       yf[:, d, c * L:c * L + n], ident)
                ins.then_inc(sem("yT_mm"), 1)


_INS = ["x_prompt", "x_sample", "mem_prompt", "cache_mem_k", "cache_mem_v", "state_mlstm_c", "state_mlstm_n",
        "state_mlstm_m", "state_gla_s", "ffn1_norm_g", "ffn1_w_gate", "ffn1_w_up", "ffn1_w_down", "mix_norm_g",
        "w_in", "mlstm_b_i", "mlstm_b_f", "mlstm_out_g", "gla_w_a2", "gla_b_a", "gla_out_g", "w_out",
        "xattn_norm_g", "mem_norm_g", "xattn_w_q", "xattn_w_k", "xattn_w_v", "xattn_w_o", "ffn2_norm_g",
        "ffn2_w_gate", "ffn2_w_up", "ffn2_w_down", "final_norm_g"]
_OUTS = [("y_prompt", (1, TP, D)), ("y_sample", (B, TS, D)), ("mem_k", (1, 1, MEM, H, D // H)),
         ("mem_v", (1, 1, MEM, H, D // H)), ("mlstm_c_p", (1, 1, H, DK, DV)), ("mlstm_n_p", (1, 1, H, DK)),
         ("mlstm_m_p", (1, 1, H)), ("gla_s_p", (1, 1, H, GK, DV)), ("mlstm_c_s", (1, B, H, DK, DV)),
         ("mlstm_n_s", (1, B, H, DK)), ("mlstm_m_s", (1, B, H)), ("gla_s_s", (1, B, H, GK, DV))]


def _constants(np):
    c = np.zeros((128, N_CONST), np.float32)
    c[:, C_ID:C_ID + 128] = np.eye(128)
    c[:, C_ONE:C_ONE + 128] = 1.0
    s, t = np.arange(128)[:, None] % 64, np.arange(64)[None, :]
    for n in range(LEVELS + 1):
        if n == 0:
            mask = s == t
        else:
            half = 1 << (n - 1)
            mask = (s // (2 * half) == t // (2 * half)) & (s % (2 * half) < half) & (t % (2 * half) >= half)
        c[:, C_LEVEL + 64 * n:C_LEVEL + 64 * n + 64] = mask * GK ** -0.5
    s, t = np.arange(128)[:, None], np.arange(128)[None, :]
    c[:, C_CAUSAL:C_CAUSAL + 128] = s <= t
    t = np.arange(T)
    c[:, C_RESTART:C_RESTART + T] = np.where(t < TP, t % L != 0, t % TS != 0)
    s, t = np.arange(NS)[:, None], np.arange(NS)[None, :]
    c[0:NS, C_SCAUSAL:C_SCAUSAL + NS] = (s <= t) & (s // TS == t // TS)
    c[0:NS, C_OWN:C_OWN + B] = s // TS == np.arange(B)[None, :]
    sel = np.zeros((H, H * 128), np.float32)
    for h in range(H):
        sel[h, h * 128:(h + 1) * 128] = 1.0
    return c, sel


def kernel(**inputs):
    import numpy as _np
    import concourse.bacc as _bacc
    from concourse import mybir as _mybir
    from concourse.bass_utils import run_bass_kernel_spmd as _run

    nc = _bacc.Bacc("TRN2", target_bir_lowering=False, num_devices=1)
    given = {name: _np.ascontiguousarray(inputs[name]) for name in _INS}
    given["consts"], given["sel"] = _constants(_np)
    arrays, a, o = {}, {}, {}
    for name, value in given.items():
        arrays[f"in_{name}"] = value
        a[name] = nc.dram_tensor(f"in_{name}", value.shape, _mybir.dt.from_np(value.dtype), kind="ExternalInput").ap()
    for name, shape in _OUTS:
        o[name] = nc.dram_tensor(f"out_{name}", shape, _mybir.dt.float32, kind="ExternalOutput").ap()
    build(nc, a, o)
    r = _run(nc, [arrays], core_ids=[0])
    return tuple(r.results[0][f"out_{name}"] for name, _ in _OUTS)
```

```python
import concourse.bass as bass
from concourse import mybir
from contextlib import ExitStack

D = 1024
ND = D // 128
TP, B, TS = 512, 8, 4
NS = B * TS
T = TP + NS
HT = T // 2
FF = 2816
NF = FF // 128
H, DK, DV, GK = 4, 128, 128, 64
L = 128
NC = TP // L
MEM = 256
EPS = 1e-6
RANK = 16
LEVELS = 6
TAU = 16.0
Z_GA, Z_GATE, Z_GQ, Z_GK, Z_GV, Z_MQ, Z_MK, Z_MV, Z_MO, Z_GG, NZ = 0, 1, 2, 4, 6, 10, 14, 18, 22, 26, 30
COL_MQ, COL_MI, COL_MF, COL_MO, COL_GQ, COL_GA, COL_GG = 0, 1536, 1540, 1544, 2056, 3080, 3096
C_ID, C_ONE, C_LEVEL, C_CAUSAL = 0, 128, 256, 256 + (LEVELS + 1) * 64
C_RESTART = C_CAUSAL + 128
C_SCAUSAL = C_RESTART + T
C_OWN = C_SCAUSAL + NS
N_CONST = C_OWN + B
G_FFN1, G_MIX, G_XA, G_MEM, G_FFN2, G_FIN, G_ML, G_GLA, G_BA, N_GAIN = 0, 8, 16, 24, 32, 40, 48, 52, 56, 58
KV_RING = 5
LOG_EXP = "natural_log_exp_and_others"
UNIT = 1024
F32, F32R = mybir.dt.float32, mybir.dt.float32r
ALU, ACT, AX = mybir.AluOpType, mybir.ActivationFunctionType, mybir.AxisListType


def build(nc, a, o):
    ctx = ExitStack()
    with ctx:
        sems = {}

        def sem(name):
            if name not in sems:
                sems[name] = ctx.enter_context(nc.semaphore(name))
            return sems[name]

        base = (nc.sbuf_base + 63) // 64 * 64
        AT_X = base
        AT_XN = AT_X + ND * T * 4
        AT_H = AT_XN + 2 * ND * T * 4
        AT_W = AT_H + 2 * NF * T * 4
        AT_MISC = AT_W + 8 * UNIT * 4
        END = AT_MISC + 32000

        def at(name, shape, offset, dt=F32):
            size = 4
            for n in shape[1:]:
                size *= n
            assert offset + size <= END, name
            return nc.alloc_sbuf_tensor_at(name, shape, dt, offset=offset), (offset + size + 31) // 32 * 32

        x, _ = at("x", [128, ND, T], AT_X)
        xn_hi, p = at("xn_hi", [128, ND, T], AT_XN, F32R)
        xn_lo, _ = at("xn_lo", [128, ND, T], p, F32R)
        h_hi, p = at("h_hi", [128, NF, T], AT_H, F32R)
        h_lo, _ = at("h_lo", [128, NF, T], p, F32R)
        raw, w_hi, w_lo = [], [], []
        p = AT_W
        for n in range(4):
            t_, p = at(f"raw{n}", [128, UNIT], p)
            raw.append(t_)
        for n in range(2):
            t_, p = at(f"w_hi{n}", [128, UNIT], p, F32R)
            w_hi.append(t_)
            t_, p = at(f"w_lo{n}", [128, UNIT], p, F32R)
            w_lo.append(t_)
        p = AT_MISC
        const, p = at("const", [128, N_CONST], p)
        sel, p = at("sel", [H, H, 128], p)
        gains, p = at("gains", [128, N_GAIN], p)
        rinv, p = at("rinv", [128, T], p)
        acc, p = at("acc", [128, T], p)
        sq, sig, hf = [], [], []
        AT_SQ = p
        for n in range(2):
            t_, p = at(f"sq{n}", [128, T], p)
            sq.append(t_)
            t_, p = at(f"sig{n}", [128, T], p)
            sig.append(t_)
            t_, p = at(f"hf{n}", [128, T], p)
            hf.append(t_)
        mem_r, p = at("mem_r", [128, 2, 2], p)
        a2w, p = at("a2w", [RANK, H * GK], p)
        gate_b, p = at("gate_b", [64, 1], p)
        m0, p = at("m0", [H, B], p)
        scan_in, p = at("scan_in", [H, 3, B, TS + 1], p)
        s_lv, p = at("s_lv", [128, 2, 2, 2, NS], p)
        p = AT_H
        mem_nat, p = at("mem_nat", [128, 2, D], p)
        xp_nat, p = at("xp_nat", [128, NC, D], p)
        xs_nat, p = at("xs_nat", [NS, D], p)
        gain_rows, p = at("gain_rows", [N_GAIN, 128], p)
        mem_gain, p = at("mem_gain", [ND, 128], p)
        mem_f, p = at("mem_f", [128, ND, MEM], p)
        mem_hi, p = at("mem_hi", [128, ND, MEM], p, F32R)
        mem_lo, p = at("mem_lo", [128, ND, MEM], p, F32R)
        mem_sq, p = at("mem_sq", [128, D], p)
        kv_out = []
        for n in range(2):
            t_, p = at(f"kv_out{n}", [128, 2, 512], p)
            kv_out.append(t_)
        assert p <= AT_W
        z, p = at("z", [128, NZ, T], AT_H)
        rows, p = at("rows", [H, 8, T], p)
        R_U, R_W, R_B, R_M, R_WI, R_EM, R_WL, R_T = range(8)
        decay, p = at("decay", [128, 2, T], p)
        gla_a, p = at("gla_a", [128, NC, H, L], p)
        assert p <= AT_W
        lv_q, lv_k = [], []
        p = AT_H + NZ * T * 4
        for n in range(2):
            t_, p = at(f"lv_q{n}", [128, 2, T], p)
            lv_q.append(t_)
            t_, p = at(f"lv_k{n}", [128, 2, T], p)
            lv_k.append(t_)
        assert p <= AT_H + NZ * T * 4 + 8 * T * 4
        lv_e, p = at("lv_e", [128, 2, T], AT_SQ)
        lv_acc, p = at("lv_acc", [128, NC, H, 64], p)
        lv_tmp, p = at("lv_tmp", [128, NC, H, 64], p)
        assert p <= AT_SQ + 6 * T * 4
        p = AT_XN
        v_tok, p = at("v_tok", [128, H, DV], p)
        kw_tok, p = at("kw_tok", [128, H, DK], p)
        gk_tok, p = at("gk_tok", [128, 2, 128], p)
        gv_tok, p = at("gv_tok", [128, H, DV], p)
        hinv = [at(f"hinv{n}", [128, 2, TP], p + n * 2 * TP * 4)[0] for n in range(2)]
        ew, p = at("ew", [128, H, L], p)
        pw, p = at("pw", [128, H, L], p)
        q_in, p = at("q_in", [128, H, L], p)
        den, p = at("den", [128, H, L], p)
        ucol, p = at("ucol", [128, 2 * H], p)
        il, p = at("il", [128, H], p)
        ring = []
        for n in range(H - 1):
            t_, p = at(f"ring{n}", [128, B, DV], p)
            ring.append(t_)
        ring.append(at(f"ring{H - 1}", [128, B, DV], AT_H)[0])
        s_ta = hf[1][0:NS, 0:12 * NS].rearrange("p (n r k t) -> p n r k t", n=3, r=2, k=2)
        s_a = hf[1][0:NS, 12 * NS:16 * NS].rearrange("p (h t) -> p h t", h=H)
        s_qn, p = at("s_qn", [128, H, NS], p)
        s_n, p = at("s_n", [128, B, H], p)
        s_n2, p = at("s_n2", [128, B, H], p)
        assert p <= AT_XN + 28672, p - AT_XN
        c_st, p = at("c_st", [128, H, DV], AT_XN + 28672)
        n_st, p = at("n_st", [128, H, 128], p)
        s_st, p = at("s_st", [128, H, DV], p)
        assert p <= AT_H
        p = AT_H + NZ * T * 4 + 8 * T * 4 + 2 * T * 4
        v_own = []
        for n in range(2):
            t_, p = at(f"v_own{n}", [2 * NS, B, DV], p)
            v_own.append(t_)
        s_nrow, _ = at("s_nrow", [NS, DK], AT_H + NZ * T * 4 + 8 * T * 4)
        s_nrow2, _ = at("s_nrow2", [NS, DK], AT_H + NZ * T * 4 + 8 * T * 4 + 512)
        p2 = AT_H + NZ * T * 4 + 8 * T * 4 + 1024
        gk_pair, p2 = at("gk_pair", [2 * NS, 2, 128], p2)
        gv_pair, p2 = at("gv_pair", [2 * NS, 2, DV], p2)
        p2 = AT_H + Z_MK * T * 4
        q_pitch, s_pitch = NS + TS, 2 * NS + TS
        q_row, p2 = at("q_row", [128, H, B * q_pitch], p2)
        num_tok, p2 = at("num_tok", [NS, H * DV], p2)
        assert p2 <= AT_H + Z_MV * T * 4
        s_row, p2 = at("s_row", [128, 2, B * s_pitch + NS], AT_H + Z_MV * T * 4)
        o_tok, p2 = at("o_tok", [2 * NS, 2 * DV], p2)
        assert p2 <= AT_H + Z_MO * T * 4
        p = AT_H
        xq, p = at("xq", [128, ND, T], p)
        kv = []
        for n in range(KV_RING):
            t_, p = at(f"kv{n}", [128, 2, D], p)
            kv.append(t_)
        kT = []
        for n in range(2):
            t_, p = at(f"kT{n}", [128, ND, MEM], p)
            kT.append(t_)
        prob, probT = [], []
        for n in range(2):
            t_, p = at(f"prob{n}", [128, H, MEM], p)
            prob.append(t_)
            t_, p = at(f"probT{n}", [128, ND, 128], p)
            probT.append(t_)
        q_pad, _ = at("q_pad", [128, ND, B, 32], AT_SQ)
        p_pad, _ = at("p_pad", [128, 2, H, B, NS], AT_H + (ND * T + KV_RING * 2 * D + 2 * ND * MEM + H * MEM) * 4)
        s_av = probT[1]
        xmx, p = at("xmx", [128, 3 * H], p)
        assert p <= AT_W
        yf, p = at("yf", [128, ND, T], AT_H)
        y_tok, p = at("y_tok", [128, NC + 1, D], p)
        assert p <= AT_W

        ps = ctx.enter_context(nc.psum_tensor("ps", [128, 8, 512], F32))
        gg_sig = [sq[0], sig[0], sq[1], sig[1]]
        S_DECAY = 7
        S_DIFF = [9 + 2 * n for n in range(LEVELS + 1)]
        S_QK = [k + 1 for k in S_DIFF]
        S_SCORES = [9] + [k + 2 for k in S_DIFF]
        S_SUM = S_SCORES[-1] + 1
        S_IN, S_OUT, S_ROWS = S_SUM + 1, S_SUM + 2, S_SUM + 3
        ident = const[:, C_ID:C_ID + 128]
        ones = const[:, C_ONE:C_ONE + 128]
        causal = const[:, C_CAUSAL:C_CAUSAL + 128]
        restart = const[:, C_RESTART:C_RESTART + T]
        s_causal = const[0:NS, C_SCAUSAL:C_SCAUSAL + NS]
        own = const[0:NS, C_OWN:C_OWN + B]
        own_rows = const[0:2 * NS, C_OWN:C_OWN + B]

        def level_mask(n):
            return const[:, C_LEVEL + 64 * n:C_LEVEL + 64 * n + 64]

        def pair(buf):
            q = 2 * (buf % 4)
            return ps[:, q:q + 2, 0:HT]

        def k_banks(n):
            q = (0, 2, 5)[n % 3]
            return ps[:, q:q + 2, :].rearrange("p b (k m) -> p (b k) m", k=2)

        def head(j):
            return z[:, Z_MQ + j, :] if j < H else z[:, Z_GV + j - H, :]

        def heads_of(tile, n):
            return tile[:, H * NS * n:H * NS * (n + 1)].rearrange("p (h t) -> p h t", h=H)

        def halves(t2d):
            return t2d.rearrange("p (h t) -> p h t", h=2)

        U_KV, B_KV = 0, 0
        U_N1 = 10
        B_N1 = 2
        U_UP1, B_UP1 = 16, 5
        U_DN1, B_DN1 = U_UP1 + 2 * NF, B_UP1 + 2 * NF
        B_N2 = B_DN1 + ND
        U_IN, B_IN = U_DN1 + 3 * ND, B_N2 + 1
        U_OUT, B_OUT = U_IN + NZ, B_IN + NZ
        B_N3 = B_OUT + ND
        assert B_IN % 4 == 2
        U_XQ, B_XQ = U_OUT + ND, B_N3 + 1
        U_XO, B_XO = U_XQ + ND, B_XQ + ND
        B_N4 = B_XO + ND
        U_UP2, B_UP2 = U_XO + ND, B_N4 + 1
        U_DN2, B_DN2 = U_UP2 + 2 * NF, B_UP2 + 2 * NF
        B_N5 = B_DN2 + ND
        U_END = U_DN2 + 3 * ND

        def by_row(w):
            return w[0].rearrange("(kt p) c -> p kt c", p=128)

        wk, wv = by_row(a["xattn_w_k"]), by_row(a["xattn_w_v"])
        w_in, w_out = by_row(a["w_in"]), by_row(a["w_out"])
        wq, wo = by_row(a["xattn_w_q"]), by_row(a["xattn_w_o"])
        gate = [by_row(a["ffn1_w_gate"]), by_row(a["ffn2_w_gate"])]
        up = [by_row(a["ffn1_w_up"]), by_row(a["ffn2_w_up"])]
        down = [by_row(a["ffn1_w_down"]), by_row(a["ffn2_w_down"])]
        DN_K = [(0, 8), (8, 15), (15, 22)]
        mem_k_out = o["mem_k"][0, 0].rearrange("(mb p) h d -> p mb (h d)", p=128)
        mem_v_out = o["mem_v"][0, 0].rearrange("(mb p) h d -> p mb (h d)", p=128)

        block = ctx.enter_context(nc.Block())

        @block.sync
        def _(sp):
            raw_ready = [sem(f"raw_ready{n}") for n in range(4)]
            lo_done = sem("lo_done")

            sp.dma_start(const[:, 0:C_LEVEL], a["consts"][:, 0:C_LEVEL]).then_inc(sem("const_in"), 16)
            sp.dma_start(mem_nat[:, :, :], a["mem_prompt"][0].rearrange("(mb p) c -> p mb c", p=128))\
              .then_inc(sem("mem_in"), 16)

            def load(slot, src, free):
                if free is not None:
                    sp.wait_ge(lo_done, free)
                kts, cols = src.shape[1], src.shape[2]
                dst = raw[slot][:, 0:kts * cols].rearrange("p (k c) -> p k c", k=kts)
                sp.dma_start(dst, src).then_inc(raw_ready[slot], 16)

            for u in range(16):
                w, c, kt = (wk, wv)[u // 8], (u // 4) % 2, 2 * (u % 4)
                load(u % 4, w[:, kt:kt + 2, 512 * c:512 * c + 512], u - 3 if u >= 4 else None)
                if u == 3:
                    sp.dma_start(xp_nat[:, :, :], a["x_prompt"][0].rearrange("(c p) d -> p c d", p=128))\
                      .then_inc(sem("x_in"), 16)

            def load_up(n, u0):
                with sp.Fori(0, NF // 2) as i:
                    for k in range(4):
                        w = (gate, up)[k % 2][n]
                        load((u0 + k) % 4, w[:, :, bass.ds(i * 256 + 128 * (k // 2), 128)], i * 4 + (u0 + k - 3))

            def load_down(n, u0):
                with sp.Fori(0, 2) as i:
                    for k in range(12):
                        lo, hi = DN_K[k % 3]
                        load((u0 + k) % 4, down[n][:, lo:hi, bass.ds(i * 512 + 128 * (k // 3), 128)],
                             i * 12 + (u0 + k - 3))

            def load_blocks(w, u0, bodies, col, step=512):
                with sp.Fori(0, bodies) as i:
                    for k in range(4):
                        load((u0 + k) % 4, w[:, :, bass.ds(i * step + (col + 128 * k), 128)], i * 4 + (u0 + k - 3))

            load_up(0, U_UP1)
            load_down(0, U_DN1)
            load(U_IN % 4, w_in[:, :, COL_GA:COL_GA + 128], U_IN - 3)
            sp.wait_ge(lo_done, U_IN + 1 - 3)
            gate_unit = raw[(U_IN + 1) % 4][:, :].rearrange("p (k c) -> p k c", k=8)
            sp.dma_start(gate_unit[:, :, 0:H], w_in[:, :, COL_MI:COL_MI + H]).then_inc(sem("gate_i_in"), 16)
            sp.wait_ge(sem("gate_i_in"), 16)
            sp.dma_start(gate_unit[:, :, 32:32 + H], w_in[:, :, COL_MF:COL_MF + H])\
              .then_inc(raw_ready[(U_IN + 1) % 4], 16)
            load_blocks(w_in, U_IN + Z_GQ, 2, COL_GQ)
            load_blocks(w_in, U_IN + Z_MQ, 3, COL_MQ)
            load_blocks(w_in, U_IN + Z_MO, 2, COL_MO, COL_GG - COL_MO)
            load_blocks(w_out, U_OUT, 2, 0)
            load_blocks(wq, U_XQ, 2, 0)
            load_blocks(wo, U_XO, 2, 0)
            load_up(1, U_UP2)
            load_down(1, U_DN2)

        @block.gpsimd
        def _(pool):
            steps = [0]

            def link(ins):
                steps[0] += 1
                ins.then_inc(sem("pool_chain"), 1)
                pool.wait_ge(sem("pool_chain"), steps[0])

            pool.dma_start(xs_nat[:, :], a["x_sample"].rearrange("b t d -> (b t) d")).then_inc(sem("xs_in"), 16)
            pool.dma_start(const[:, C_LEVEL:], a["consts"][:, C_LEVEL:]).then_inc(sem("small_in"), 16)
            pool.dma_start(sel[:, :, :], a["sel"].rearrange("h (k p) -> h k p", k=H)).then_inc(sem("small_in"), 16)
            pool.dma_start(a2w[:, :], a["gla_w_a2"][0]).then_inc(sem("small_in"), 16)
            pool.dma_start(gate_b[0:H, :], a["mlstm_b_i"].rearrange("a h -> h a")).then_inc(sem("small_in"), 16)
            pool.dma_start(gate_b[32:32 + H, :], a["mlstm_b_f"].rearrange("a h -> h a")).then_inc(sem("small_in"), 16)
            pool.dma_start(m0[:, :], a["state_mlstm_m"][0].rearrange("b h -> h b"),
                           allow_slow_non_contiguous=True).then_inc(sem("small_in"), 16)

            for n in range(4):
                pool.wait_ge(sem("evac"), (1, 2, 4, 5)[n])
                dst = (mem_k_out, mem_v_out)[n // 2][:, :, 512 * (n % 2):512 * (n % 2) + 512]
                pool.dma_start(dst, kv_out[n % 2][:, :, :]).then_inc(sem(f"kv_stored{n % 2}"), 16)

            pool.wait_ge(sem("evac"), B_IN)
            pool.memset(gla_a[64:128, :, :, 0:64], 0.0).then_inc(sem("zeros_set"), 1)
            pool.wait_ge(sem("zeros_set"), 1)
            for n in range(1, LEVELS):
                pool.wait_ge(sem("lv_masked"), n + 1)
                pool.tensor_tensor(lv_acc[:, :, :, :], lv_acc[:, :, :, :], lv_tmp[:, :, :, :], ALU.add)\
                    .then_inc(sem("lv_added"), 1)

            c_in = a["state_mlstm_c"][0].rearrange("b h k v -> h k b v")
            s_in = a["state_gla_s"][0].rearrange("b (p r) k v -> p (r k) b v", r=2)
            c_out = o["mlstm_c_s"][0].rearrange("b h k v -> h k b v")
            s_out = o["gla_s_s"][0].rearrange("b (p r) k v -> p (r k) b v", r=2)

            def load_state(n):
                src = c_in[n] if n < H else s_in[n - H]
                pool.dma_start(ring[n % H][:, :, :], src).then_inc(sem(f"state_in{n % H}"), 16)

            pool.wait_ge(sem("pe_unit"), U_IN + NZ)
            pool.memset(s_st[:, :, :], 0.0).then_inc(sem("zeros_set"), 1)
            pool.wait_ge(sem("zeros_set"), 2)
            pool.wait_ge(sem("levels_done"), 1)
            pool.dma_start(s_nrow[:, :], a["state_mlstm_n"][0].rearrange("b h k -> (b h) k"))\
                .then_inc(sem("n_in"), 16)
            pool.wait_ge(sem("rows_made"), 1)
            for n in range(H):
                load_state(n)

            for c in range(NC + 1):
                pool.wait_ge(sem("w_exp"), c + 1)
                if c < NC:
                    pool.tensor_tensor(ew[:, :, :], ew[:, :, :], causal.unsqueeze(1).broadcast_to([128, H, L]),
                                       ALU.mult).then_inc(sem("w_masked"), 1)
                else:
                    pool.tensor_tensor(ew[0:NS, :, 0:NS], ew[0:NS, :, 0:NS],
                                       s_causal.unsqueeze(1).broadcast_to([NS, H, NS]), ALU.mult)\
                        .then_inc(sem("w_masked"), 1)

            pool.wait_ge(sem("kw_done"), NC + 1)
            pool.memset(q_row[:, :, :], 0.0).then_inc(sem("row_zeros"), 1)
            pool.wait_ge(sem("tok_done"), 3 * NC + 3)
            pool.memset(s_row[:, :, :], 0.0).then_inc(sem("row_zeros"), 1)

            pool.wait_ge(sem("chunk_done"), NC)
            pool.wait_ge(sem("gla_out"), NC)
            pool.dma_start(o["mlstm_c_p"][0, 0].rearrange("h k v -> k h v"), c_st[:, :, :]).then_inc(sem("st_out"), 16)
            pool.dma_start(o["mlstm_n_p"][0, 0].rearrange("h k -> k h"), n_st[:, :, 0],
                           allow_slow_non_contiguous=True).then_inc(sem("st_out"), 16)
            pool.dma_start(o["mlstm_m_p"][0, 0].rearrange("(h a) -> h a", a=1), rows[:, R_M, TP - 1:TP])\
                .then_inc(sem("st_out"), 16)
            for h in range(H):
                r = 64 * (h % 2)
                pool.dma_start(o["gla_s_p"][0, 0, h], s_st[r:r + 64, h, :]).then_inc(sem("st_out"), 16)
            pool.dma_start(o["mlstm_m_s"][0].rearrange("b h -> h b"),
                           rows[:, R_M, TP + TS - 1:T:TS], allow_slow_non_contiguous=True)\
                .then_inc(sem("st_out"), 16)
            for n in range(H + 2):
                pool.wait_ge(sem("upd_free"), n + 1)
                dst = c_out[n] if n < H else s_out[n - H]
                pool.dma_start(dst, ring[n % H][:, :, :]).then_inc(sem(f"state_out{n % H}"), 16)
                if n + H < H + 2:
                    pool.wait_ge(sem(f"state_out{n % H}"), 16)
                    load_state(n + H)
            pool.wait_ge(sem("n_new"), 1)
            pool.dma_start(o["mlstm_n_s"][0].rearrange("b h k -> (b h) k"), s_nrow2[:, :]).then_inc(sem("st_out"), 16)
            pool.wait_ge(sem("st_out"), 16 * 9)
            for n in range(H):
                pool.wait_ge(sem(f"state_out{n}"), 32 if n < 2 else 16)
            pool.sem_inc(sem("mixer_stored"), 1)

            for n in range(18):
                if n == 0:
                    pool.wait_ge(sem("ym_lo"), 8)
                    pool.wait_ge(sem("kv_stored0"), 32)
                    pool.wait_ge(sem("kv_stored1"), 32)
                if n >= KV_RING:
                    was = n - KV_RING
                    name, value = (("av_mm", NC) if was == 1 else ("kT_mm", 1 + 2 * max(was - 1, 0)) if was < 10
                                   else ("sav_mm", was - 9))
                    pool.wait_ge(sem(name), value)
                if n < 2:
                    src = (mem_k_out, mem_v_out)[n]
                else:
                    src = (a["cache_mem_k"], a["cache_mem_v"])[n // 10][0, (n - 2) % 8]\
                        .rearrange("(mb p) h d -> p mb (h d)", p=128)
                pool.dma_start(kv[n % KV_RING][:, :, :], src).then_inc(sem(f"kv_in{n % KV_RING}"), 16)

            for c in range(NC):
                pool.wait_ge(sem("y_copied"), c + 1)
                pool.dma_start(o["y_prompt"][0, c * L:(c + 1) * L, :], y_tok[:, c, :]).then_inc(sem("y_out"), 16)
            pool.wait_ge(sem("y_copied"), NC + 1)
            pool.dma_start(o["y_sample"].rearrange("b t d -> (b t) d"), y_tok[0:NS, NC, :]).then_inc(sem("y_out"), 16)
            pool.wait_ge(sem("y_out"), 16 * (NC + 1))

        @block.scalar
        def _(act):
            raw_ready = [sem(f"raw_ready{n}") for n in range(4)]
            pe_unit, evac = sem("pe_unit"), sem("evac")
            steps = [0]

            def link(ins):
                steps[0] += 1
                ins.then_inc(sem("act_chain"), 1)
                act.wait_ge(sem("act_chain"), steps[0])

            def split(u0, i=0, per=0):
                act.wait_ge(raw_ready[u0 % 4], 16 * (u0 // 4 + 1) + i * (4 * per))
                if u0 >= 2:
                    act.wait_ge(pe_unit, i * per + (u0 - 1))
                act.activation(w_hi[u0 % 2][:, :], raw[u0 % 4][:, :], ACT.Copy).then_inc(sem("hi_done"), 1)

            def square(r, src, ready, value, i=0, per=0):
                act.wait_ge(ready, value)
                if r >= 2:
                    act.wait_ge(sem("acc_done"), i * per + (r - 1))
                act.activation(sq[r % 2][:, :], src, ACT.Square).then_inc(sem("sq_done"), 1)

            def norm_inverse(g, buf):
                act.preload_act_table_set(LOG_EXP)
                act.wait_ge(sem("norm_mm"), g + 1)
                act.activation(halves(sig[0][:, :]), pair(buf), ACT.Ln, bias=EPS, scale=1.0 / D).then_inc(evac, 1)
                act.wait_ge(evac, buf + 1)
                act.activation(rinv[:, :], sig[0][:, :], ACT.Exp, scale=-0.5).then_inc(sem("norm_inv"), 1)

            def norm_hi(g, d):
                act.wait_ge(sem("xf_done"), 8 * g + d + 1)
                act.activation(xn_hi[:, d, :], hf[d % 2][:, :], ACT.Copy).then_inc(sem("xnh_done"), 1)

            def norm(g, buf):
                norm_inverse(g, buf)
                for d in range(ND):
                    norm_hi(g, d)

            act.dma_start(mem_gain[:, :], a["mem_norm_g"][0].rearrange("(n p) -> n p", p=128))\
               .then_inc(sem("mem_gain_in"), 16)
            rows_of = [("ffn1_norm_g", G_FFN1, 8), ("mix_norm_g", G_MIX, 8), ("xattn_norm_g", G_XA, 8),
                       ("ffn2_norm_g", G_FFN2, 8), ("final_norm_g", G_FIN, 8),
                       ("mem_norm_g", G_MEM, 8), ("mlstm_out_g", G_ML, 4), ("gla_out_g", G_GLA, 4), ("gla_b_a", G_BA, 2)]
            for name, g, n in rows_of:
                src = a[name] if name == "final_norm_g" else a[name][0]
                act.dma_start(gain_rows[g:g + n, :], src.rearrange("(n p) -> n p", p=128))\
                    .then_inc(sem("gains_in"), 16)
            act.preload_act_table_set(LOG_EXP)
            for n in range(2):
                act.wait_ge(sem("mem_f_done"), 4 * n + 4)
                act.activation(mem_hi[:, 4 * n:4 * n + 4, :], mem_f[:, 4 * n:4 * n + 4, :], ACT.Copy)\
                   .then_inc(sem("mem_hi_done"), 1)
                split(n)
            act.wait_ge(sem("mem_in"), 16)
            for mb in range(2):
                link(act.activation(mem_sq[:, :], mem_nat[:, mb, :], ACT.Square, accum_out=mem_r[:, 0, mb:mb + 1]))
            link(act.activation(mem_r[:, 1, :], mem_r[:, 0, :], ACT.Ln, bias=EPS, scale=1.0 / D))
            link(act.activation(mem_r[:, 0, :], mem_r[:, 1, :], ACT.Exp, scale=-0.5))
            def kv_evac(n, buf, last_unit):
                act.wait_ge(pe_unit, last_unit + 1)
                if n >= 2:
                    act.wait_ge(sem(f"kv_stored{n % 2}"), 16)
                act.activation(kv_out[n % 2][:, 0, :], ps[:, 2 * (buf % 4), :], ACT.Copy, scale=mem_r[:, 0, 0:1])
                act.activation(kv_out[n % 2][:, 1, :], ps[:, 2 * (buf % 4) + 1, :], ACT.Copy,
                               scale=mem_r[:, 0, 1:2]).then_inc(evac, 1)

            for u in range(16):
                if u == 3:
                    kv_evac(0, 0, 3)
                if u == 7:
                    kv_evac(1, 1, 7)
                if u == U_N1:
                    norm_inverse(0, B_N1)
                if u == 11:
                    kv_evac(2, 0, 11)
                if u == 15:
                    kv_evac(3, 1, 15)
                split(u + 2)
                if 1 <= u <= ND:
                    square(u - 1, x[:, u - 1, :], sem("x_made"), u)
                if u >= U_N1:
                    norm_hi(0, u - U_N1)
            for d in range(16 - U_N1, ND):
                norm_hi(0, d)

            def ffn_up(n, u0, b0):
                act.preload_act_table(ACT.Sigmoid)
                with act.Fori(0, NF // 2) as i:
                    for k in range(4):
                        j = k // 2
                        if k % 2 == 0:
                            act.wait_ge(pe_unit, i * 4 + (u0 + k + 1))
                            act.wait_ge(evac, i * 4 + (b0 + k - 2))
                            act.activation(halves(sig[j][:, :]), pair(b0 + k), ACT.Sigmoid)\
                               .then_inc(sem("sig_done"), 1)
                            split(u0 + k + 2, i, 4)
                        else:
                            split(u0 + k + 2, i, 4)
                            act.wait_ge(evac, i * 4 + (b0 + k + 1))
                            act.activation(h_hi[:, bass.ds(i * 2 + j, 1), :].rearrange("p a t -> p (a t)"),
                                           hf[j][:, :], ACT.Copy).then_inc(sem("hh_done"), 1)

            def ffn_down(u0, b0, r0, last):
                def body(i, splits):
                    for k in range(12):
                        if k % 3 == 2:
                            d = k // 3
                            square(r0 + d, x[:, bass.ds(i * 4 + d, 1), :].rearrange("p a t -> p (a t)"), evac,
                                   i * 4 + (b0 + d + 1), i, 4)
                        if k < splits:
                            split(u0 + k + 2, i, 12)
                if last:
                    body(0, 12)
                    for k in range(12):
                        if k % 3 == 2:
                            d = k // 3
                            square(r0 + 4 + d, x[:, 4 + d, :], evac, b0 + 4 + d + 1)
                        if k < 10:
                            split(u0 + 12 + k + 2)
                else:
                    with act.Fori(0, 2) as i:
                        body(i, 12)

            def residual(u0, b0, r0):
                with act.Fori(0, 2) as i:
                    for k in range(4):
                        square(r0 + k, x[:, bass.ds(i * 4 + k, 1), :].rearrange("p a t -> p (a t)"), evac,
                               i * 4 + (b0 + k + 1), i, 4)
                        split(u0 + k + 2, i, 4)

            act.wait_ge(sem("kv_stored0"), 32)
            act.wait_ge(sem("kv_stored1"), 32)
            ffn_up(0, U_UP1, B_UP1)
            ffn_down(U_DN1, B_DN1, 8, False)
            norm(1, B_N2)
            act.preload_act_table_set(LOG_EXP)

            def level_exp(n):
                act.wait_ge(sem("lv_diff"), n)
                link(act.activation(lv_e[:, :, :], lv_e[:, :, :], ACT.Abs))
                act.activation(lv_e[:, :, :], lv_e[:, :, :], ACT.Exp, scale=-1.0 / TAU).then_inc(sem("lv_exp"), 1)

            for k in range(NZ):
                split(U_IN + k + 2)
                if k == S_DECAY:
                    act.wait_ge(sem("y_decay"), 1)
                    link(act.activation(lv_e[:, :, :], decay[:, :, :], ACT.Abs))
                    link(act.activation(lv_e[:, :, :], lv_e[:, :, :], ACT.Exp, scale=-1.0))
                    act.activation(lv_e[:, :, :], lv_e[:, :, :], ACT.Ln, bias=1.0).then_inc(sem("log_decay"), 1)
                if k in S_DIFF:
                    level_exp(S_DIFF.index(k) + 1)
                if k == S_SUM:
                    act.wait_ge(sem("lv_qk"), LEVELS + 1)
                    act.activation(lv_e[:, :, :], decay[:, :, :], ACT.Exp, scale=1.0 / TAU).then_inc(sem("in_exp"), 1)
                if k == S_IN:
                    act.wait_ge(sem("in_diff"), 1)
                    act.activation(lv_e[:, :, :], lv_e[:, :, :], ACT.Exp, scale=1.0 / TAU).then_inc(sem("in_exp"), 1)
                if k == S_IN:
                    act.wait_ge(sem("y_rows"), 1)
                    link(act.activation(rows[:, R_T, :], rows[:, R_W, :], ACT.Abs))
                    link(act.activation(rows[:, R_T, :], rows[:, R_T, :], ACT.Exp, scale=-1.0))
                    act.activation(rows[:, R_T, :], rows[:, R_T, :], ACT.Ln, bias=1.0).then_inc(sem("log_rows"), 1)
                if k == S_ROWS:
                    act.wait_ge(sem("rows_made"), 1)
                    for dst, src, scale in ((R_WI, R_WI, 1.0), (R_EM, R_M, -1.0), (R_WL, R_WL, 1.0)):
                        act.activation(rows[:, dst, :], rows[:, src, :], ACT.Exp, scale=scale)\
                           .then_inc(sem("rows_exp"), 1)
            act.wait_ge(evac, B_IN + NZ)
            act.activation(z[:, Z_MO:Z_MO + 4, :], z[:, Z_MO:Z_MO + 4, :], ACT.Sigmoid)
            act.wait_ge(sem("levels_done"), 1)
            for j in range(4):
                act.activation(gg_sig[j][:, :], z[:, Z_GG + j, :], ACT.Sigmoid).then_inc(sem("gg_sig"), 1)

            act.preload_act_table_set(LOG_EXP)

            def chunk(c, n):
                act.wait_ge(sem("w_arg"), c + 1)
                act.activation(ew[0:n, :, 0:n], ew[0:n, :, 0:n], ACT.Exp).then_inc(sem("w_exp"), 1)
                act.wait_ge(sem("pe_a"), 9 * c + 7)
                act.activation(v_tok[0:n, :, :], ps[0:n, 5, :].rearrange("p (h v) -> p h v", h=H), ACT.Copy)\
                   .then_inc(sem("tok_done"), 1)
                act.wait_ge(sem("pe_a"), 9 * c + 8)
                act.activation(gk_tok[0:n, :, :], ps[0:n, 6, 0:256].rearrange("p (h v) -> p h v", h=2), ACT.Copy)\
                   .then_inc(sem("tok_done"), 1)
                act.wait_ge(sem("pe_a"), 9 * c + 9)
                act.activation(gv_tok[0:n, :, :], ps[0:n, 7, :].rearrange("p (h v) -> p h v", h=H), ACT.Copy)\
                   .then_inc(sem("tok_done"), 1)
                if c == NC:
                    act.wait_ge(sem("pair_zero"), 1)
                    for r in range(2):
                        act.activation(gk_pair[32 * r:32 * r + 32, :, 64 * r:64 * r + 64],
                                       ps[32 * r:32 * r + 32, 6, 0:256].rearrange("p (k f) -> p k f", k=2)
                                       [:, :, 64 * r:64 * r + 64], ACT.Copy)
                    act.activation(gv_pair[0:n, :, :], ps[0:n, 7, :].rearrange("p (k r v) -> p k r v", k=2, r=2)
                                   [:, :, 0, :], ACT.Copy)
                    act.activation(gv_pair[n:2 * n, :, :], ps[n:2 * n, 7, 0:256].rearrange("p (k v) -> p k v", k=2),
                                   ACT.Copy).then_inc(sem("pair_made"), 1)
                act.wait_ge(sem("den_mm"), c + 1)
                act.activation(den[:, :, 0:n], ps[:, 3, 0:H * n].rearrange("p (h t) -> p h t", h=H), ACT.Abs)\
                   .then_inc(sem("den_abs"), 1)
                if c == NC:
                    act.wait_ge(sem("num_s"), H)
                    act.activation(num_tok[:, :], ps[0:NS, 0, :], ACT.Copy).then_inc(sem("num_copied"), 1)
                    return
                act.wait_ge(sem("gla_mm"), c + 1)
                act.activation(z[:, Z_GV:Z_GV + H, c * L:c * L + n],
                               ps[:, 7, 0:H * n].rearrange("p (h t) -> p h t", h=H), ACT.Copy)\
                   .then_inc(sem("gla_out"), 1)

            for c in range(NC):
                chunk(c, L)
            chunk(NC, NS)

            act.wait_ge(sem("heads_done"), NC + 1)

            def head_squares(n):
                for j in (2 * n, 2 * n + 1):
                    if n:
                        act.wait_ge(sem("hn_mm"), j - 1)
                    act.activation(sq[j % 2][:, 0:TP], head(j)[:, 0:TP], ACT.Square).then_inc(sem("hn_sq"), 1)

            def head_inverse(n, mms, src, dst):
                act.wait_ge(sem("hn_mm"), mms)
                act.activation(dst, src, ACT.Ln, bias=EPS, scale=1.0 / DV).then_inc(sem("hn_root"), 1)
                act.wait_ge(sem("hn_root"), n + 1)
                act.activation(dst, dst, ACT.Exp, scale=-0.5).then_inc(sem("hn_inv"), 1)

            head_squares(0)
            for n in range(H):
                if n + 1 < H:
                    head_squares(n + 1)
                if n >= 2:
                    act.wait_ge(sem("hn_y"), 2 * n - 2)
                head_inverse(n, 2 * n + 2, ps[:, 2:4, :], hinv[n % 2][:, :, :])
            act.wait_ge(sem("o_s"), 2)
            act.activation(o_tok[:, :], ps[0:2 * NS, 1, 0:2 * DV], ACT.Copy).then_inc(sem("o_copied"), 1)
            act.wait_ge(sem("o_back"), 1)
            link(act.activation(z[:, Z_GV:Z_GV + H, TP:T], ps[:, 1, 0:H * NS].rearrange("p (h t) -> p h t", h=H),
                                ACT.Copy))
            for n, zb in enumerate((Z_MQ, Z_GV)):
                ins = act.activation(heads_of(sq[0], n), z[:, zb:zb + H, TP:T], ACT.Square)
            ins.then_inc(sem("hn_sq"), 1)
            act.wait_ge(sem("hn_y"), 2 * H)
            head_inverse(H, 2 * H + 1, ps[:, 2, 0:2 * H * NS], sig[0][:, 0:2 * H * NS])
            act.wait_ge(sem("mixer_stored"), 1)
            act.wait_ge(sem("hn_y"), 2 * H + 1)
            for j in range(2 * H):
                act.activation(xn_hi[:, j, :], head(j), ACT.Copy).then_inc(sem("ym_hi"), 1)
            residual(U_OUT, B_OUT, 16)
            norm(2, B_N3)
            with act.Fori(0, 2) as i:
                for k in range(4):
                    split(U_XQ + k + 2, i, 4)

            def exp_rows(n_mx, heads, scores, dst):
                for h in range(heads):
                    ins = act.activation(dst(h), scores(h), ACT.Exp, bias=xmx[:, h:h + 1], scale=1.0 / 16,
                                         accum_out=xmx[:, 4 + h:5 + h])
                ins.then_inc(sem("x_exp"), 1)

            act.wait_ge(sem("kT_mm"), 1)
            act.activation(kT[0][:, 0:4, :], ps[:, 0:2, :].rearrange("p b (k m) -> p (b k) m", k=2), ACT.Copy)\
               .then_inc(sem("kT_act"), 1)

            def prompt_exp(tb):
                act.wait_ge(sem("x_max"), tb + 1)
                if tb >= 2:
                    act.wait_ge(sem("pT_mm"), tb - 1)
                sc = ps[:, 4 * (tb % 2):4 * (tb % 2) + 2, :].rearrange("p b (k m) -> p (b k) m", k=2)
                exp_rows(tb, H, lambda h: sc[:, h, :], lambda h: prob[tb % 2][:, h, :])

            prompt_exp(0)
            for tb in range(NC):
                if tb + 1 < NC:
                    prompt_exp(tb + 1)
                act.wait_ge(sem("av_mm"), tb + 1)
                q = 4 * (tb % 2)
                act.activation(xn_hi[:, :, tb * 128:tb * 128 + 128],
                               ps[:, q:q + 2, :].rearrange("p b (k t) -> p (b k) t", k=4), ACT.Copy)\
                   .then_inc(sem("av_hi"), 1)
            for b in range(B):
                act.wait_ge(sem("kT_mm"), 2 * b + 2)
                if b >= 2:
                    act.wait_ge(sem("ssc_mm"), b - 1)
                act.activation(kT[(b + 1) % 2][:, 0:4, :], k_banks(2 * b), ACT.Copy).then_inc(sem("kT_act"), 1)
            act.wait_ge(sem("x_max"), NC + 1)
            exp_rows(NC, 1, lambda h: ps[:, 4, 0:MEM], lambda h: prob[0][:, 0, :])
            act.wait_ge(sem("savT_mm"), 1)
            act.activation(xn_hi[:, :, TP:T], ps[:, 5, 0:ND * NS].rearrange("p (k t) -> p k t", k=ND), ACT.Copy)\
               .then_inc(sem("av_hi"), 1)

            residual(U_XO, B_XO, 24)
            norm(3, B_N4)
            ffn_up(1, U_UP2, B_UP2)
            ffn_down(U_DN2, B_DN2, 32, True)
            norm_inverse(4, B_N5)
            for c in range(NC + 1):
                n = L if c < NC else NS
                act.wait_ge(sem("yT_mm"), c + 1)
                q = 2 * (c % 4)
                act.activation(y_tok[0:n, c, :].rearrange("p (b f) -> p b f", b=2), ps[0:n, q:q + 2, :], ACT.Copy)\
                   .then_inc(sem("y_copied"), 1)

        @block.vector
        def _(dve):
            pe_unit, evac = sem("pe_unit"), sem("evac")
            steps = [0]

            def link(ins):
                steps[0] += 1
                ins.then_inc(sem("dve_chain"), 1)
                dve.wait_ge(sem("dve_chain"), steps[0])

            def split(u0, i=0, per=0):
                dve.wait_ge(sem("hi_done"), i * per + (u0 + 1))
                dve.tensor_tensor(w_lo[u0 % 2][:, :], raw[u0 % 4][:, :], w_hi[u0 % 2][:, :].bitcast(F32),
                                  ALU.subtract).then_inc(sem("lo_done"), 1)

            def add_square(r, i=0, per=0):
                dve.wait_ge(sem("sq_done"), i * per + (r + 1))
                if r:
                    dve.wait_ge(sem("acc_done"), i * per + r)
                dve.tensor_tensor(acc[:, :], acc[:, :], sq[r % 2][:, :], ALU.add).then_inc(sem("acc_done"), 1)


            def norm_scale(g, gain, d):
                if d == 0:
                    dve.wait_ge(sem("norm_inv"), g + 1)
                if d == 2:
                    dve.memset(acc[:, :], 0.0)
                if d < ND:
                    if d >= 2:
                        dve.wait_ge(sem("xnl_done"), 8 * g + d - 1)
                    dve.scalar_tensor_tensor(out=hf[d % 2][:, :], in0=x[:, d, :],
                                             scalar=gains[:, gain + d:gain + d + 1], in1=rinv[:, :], op0=ALU.mult,
                                             op1=ALU.mult).then_inc(sem("xf_done"), 1)
                if d >= 1:
                    dve.wait_ge(sem("xnh_done"), 8 * g + d)
                    dve.tensor_tensor(xn_lo[:, d - 1, :], hf[(d - 1) % 2][:, :], xn_hi[:, d - 1, :].bitcast(F32),
                                      ALU.subtract).then_inc(sem("xnl_done"), 1)

            def norm(g, gain):
                for d in range(ND + 1):
                    norm_scale(g, gain, d)

            link(dve.memset(acc[:, :], 0.0))
            dve.wait_ge(sem("gain_mm"), 1)
            link(dve.tensor_copy(gains[:, G_MEM:G_MEM + 8], ps[:, 7, 0:8]))
            for d in range(ND):
                dve.wait_ge(sem("memT_mm"), 2 * (d // 2) + 2)
                dve.tensor_scalar(mem_f[:, d, :], ps[:, d // 2, MEM * (d % 2):MEM * (d % 2) + MEM],
                                  gains[:, G_MEM + d:G_MEM + d + 1], None, ALU.mult).then_inc(sem("mem_f_done"), 1)
            for n in range(2):
                dve.wait_ge(sem("mem_hi_done"), n + 1)
                dve.tensor_tensor(mem_lo[:, 4 * n:4 * n + 4, :], mem_f[:, 4 * n:4 * n + 4, :],
                                  mem_hi[:, 4 * n:4 * n + 4, :].bitcast(F32), ALU.subtract)\
                   .then_inc(sem("mem_lo_done"), 1)
                split(n)
            for u in range(16):
                split(u + 2)
                if u < ND:
                    q = 4 + 2 * (u % 2)
                    dve.wait_ge(sem("xT_mm"), u + 1)
                    dve.tensor_copy(x[:, u, 0:TP], ps[:, q, :])
                    dve.tensor_copy(x[:, u, TP:T], ps[:, q + 1, 0:NS]).then_inc(sem("x_made"), 1)
                    if u >= 1:
                        add_square(u - 1)
                if u == ND:
                    add_square(u - 1)
                    dve.wait_ge(sem("gain_mm"), 2)
                    dve.tensor_copy(gains[:, :], ps[:, 5, 256:256 + N_GAIN]).then_inc(sem("gains_made"), 1)
                    dve.wait_ge(sem("gains_made"), 1)
                if u >= U_N1:
                    norm_scale(0, G_FFN1, u - U_N1)
            for d in range(16 - U_N1, ND + 1):
                norm_scale(0, G_FFN1, d)

            def ffn_up(n, u0, b0):
                p0 = NF * n
                with dve.Fori(0, NF // 2) as i:
                    for k in range(4):
                        j = k // 2
                        if k % 2 == 0:
                            dve.wait_ge(sem("sig_done"), i * 2 + (p0 + j + 1))
                            dve.tensor_tensor(halves(sig[j][:, :]), pair(b0 + k), halves(sig[j][:, :]), ALU.mult)\
                               .then_inc(evac, 1)
                            split(u0 + k + 2, i, 4)
                        else:
                            dve.wait_ge(pe_unit, i * 4 + (u0 + k + 1))
                            dve.wait_ge(evac, i * 4 + (b0 + k))
                            dve.tensor_tensor(halves(hf[j][:, :]), pair(b0 + k), halves(sig[j][:, :]), ALU.mult)\
                               .then_inc(evac, 1)
                            split(u0 + k + 2, i, 4)
                            dve.wait_ge(sem("hh_done"), i * 2 + (p0 + j + 1))
                            fb = bass.ds(i * 2 + j, 1)
                            dve.tensor_tensor(h_lo[:, fb, :].rearrange("p a t -> p (a t)"), hf[j][:, :],
                                              h_hi[:, fb, :].bitcast(F32).rearrange("p a t -> p (a t)"),
                                              ALU.subtract).then_inc(sem("hl_done"), 1)

            def add_block(d, buf, scale):
                dve.scalar_tensor_tensor(out=halves(x[:, d, :].rearrange("p a t -> p (a t)")), in0=pair(buf),
                                         scalar=scale, in1=halves(x[:, d, :].rearrange("p a t -> p (a t)")),
                                         op0=ALU.mult, op1=ALU.add).then_inc(evac, 1)

            def ffn_down(u0, b0, r0, last):
                def body(i, i0, splits):
                    for k in range(12):
                        if k % 3 == 2:
                            d = k // 3
                            dve.wait_ge(pe_unit, i * 12 + (u0 + 12 * i0 + k + 1))
                            at_d = bass.ds(i * 4 + (4 * i0 + d), 1) if not i0 else slice(4 * i0 + d, 4 * i0 + d + 1)
                            add_block(at_d, b0 + 4 * i0 + d, 0.5)
                            add_square(r0 + 4 * i0 + d, i, 4)
                        if k < splits:
                            split(u0 + 12 * i0 + k + 2, i, 12)
                if last:
                    body(0, 0, 12)
                    body(0, 1, 10)
                else:
                    with dve.Fori(0, 2) as i:
                        body(i, 0, 12)

            def residual(u0, b0, r0):
                with dve.Fori(0, 2) as i:
                    for k in range(4):
                        dve.wait_ge(pe_unit, i * 4 + (u0 + k + 1))
                        add_block(bass.ds(i * 4 + k, 1), b0 + k, 1.0)
                        add_square(r0 + k, i, 4)
                        split(u0 + k + 2, i, 4)

            dve.wait_ge(sem("kv_stored0"), 32)
            dve.wait_ge(sem("kv_stored1"), 32)
            ffn_up(0, U_UP1, B_UP1)
            ffn_down(U_DN1, B_DN1, 8, False)
            norm(1, G_MIX)

            def row(r, lo=0, hi=T):
                return rows[:, r, lo:hi]

            def by_chunk(r):
                return rows[:, r, 0:TP].rearrange("p (c t) -> p c t", c=NC)

            def by_seq(r):
                return rows[:, r, TP:T].rearrange("p (b t) -> p b t", b=B)

            def make_decay():
                dve.wait_ge(sem("log_decay"), 1)
                link(dve.scalar_tensor_tensor(out=lv_e[:, :, :], in0=decay[:, :, :], scalar=0.0, in1=lv_e[:, :, :],
                                              op0=ALU.min, op1=ALU.subtract))
                for n in range(2):
                    ins = dve.tensor_tensor_scan(decay[:, n, :], restart, lv_e[:, n, :], 0.0, ALU.mult, ALU.add)
                link(ins)

            def level_diff(n):
                half = 1 << (n - 1)
                if n >= 2:
                    dve.wait_ge(sem("lv_qk"), n - 1)
                if half <= 16:
                    dst = lv_e[:, :, :].rearrange("p f t -> p (f t)").rearrange("p (b t) -> p b t", t=2 * half)
                    src = decay[:, :, :].rearrange("p f t -> p (f t)").rearrange("p (b t) -> p b t", t=2 * half)
                    dve.tensor_tensor(dst, src, src[:, :, half - 1:half].broadcast_to(list(src.shape)),
                                      ALU.subtract).then_inc(sem("lv_diff"), 1)
                else:
                    dst = lv_e[:, :, 0:TP].rearrange("p f (b t) -> p f b t", t=2 * half)
                    src = decay[:, :, 0:TP].rearrange("p f (b t) -> p f b t", t=2 * half)
                    dve.tensor_tensor(dst, src, src[:, :, :, half - 1:half].broadcast_to(list(src.shape)),
                                      ALU.subtract).then_inc(sem("lv_diff"), 1)

            def level_qk(n):
                if n >= 3:
                    dve.wait_ge(sem("lv_mm"), n - 1)
                dve.wait_ge(sem("lv_exp"), n)
                if n <= 2:
                    dve.tensor_tensor(s_lv[:, n - 1, 0, :, :], z[:, Z_GQ:Z_GQ + 2, TP:T], lv_e[:, :, TP:T], ALU.mult)
                    dve.tensor_tensor(s_lv[:, n - 1, 1, :, :], z[:, Z_GK:Z_GK + 2, TP:T], lv_e[:, :, TP:T], ALU.mult)
                dve.tensor_tensor(lv_q[n % 2][:, :, 0:TP], z[:, Z_GQ:Z_GQ + 2, 0:TP], lv_e[:, :, 0:TP], ALU.mult)
                dve.tensor_tensor(lv_k[n % 2][:, :, 0:TP], z[:, Z_GK:Z_GK + 2, 0:TP], lv_e[:, :, 0:TP], ALU.mult)\
                   .then_inc(sem("lv_qk"), 1)

            def level_masked(m):
                dve.wait_ge(sem("lv_mm"), m + 1)
                if m >= 2:
                    dve.wait_ge(sem("lv_added"), m - 1)
                for r in range(2):
                    dst = (lv_acc if m == 0 else lv_tmp)[:, :, r::2, :]
                    src = ps[:, 4 + 2 * (m % 2) + r, :].rearrange("p (c k t) -> p c k t", c=NC, k=2)
                    mask = level_mask(m).unsqueeze(1).unsqueeze(1).broadcast_to([128, NC, 2, 64])
                    ins = dve.tensor_tensor(dst, src, mask, ALU.mult)
                ins.then_inc(sem("lv_masked"), 1)

            def level_sum():
                dve.wait_ge(sem("lv_added"), LEVELS - 1)
                dve.wait_ge(sem("lv_masked"), LEVELS + 1)
                dve.wait_ge(sem("zeros_set"), 1)
                for lo in (0, 64):
                    dve.tensor_tensor(gla_a[lo:lo + 64, :, :, lo:lo + 64], lv_acc[lo:lo + 64, :, :, :],
                                      lv_tmp[lo:lo + 64, :, :, :], ALU.add)
                dve.wait_ge(sem("lv_mm"), LEVELS + 2)
                m = LEVELS + 1
                for r in range(2):
                    ins = dve.tensor_scalar(gla_a[0:64, :, r::2, 64:128],
                                            ps[0:64, 4 + 2 * (m % 2) + r, :].rearrange("p (c k t) -> p c k t", c=NC, k=2),
                                            GK ** -0.5, None, ALU.mult)
                link(ins)
                for r in range(2):
                    ins = dve.tensor_tensor(s_ta[:, :, r, :, :],
                                            ps[0:NS, 4 + r, 0:3 * 2 * NS].rearrange("p (n k t) -> p n k t", n=3, k=2),
                                            const[0:NS, C_LEVEL:C_LEVEL + 192].rearrange("p (n t) -> p n t", n=3)
                                            [:, :, 0:NS].unsqueeze(2).broadcast_to([NS, 3, 2, NS]), ALU.mult)
                link(ins)
                s_a_v = s_a[:, :, :].rearrange("p (k r) t -> p r k t", r=2)
                link(dve.tensor_tensor(s_a_v, s_ta[:, 0, :, :, :], s_ta[:, 1, :, :, :], ALU.add))
                link(dve.tensor_tensor(s_a_v, s_a_v, s_ta[:, 2, :, :, :], ALU.add))

            e_last = hf[0][:, 0:2 * (NC + B)].rearrange("p (f n) -> p f n", f=2)

            def into_chunk():
                dve.wait_ge(sem("in_exp"), 1)
                dve.scalar_tensor_tensor(out=z[:, Z_GQ:Z_GQ + 2, :], in0=z[:, Z_GQ:Z_GQ + 2, :],
                                         scalar=GK ** -0.5, in1=lv_e[:, :, :], op0=ALU.mult, op1=ALU.mult)
                dve.tensor_copy(e_last[:, :, 0:NC], lv_e[:, :, L - 1:TP:L])
                link(dve.tensor_copy(e_last[:, :, NC:NC + B], lv_e[:, :, TP + TS - 1:T:TS]))
                for n in range(2):
                    src = decay[:, n, 0:TP].rearrange("p (c t) -> p c t", c=NC)
                    dve.tensor_tensor(lv_e[:, n, 0:TP].rearrange("p (c t) -> p c t", c=NC),
                                      src[:, :, L - 1:L].broadcast_to([128, NC, L]), src, ALU.subtract)
                    src = decay[:, n, TP:T].rearrange("p (b t) -> p b t", b=B)
                    ins = dve.tensor_tensor(lv_e[:, n, TP:T].rearrange("p (b t) -> p b t", b=B),
                                            src[:, :, TS - 1:TS].broadcast_to([128, B, TS]), src, ALU.subtract)
                ins.then_inc(sem("in_diff"), 1)

            def out_of_chunk():
                dve.wait_ge(sem("in_exp"), 2)
                dve.tensor_tensor(z[:, Z_GK:Z_GK + 2, :], z[:, Z_GK:Z_GK + 2, :], lv_e[:, :, :], ALU.mult)\
                   .then_inc(sem("levels_done"), 1)

            def make_rows():
                dve.wait_ge(sem("log_rows"), 1)
                link(dve.scalar_tensor_tensor(out=row(R_W), in0=row(R_W), scalar=0.0, in1=row(R_T), op0=ALU.min,
                                              op1=ALU.subtract))
                dve.tensor_tensor_scan(row(R_B), restart[0:H, :], row(R_W), 0.0, ALU.mult, ALU.add)
                dve.tensor_tensor_scan(row(R_M, 0, TP), row(R_W, 0, TP), row(R_U, 0, TP), 0.0, ALU.add, ALU.max)
                dve.memset(scan_in[:, 0, :, 0:1], -3.0e38)
                dve.tensor_copy(scan_in[:, 1, :, 0:1], m0[:, :].unsqueeze(2))
                dve.tensor_copy(scan_in[:, 0, :, 1:], by_seq(R_W))
                dve.memset(row(R_WI, 0, L), 0.0)
                link(dve.tensor_copy(scan_in[:, 1, :, 1:], by_seq(R_U)))
                link(dve.tensor_tensor_scan(scan_in[:, 2, :, :].rearrange("p b t -> p (b t)"),
                                            scan_in[:, 0, :, :].rearrange("p b t -> p (b t)"),
                                            scan_in[:, 1, :, :].rearrange("p b t -> p (b t)"), 0.0, ALU.add, ALU.max))
                link(dve.tensor_copy(by_seq(R_M), scan_in[:, 2, :, 1:]))

            def make_weight_rows():
                dve.tensor_tensor(row(R_U), row(R_U), row(R_B), ALU.subtract)
                dve.tensor_tensor(row(R_W), row(R_B), row(R_M), ALU.subtract)
                dve.tensor_copy(by_chunk(R_WI)[:, 1:NC, :],
                                by_chunk(R_M)[:, 0:NC - 1, L - 1:L].broadcast_to([H, NC - 1, L]))
                link(dve.tensor_copy(by_seq(R_WI), m0[:, :].unsqueeze(2).broadcast_to([H, B, TS])))
                dve.tensor_tensor(row(R_WI), row(R_WI), row(R_W), ALU.add)
                dve.tensor_tensor(by_chunk(R_WL), by_chunk(R_U), by_chunk(R_W)[:, :, L - 1:L].broadcast_to([H, NC, L]),
                                  ALU.add)
                dve.tensor_tensor(by_seq(R_WL), by_seq(R_U), by_seq(R_W)[:, :, TS - 1:TS].broadcast_to([H, B, TS]),
                                  ALU.add).then_inc(sem("rows_made"), 1)

            for k in range(NZ):
                dve.wait_ge(pe_unit, U_IN + k + 1)
                dve.tensor_copy(halves(z[:, k, :]), pair(B_IN + k if k < Z_GV else k % 2)).then_inc(evac, 1)
                split(U_IN + k + 2)
                if k == S_DECAY:
                    dve.wait_ge(sem("small_in"), 16 * 6)
                    dve.wait_ge(sem("a2_mm"), 1)
                    for n in range(2):
                        ins = dve.tensor_scalar(halves(decay[:, n, :]), ps[:, 4 + 2 * n:6 + 2 * n, 0:HT],
                                                gains[:, G_BA + n:G_BA + n + 1], None, ALU.add)
                    ins.then_inc(sem("y_decay"), 1)
                if k == S_DECAY + 1:
                    make_decay()
                if k in S_DIFF:
                    level_diff(S_DIFF.index(k) + 1)
                if k in S_QK:
                    level_masked(S_QK.index(k))
                    level_qk(S_QK.index(k) + 1)
                if k == S_SUM:
                    level_sum()
                if k == S_IN:
                    into_chunk()
                    dve.tensor_scalar(row(R_U), z[0:H, Z_GATE, :], gate_b[0:H, 0:1], None, ALU.add)
                    dve.tensor_scalar(row(R_W), z[32:32 + H, Z_GATE, :], gate_b[32:32 + H, 0:1], None, ALU.add)\
                       .then_inc(sem("y_rows"), 1)
                if k == S_OUT:
                    out_of_chunk()
                    make_rows()
                if k == S_ROWS:
                    make_weight_rows()

            def gla_gate(j):
                dve.wait_ge(sem("gg_sig"), j + 1)
                dve.tensor_tensor(z[:, Z_GG + j, :], z[:, Z_GG + j, :], gg_sig[j][:, :], ALU.mult)

            def chunk_weights(c, n):
                t0 = c * L
                dve.wait_ge(sem("pe_a"), 9 * c + 1)
                link(dve.tensor_copy(ucol[0:n, :], ps[0:n, 7, 0:2 * H]))
                dve.wait_ge(sem("pe_a"), 9 * c + 2)
                for h in range(H):
                    ins = dve.tensor_scalar(ew[0:n, h, 0:n], ps[0:n, 0, h * n:h * n + n], ucol[0:n, h:h + 1], 0.0,
                                            ALU.add, ALU.min)
                ins.then_inc(sem("w_arg"), 1)
                dve.wait_ge(sem("pe_a"), 9 * c + 3)
                wi = ps[:, 1, 0:H * n].rearrange("p (h t) -> p h t", h=H)
                dve.tensor_copy(il[:, :], wi[:, :, n - 1])
                dve.tensor_tensor(q_in[:, :, 0:n], wi, z[:, Z_MQ:Z_MQ + H, t0:t0 + n], ALU.mult)\
                   .then_inc(sem("q_in_done"), 1)
                dve.wait_ge(sem("pe_a"), 9 * c + 6)
                for h in range(H):
                    ins = dve.tensor_scalar(kw_tok[0:n, h, :], ps[0:n, 4, h * DK:(h + 1) * DK],
                                            ucol[0:n, H + h:H + h + 1], DK ** -0.5, ALU.mult, ALU.mult)
                ins.then_inc(sem("kw_done"), 1)
                dve.wait_ge(sem("w_masked"), c + 1)
                dve.wait_ge(sem("pe_a"), 9 * c + 4)
                dve.scalar_tensor_tensor(out=pw[0:n, :, 0:n], in0=ps[0:n, 3, 0:H * n]
                                         .rearrange("p (h t) -> p h t", h=H), scalar=DK ** -0.5,
                                         in1=ew[0:n, :, 0:n], op0=ALU.mult, op1=ALU.mult).then_inc(sem("p_done"), 1)

            def chunk_heads(c, n):
                t0 = c * L
                dve.wait_ge(sem("pe_a"), 9 * c + 5)
                dve.wait_ge(sem("den_abs"), c + 1)
                if c < NC:
                    dve.wait_ge(sem("num_mm"), c + 1)
                else:
                    dve.wait_ge(sem("num_back"), 1)
                link(dve.tensor_tensor(den[:, :, 0:n], ps[:, 2, 0:H * n].rearrange("p (h t) -> p h t", h=H),
                                       den[:, :, 0:n], ALU.max))
                link(dve.reciprocal(den[:, :, 0:n], den[:, :, 0:n]))
                dve.tensor_tensor(z[:, Z_MQ:Z_MQ + H, t0:t0 + n],
                                  ps[:, 0, 0:H * n].rearrange("p (h t) -> p h t", h=H), den[:, :, 0:n], ALU.mult)\
                   .then_inc(sem("heads_done"), 1)

            for c in range(NC):
                chunk_weights(c, L)
                gla_gate(c)
                chunk_heads(c, L)
                dve.wait_ge(sem("state_mm"), c + 1)
                if c == 0:
                    dve.wait_ge(sem("zeros_set"), 2)
                    dve.tensor_copy(c_st[:, :, :], ps[:, 4, :].rearrange("p (h v) -> p h v", h=H))
                    dve.tensor_copy(n_st[:, :, :], ps[:, 5, :].rearrange("p (h v) -> p h v", h=H))
                    for h in range(H):
                        r = 64 * (h % 2)
                        ins = dve.tensor_copy(s_st[r:r + 64, h, :], ps[r:r + 64, 6, h * DV:(h + 1) * DV])
                else:
                    for h in range(H):
                        dve.scalar_tensor_tensor(out=c_st[:, h, :], in0=c_st[:, h, :], scalar=il[:, h:h + 1],
                                                 in1=ps[:, 4, h * DV:(h + 1) * DV], op0=ALU.mult, op1=ALU.add)
                        dve.scalar_tensor_tensor(out=n_st[:, h, :], in0=n_st[:, h, :], scalar=il[:, h:h + 1],
                                                 in1=ps[:, 5, h * 128:(h + 1) * 128], op0=ALU.mult, op1=ALU.add)
                        r = 64 * (h % 2)
                        ins = dve.scalar_tensor_tensor(out=s_st[r:r + 64, h, :], in0=s_st[r:r + 64, h, :],
                                                 scalar=e_last[r:r + 64, h // 2, c:c + 1],
                                                 in1=ps[r:r + 64, 6, h * DV:(h + 1) * DV], op0=ALU.mult, op1=ALU.add)
                ins.then_inc(sem("chunk_done"), 1)
                dve.wait_ge(sem("chunk_done"), c + 1)

            c, n = NC, NS
            chunk_weights(c, n)
            dve.memset(gk_pair[:, :, :], 0.0).then_inc(sem("pair_zero"), 1)
            dve.wait_ge(sem("n_mm"), 1)
            link(dve.tensor_copy(s_n[:, :, :], ps[:, 2, 300:300 + NS].rearrange("p (b h) -> p b h", b=B)))
            dve.tensor_tensor(s_qn[:, :, :].rearrange("p h (b t) -> p h b t", b=B),
                              q_in[:, :, 0:NS].rearrange("p h (b t) -> p h b t", b=B),
                              s_n[:, :, :].rearrange("p b h -> p h b").unsqueeze(3).broadcast_to([128, H, B, TS]),
                              ALU.mult).then_inc(sem("qn_done"), 1)
            il_s = rinv[:, 0:H * B].rearrange("p (h b) -> p h b", h=H)
            dve.tensor_copy(il_s, ps[:, 1, 0:H * n].rearrange("p (h b t) -> p h b t", h=H, b=B)[:, :, :, TS - 1])\
               .then_inc(sem("il_s_done"), 1)
            dve.wait_ge(sem("il_s_done"), 1)

            def own_values(u):
                if u >= 2:
                    dve.wait_ge(sem("upd_mm"), u - 1)
                if u == H:
                    dve.wait_ge(sem("pair_made"), 1)
                m = NS if u < H else 2 * NS
                src = v_tok[0:NS, u, :] if u < H else gv_pair[:, u - H, :]
                dve.tensor_tensor(v_own[u % 2][0:m, :, :], src.unsqueeze(1).broadcast_to([m, B, DV]),
                                  own_rows[0:m, :].unsqueeze(2).broadcast_to([m, B, DV]), ALU.mult)\
                   .then_inc(sem("v_own"), 1)

            def in_banks(t3d):
                return t3d.rearrange("p b v -> p (b v)").rearrange("p (k f) -> p k f", k=2)

            dve.wait_ge(sem("row_zeros"), 1)
            dve.tensor_copy(q_row[:, :, :].rearrange("p h (b x) -> p h b x", b=B)[:, :, :, 0:TS],
                            q_in[:, :, 0:NS].rearrange("p h (b t) -> p h b t", b=B)).then_inc(sem("rows_filled"), 1)
            dve.wait_ge(sem("tok_done"), 3 * c + 3)
            own_values(0)
            dve.wait_ge(sem("row_zeros"), 2)
            for r in range(2):
                ins = dve.tensor_copy(s_row[64 * r:64 * r + 64, :, NS * r:NS * r + B * s_pitch]
                                      .rearrange("p k (b x) -> p k b x", b=B)[:, :, :, 0:TS],
                                      z[64 * r:64 * r + 64, Z_GQ:Z_GQ + 2, TP:T].rearrange("p k (b t) -> p k b t", b=B))
            ins.then_inc(sem("rows_filled"), 1)
            for h in range(H):
                if h + 1 < H:
                    own_values(h + 1)
                st = ring[h]
                dve.wait_ge(sem(f"state_in{h}"), 16)
                dve.wait_ge(sem("num_s"), h + 1)
                link(dve.tensor_tensor(st[:, :, :], st[:, :, :], il_s[:, h, :].unsqueeze(2).broadcast_to([128, B, DV]),
                                       ALU.mult))
                dve.wait_ge(sem("upd_mm"), h + 1)
                q = 4 + 2 * (h % 2)
                dve.tensor_tensor(in_banks(st[:, :, :]), ps[:, q:q + 2, :], in_banks(st[:, :, :]), ALU.add)\
                   .then_inc(sem("upd_free"), 1)
            dve.wait_ge(sem("nnew_mm"), 1)
            link(dve.tensor_tensor(s_n2[:, :, :], s_n[:, :, :], il_s.rearrange("p h b -> p b h"), ALU.mult))
            dve.tensor_tensor(s_n2[:, :, :].rearrange("p b h -> p h b"),
                              ps[:, 3, 256:256 + H * B].rearrange("p (h b) -> p h b", h=H),
                              s_n2[:, :, :].rearrange("p b h -> p h b"), ALU.add).then_inc(sem("n2_done"), 1)
            dve.wait_ge(sem("n2_mm"), 1)
            dve.tensor_copy(s_nrow2[:, :], ps[0:NS, 3, 384:384 + DK]).then_inc(sem("n_new"), 1)
            chunk_heads(c, n)

            def gated(j, lo, hi):
                og = z[:, Z_MO + j, lo:hi] if j < H else z[:, Z_GG + j - H, lo:hi]
                gc = G_ML + j if j < H else G_GLA + j - H
                return dve.scalar_tensor_tensor(out=head(j)[:, lo:hi], in0=head(j)[:, lo:hi],
                                                scalar=gains[:, gc:gc + 1], in1=og, op0=ALU.mult, op1=ALU.mult)

            def prompt_heads(n):
                for j in (2 * n, 2 * n + 1):
                    dve.wait_ge(sem("hn_sq"), j + 1)
                    ins = gated(j, 0, TP)
                link(ins)
                dve.wait_ge(sem("hn_inv"), n + 1)
                for j in (2 * n, 2 * n + 1):
                    dve.tensor_tensor(head(j)[:, 0:TP], head(j)[:, 0:TP], hinv[n % 2][:, j % 2, :], ALU.mult)\
                       .then_inc(sem("hn_y"), 1)

            own_values(H)
            for pr in range(2):
                u, st = H + pr, ring[pr]
                if pr == 0:
                    own_values(u + 1)
                dve.wait_ge(sem(f"state_in{pr}"), 32)
                dve.wait_ge(sem("o_s"), pr + 1)
                link(dve.tensor_tensor(st[:, :, :], st[:, :, :],
                                       e_last[:, pr, NC:NC + B].unsqueeze(2).broadcast_to([128, B, DV]), ALU.mult))
                dve.wait_ge(sem("upd_mm"), u + 1)
                q = 4 + 2 * (u % 2)
                dve.tensor_tensor(in_banks(st[:, :, :]), ps[:, q:q + 2, :], in_banks(st[:, :, :]), ALU.add)\
                   .then_inc(sem("upd_free"), 1)
                prompt_heads(pr)
            for n in range(2, H):
                prompt_heads(n)

            dve.wait_ge(sem("hn_sq"), 2 * H + 1)
            for j in range(2 * H):
                ins = gated(j, TP, T)
            link(ins)
            dve.wait_ge(sem("hn_inv"), H + 1)
            for n, zb in enumerate((Z_MQ, Z_GV)):
                ins = dve.tensor_tensor(z[:, zb:zb + H, TP:T], z[:, zb:zb + H, TP:T], heads_of(sig[0], n), ALU.mult)
            ins.then_inc(sem("hn_y"), 1)
            for j in range(2 * H):
                dve.wait_ge(sem("ym_hi"), j + 1)
                dve.tensor_tensor(xn_lo[:, j, :], head(j), xn_hi[:, j, :].bitcast(F32), ALU.subtract)\
                   .then_inc(sem("ym_lo"), 1)
            residual(U_OUT, B_OUT, 16)
            norm(2, G_XA)
            dve.wait_ge(sem("xnl_done"), 8 * 3)
            dve.memset(q_pad[:, :, :, :], 0.0)
            with dve.Fori(0, 2) as i:
                for k in range(4):
                    dve.wait_ge(pe_unit, i * 4 + (U_XQ + k + 1))
                    dve.tensor_copy(halves(xq[:, bass.ds(i * 4 + k, 1), :].rearrange("p a t -> p (a t)")),
                                    pair(B_XQ + k)).then_inc(evac, 1)
                    split(U_XQ + k + 2, i, 4)

            def softmax_max(scores, heads):
                link(dve.tensor_reduce(xmx[:, 8:8 + heads], scores, AX.X, ALU.max))
                dve.tensor_scalar(xmx[:, 0:heads], xmx[:, 8:8 + heads], -1.0 / 16, None, ALU.mult)\
                   .then_inc(sem("x_max"), 1)

            def softmax_scale(k, pr, heads):
                dve.wait_ge(sem("x_exp"), k + 1)
                link(dve.reciprocal(xmx[:, 8:8 + heads], xmx[:, 4:4 + heads]))
                for h in range(heads):
                    ins = dve.tensor_scalar(pr[:, h, :], pr[:, h, :], xmx[:, 8 + h:9 + h], None, ALU.mult)
                ins.then_inc(sem("p_ready"), 1)

            dve.wait_ge(sem("kT_mm"), 1)
            dve.tensor_copy(kT[0][:, 4:8, :], ps[:, 2:4, :].rearrange("p b (k m) -> p (b k) m", k=2))\
               .then_inc(sem("kT_dve"), 1)

            def prompt_softmax(tb):
                q = 4 * (tb % 2)
                dve.wait_ge(sem("sc_mm"), tb + 1)
                softmax_max(ps[:, q:q + 2, :].rearrange("p b (k m) -> p (b k) m", k=2), H)
                softmax_scale(tb, prob[tb % 2], H)

            prompt_softmax(0)
            for h in range(H):
                for par in range(2):
                    row = 16 * par + TS * h
                    ins = dve.tensor_copy(q_pad[:, 2 * h:2 * h + 2, par::2, row:row + TS],
                                          xq[:, 2 * h:2 * h + 2, TP:T].rearrange("p k (b t) -> p k b t", b=B)
                                          [:, :, par::2, :])
            ins.then_inc(sem("q_padded"), 1)
            for tb in range(NC):
                q = 4 * (tb % 2)
                dve.wait_ge(sem("pT_mm"), tb + 1)
                dve.tensor_copy(probT[tb % 2][:, :, :], ps[:, q + 2:q + 4, :].rearrange("p b (k t) -> p (b k) t", k=4))\
                   .then_inc(sem("pT_copied"), 1)
                if tb + 1 < NC:
                    prompt_softmax(tb + 1)
                dve.wait_ge(sem("av_hi"), tb + 1)
                dve.tensor_tensor(xn_lo[:, :, tb * 128:tb * 128 + 128],
                                  ps[:, q:q + 2, :].rearrange("p b (k t) -> p (b k) t", k=4),
                                  xn_hi[:, :, tb * 128:tb * 128 + 128].bitcast(F32), ALU.subtract)\
                   .then_inc(sem("av_lo"), 1)
            for b in range(B):
                dve.wait_ge(sem("kT_mm"), 2 * b + 3)
                if b >= 2:
                    dve.wait_ge(sem("ssc_mm"), b - 1)
                dve.tensor_copy(kT[(b + 1) % 2][:, 4:8, :], k_banks(2 * b + 1)).then_inc(sem("kT_dve"), 1)
            dve.memset(p_pad[:, :, :, :, :], 0.0)
            dve.wait_ge(sem("ssc_mm"), B)
            softmax_max(ps[:, 4, 0:MEM].unsqueeze(1), 1)
            softmax_scale(NC, prob[0], 1)
            dve.wait_ge(sem("pT_mm"), NC + 1)
            p_rows = ps[:, 7, 0:MEM].rearrange("p (m b h t) -> p m h b t", m=2, b=B, h=H)
            for b in range(B):
                ins = dve.tensor_copy(p_pad[:, :, :, b, TS * b:TS * b + TS], p_rows[:, :, :, b, :])
            ins.then_inc(sem("pT_copied"), 1)
            dve.wait_ge(sem("sav_mm"), B)
            dve.tensor_copy(s_av[0:NS, :, :].rearrange("p (h e) f -> p h (e f)", h=H), ps[0:NS, 0:H, 0:256])\
               .then_inc(sem("sav_copied"), 1)
            dve.wait_ge(sem("av_hi"), NC + 1)
            dve.tensor_tensor(xn_lo[:, :, TP:T], ps[:, 5, 0:ND * NS].rearrange("p (k t) -> p k t", k=ND),
                              xn_hi[:, :, TP:T].bitcast(F32), ALU.subtract).then_inc(sem("av_lo"), 1)

            residual(U_XO, B_XO, 24)
            norm(3, G_FFN2)
            ffn_up(1, U_UP2, B_UP2)
            ffn_down(U_DN2, B_DN2, 32, True)
            dve.wait_ge(sem("norm_inv"), 5)
            for d in range(ND):
                dve.scalar_tensor_tensor(out=yf[:, d, :], in0=x[:, d, :], scalar=gains[:, G_FIN + d:G_FIN + d + 1],
                                         in1=rinv[:, :], op0=ALU.mult, op1=ALU.mult).then_inc(sem("yf_done"), 1)

        @block.tensor
        def _(pe):
            pe_unit, evac, lo_done = sem("pe_unit"), sem("evac"), sem("lo_done")

            def mm(out, lhsT, rhs, start=True, stop=True):
                return pe.matmul(out, lhsT, rhs, start=start, stop=stop)

            pe.wait_ge(sem("const_in"), 16)
            pe.wait_ge(sem("mem_gain_in"), 16)
            pe.transpose(ps[:, 7, 0:ND], mem_gain[:, :], const[0:ND, 0:ND]).then_inc(sem("gain_mm"), 1)
            pe.wait_ge(sem("mem_in"), 16)
            for d in range(ND):
                for mb in range(2):
                    c = MEM * (d % 2) + 128 * mb
                    ins = pe.transpose(ps[:, d // 2, c:c + 128], mem_nat[:, mb, d * 128:d * 128 + 128], ident)
                ins.then_inc(sem("memT_mm"), 1)

            def transpose_x(d):
                q = 4 + 2 * (d % 2)
                if d == 0:
                    pe.wait_ge(sem("x_in"), 16)
                    pe.wait_ge(sem("xs_in"), 16)
                if d >= 2:
                    pe.wait_ge(sem("x_made"), d - 1)
                for c in range(NC):
                    pe.transpose(ps[:, q, c * L:(c + 1) * L], xp_nat[:, c, d * 128:d * 128 + 128], ident)
                pe.transpose(ps[:, q + 1, 0:NS], xs_nat[:, d * 128:d * 128 + 128], const[0:NS, 0:NS])\
                  .then_inc(sem("xT_mm"), 1)
                if d == ND - 1:
                    pe.wait_ge(sem("x_made"), d)
                    pe.wait_ge(sem("gains_in"), 16 * 9)
                    pe.transpose(ps[:, 5, 256:256 + N_GAIN], gain_rows[:, :], const[0:N_GAIN, 0:N_GAIN])\
                      .then_inc(sem("gain_mm"), 1)

            def norm(g, buf):
                pe.wait_ge(sem("acc_done"), 8 * (g + 1))
                if buf >= 4:
                    pe.wait_ge(evac, buf - 3)
                mm(pair(buf)[:, 0, :], ones, acc[:, 0:HT])
                mm(pair(buf)[:, 1, :], ones, acc[:, HT:T]).then_inc(sem("norm_mm"), 1)

            for u in range(16):
                if u == U_N1:
                    pe.wait_ge(sem("x_made"), ND)
                    pe.wait_ge(sem("gains_made"), 1)
                    norm(0, B_N1)
                pe.wait_ge(lo_done, u + 1)
                if u < 4:
                    pe.wait_ge(sem("mem_lo_done"), 1 + u // 2)
                buf = (u // 4) % 2
                if u == 8:
                    pe.wait_ge(evac, 1)
                if u == 12:
                    pe.wait_ge(evac, 2)
                for kt in range(2):
                    k = 2 * (u % 4) + kt
                    cols = slice(512 * kt, 512 * kt + 512)
                    for mb in range(2):
                        dst, toks = ps[:, 2 * (buf % 4) + mb, :], slice(128 * mb, 128 * mb + 128)
                        mm(dst, mem_hi[:, k, toks], w_hi[u % 2][:, cols], k == 0, False)
                        mm(dst, mem_hi[:, k, toks], w_lo[u % 2][:, cols], False, False)
                        ins = mm(dst, mem_lo[:, k, toks], w_hi[u % 2][:, cols], False, k == 7)
                ins.then_inc(pe_unit, 1)
                if u < ND:
                    transpose_x(u)

            def unit(u, buf, hi, lo, k0, nk, first, last, only=None, made=None, base_=0):
                for j in (range(nk) if only is None else (only,)):
                    wh = w_hi[u % 2][:, 128 * j:128 * j + 128]
                    wl = w_lo[u % 2][:, 128 * j:128 * j + 128]
                    for n, (w, m) in enumerate(((wh, hi), (wl, hi), (wh, lo))):
                        if made is not None and n in (0, 2):
                            pe.wait_ge(made[n // 2], base_ + j + 1)
                        for half in range(2):
                            ins = mm(ps[:, 2 * (buf % 4) + half, 0:HT], w, m[:, k0 + j, half * HT:(half + 1) * HT],
                                     first and j == 0 and n == 0, last and j == nk - 1 and n == 2)
                if only is None or only == nk - 1:
                    ins.then_inc(pe_unit, 1)

            LAG = 2
            XN_MADE = (sem("xnh_done"), sem("xnl_done"))

            def first_two(u0, b0, made, base_):
                pe.wait_ge(lo_done, u0 + 2)
                pe.wait_ge(evac, b0)
                for d in range(ND + LAG):
                    if d < ND:
                        unit(u0, b0, xn_hi, xn_lo, 0, 8, True, True, d, made, base_)
                    if d >= LAG:
                        unit(u0 + 1, b0 + 1, xn_hi, xn_lo, 0, 8, True, True, d - LAG)

            def blocks(u0, b0, bodies, made=None, base_=0):
                def step(k, i=0):
                    pe.wait_ge(lo_done, i * 4 + (u0 + k + 1))
                    pe.wait_ge(evac, i * 4 + (b0 + k - 3))
                    unit(u0 + k, b0 + k, xn_hi, xn_lo, 0, 8, True, True)

                if made is not None:
                    first_two(u0, b0, made, base_)
                    for k in (2, 3):
                        step(k)
                    bodies, u0, b0 = bodies - 1, u0 + 4, b0 + 4
                with pe.Fori(0, bodies) as i:
                    for k in range(4):
                        step(k, i)

            def ffn_down(n, u0, b0):
                with pe.Fori(0, 2) as i:
                    for k in range(12):
                        pe.wait_ge(lo_done, i * 12 + (u0 + k + 1))
                        if k % 3 == 0:
                            pe.wait_ge(evac, i * 4 + (b0 + k // 3 - 3))
                        lo, hi = DN_K[k % 3]
                        if k < 3:
                            pe.wait_ge(sem("hl_done"), NF * n + hi)
                        unit(u0 + k, b0 + k // 3, h_hi, h_lo, lo, hi - lo, k % 3 == 0, k % 3 == 2)

            blocks(U_UP1, B_UP1, NF // 2, XN_MADE, 0)
            ffn_down(0, U_DN1, B_DN1)
            norm(1, B_N2)
            first_two(U_IN, B_IN, XN_MADE, 8)

            def decay_product():
                pe.wait_ge(evac, B_IN + Z_GV)
                pe.wait_ge(sem("small_in"), 16 * 6)
                for n in range(2):
                    for half in range(2):
                        ins = mm(ps[:, 4 + 2 * n + half, 0:HT], a2w[:, 128 * n:128 * n + 128],
                                 z[0:RANK, Z_GA, half * HT:(half + 1) * HT])
                ins.then_inc(sem("a2_mm"), 1)

            def level_scores(n):
                if n == 0:
                    q_, k_ = z[:, Z_GQ:Z_GQ + 2, :], z[:, Z_GK:Z_GK + 2, :]
                    pe.wait_ge(evac, B_IN + Z_GV)
                    pe.wait_ge(sem("y_decay"), 1)
                else:
                    q_, k_ = lv_q[n % 2][:, :, :], lv_k[n % 2][:, :, :]
                    pe.wait_ge(sem("lv_qk"), n)
                if n >= 2:
                    pe.wait_ge(sem("lv_masked"), n - 1)
                for r in range(2):
                    rr = slice(64 * r, 64 * r + 64)
                    bank = 4 + 2 * (n % 2) + r
                    for c in range(NC):
                        for pr in range(2):
                            at_ = (c * 2 + pr) * 64
                            if n <= LEVELS:
                                for j in range(2):
                                    tt = slice(c * L + 64 * j, c * L + 64 * j + 64)
                                    ins = mm(ps[64 * j:64 * j + 64, bank, at_:at_ + 64], k_[rr, pr, tt],
                                             q_[rr, pr, tt])
                            else:
                                ins = mm(ps[0:64, bank, at_:at_ + 64], k_[rr, pr, c * L:c * L + 64],
                                         q_[rr, pr, c * L + 64:c * L + 128])
                if n == LEVELS + 1:
                    pe.wait_ge(sem("lv_masked"), n)
                    for m in range(3):
                        for r in range(2):
                            rr = slice(64 * r, 64 * r + 64)
                            for pr in range(2):
                                at_ = (m * 2 + pr) * NS
                                k_ = s_lv[rr, m - 1, 1, pr, :] if m else z[rr, Z_GK + pr, TP:T]
                                q_ = s_lv[rr, m - 1, 0, pr, :] if m else z[rr, Z_GQ + pr, TP:T]
                                ins = mm(ps[0:NS, 4 + r, at_:at_ + NS], k_, q_)
                ins.then_inc(sem("lv_mm"), 1)

            for k in range(2, NZ):
                pe.wait_ge(lo_done, U_IN + k + 1)
                pe.wait_ge(evac, B_IN + k - (3 if k < Z_GV else 1))
                unit(U_IN + k, B_IN + k if k < Z_GV else k % 2, xn_hi, xn_lo, 0, 8, True, True)
                if k == S_DECAY - 1:
                    decay_product()
                if k in S_SCORES:
                    level_scores(S_SCORES.index(k))

            def chunk_first(c, n):
                t0 = c * L
                tt = slice(t0, t0 + n)
                if c == 0:
                    pe.wait_ge(sem("levels_done"), 1)
                    pe.wait_ge(sem("rows_exp"), 3)
                    pe.wait_ge(evac, B_IN + NZ)
                else:
                    pe.wait_ge(sem("heads_done"), c)
                    pe.wait_ge(sem("gla_out"), c)

                def spread(bank, r):
                    for h in range(H):
                        ins = mm(ps[:, bank, h * n:h * n + n], sel[:, h, :], rows[:, r, tt])
                    ins.then_inc(sem("pe_a"), 1)

                pe.transpose(ps[0:n, 7, 0:H], rows[:, R_U, tt], const[0:H, 0:H])
                pe.transpose(ps[0:n, 7, H:2 * H], rows[:, R_WL, tt], const[0:H, 0:H])\
                  .then_inc(sem("pe_a"), 1)
                spread(0, R_W)
                spread(1, R_WI)
                for h in range(H):
                    ins = mm(ps[0:n, 3, h * n:h * n + n], z[:, Z_MK + h, tt], z[:, Z_MQ + h, tt])
                ins.then_inc(sem("pe_a"), 1)
                spread(2, R_EM)
                if c:
                    pe.wait_ge(sem("chunk_done"), c)

                def to_tokens(bank, zb, blocks_):
                    for h in range(blocks_):
                        ins = pe.transpose(ps[0:n, bank, h * 128:h * 128 + 128], z[:, zb + h, tt], ident)
                    ins.then_inc(sem("pe_a"), 1)

                to_tokens(4, Z_MK, 4)
                to_tokens(5, Z_MV, 4)
                to_tokens(6, Z_GK, 2)
                pe.wait_ge(sem("w_arg"), c + 1)
                if c == NC:
                    for pr in range(2):
                        mm(ps[n:2 * n, 6, pr * 128:pr * 128 + 128], z[:, Z_GK + pr, tt], ident)
                        mm(ps[n:2 * n, 7, pr * 128:pr * 128 + 128], z[:, Z_GV + 2 * pr + 1, tt], ident)
                to_tokens(7, Z_GV, 4)

            for c in range(NC):
                chunk_first(c, L)
                tt = slice(c * L, c * L + L)
                pe.wait_ge(sem("q_in_done"), c + 1)
                pe.wait_ge(sem("kw_done"), c + 1)
                pe.wait_ge(sem("p_done"), c + 1)
                pe.wait_ge(sem("tok_done"), 3 * c + 3)
                for h in range(H):
                    hh = slice(h * L, h * L + L)
                    ins = mm(ps[:, 3, hh], ones, pw[:, h, :], True, c == 0)
                    if c:
                        ins = mm(ps[:, 3, hh], n_st[:, h, :], q_in[:, h, :], False, True)
                ins.then_inc(sem("den_mm"), 1)
                for h in range(H):
                    hh = slice(h * L, h * L + L)
                    ins = mm(ps[:, 0, hh], v_tok[:, h, :], pw[:, h, :], True, c == 0)
                    if c:
                        ins = mm(ps[:, 0, hh], c_st[:, h, :], q_in[:, h, :], False, True)
                ins.then_inc(sem("num_mm"), 1)
                for h in range(H):
                    hh = slice(h * L, h * L + L)
                    ins = mm(ps[:, 7, hh], gv_tok[:, h, :], gla_a[:, c, h, :], True, c == 0)
                    if c:
                        ins = mm(ps[:, 7, hh], s_st[:, h, :], z[:, Z_GQ + h // 2, tt], False, True)
                ins.then_inc(sem("gla_mm"), 1)
                for h in range(H):
                    mm(ps[:, 4, h * DV:(h + 1) * DV], kw_tok[:, h, :], v_tok[:, h, :])
                    mm(ps[:, 5, h * 128:(h + 1) * 128], kw_tok[:, h, :], ones)
                for pr in range(2):
                    ins = mm(ps[:, 6, 256 * pr:256 * pr + 256], gk_tok[:, pr, :],
                             gv_tok[:, 2 * pr:2 * pr + 2, :].rearrange("p h v -> p (h v)"))
                ins.then_inc(sem("state_mm"), 1)

            c, n = NC, NS
            chunk_first(c, n)
            pe.wait_ge(sem("n_in"), 16)
            pe.wait_ge(sem("tok_done"), 3 * c + 3)
            pe.transpose(ps[:, 2, 300:300 + NS], s_nrow[:, :], const[0:NS, 0:NS]).then_inc(sem("n_mm"), 1)
            pe.wait_ge(sem("kw_done"), c + 1)
            pe.wait_ge(sem("p_done"), c + 1)
            pe.wait_ge(sem("qn_done"), 1)
            for h in range(H):
                mm(ps[:, 3, h * n:h * n + n], const[0:NS, C_ONE:C_ONE + 128], pw[0:n, h, 0:n], True, False)
                ins = mm(ps[:, 3, h * n:h * n + n], ones, s_qn[:, h, :], False, True)
            ins.then_inc(sem("den_mm"), 1)

            def update(u, keys):
                pe.wait_ge(sem("v_own"), u + 1)
                if u == 1:
                    pe.wait_ge(sem("pair_made"), 1)
                if u >= 2:
                    pe.wait_ge(sem("upd_free"), u - 1)
                q = 4 + 2 * (u % 2)
                vo = v_own[u % 2][0:NS if u < H else 2 * NS, :, :].rearrange("p b v -> p (b v)")
                mm(ps[:, q, :], keys, vo[:, 0:512])
                mm(ps[:, q + 1, :], keys, vo[:, 512:1024]).then_inc(sem("upd_mm"), 1)

            pe.wait_ge(sem("rows_filled"), 1)
            for h in range(H):
                pe.wait_ge(sem(f"state_in{h}"), 16)
                dst = ps[0:n, 0, h * DV:(h + 1) * DV]
                mm(dst, pw[0:n, h, 0:n], v_tok[0:n, h, :], True, False)
                for b in range(B):
                    ins = mm(dst, q_row[:, h, b * n:(b + 1) * n], ring[h][:, b, :], False, b == B - 1)
                ins.then_inc(sem("num_s"), 1)
                update(h, kw_tok[0:n, h, :])
            pe.wait_ge(sem("den_abs"), c + 1)
            for h in range(H):
                ins = mm(ps[:, 3, 256 + h * B:256 + h * B + B], kw_tok[0:n, h, :], own)
            ins.then_inc(sem("nnew_mm"), 1)
            pe.wait_ge(sem("num_copied"), 1)
            for h in range(H):
                ins = pe.transpose(ps[:, 0, h * n:h * n + n], num_tok[:, h * DV:(h + 1) * DV], const[0:n, 0:n])
            ins.then_inc(sem("num_back"), 1)
            pe.wait_ge(sem("n2_done"), 1)
            pe.transpose(ps[0:NS, 3, 384:384 + DK], s_n2[:, :, :].rearrange("p b h -> p (b h)"), ident)\
              .then_inc(sem("n2_mm"), 1)
            pe.wait_ge(sem("il_s_done"), 1)

            def head_sum(n, dst, squares):
                pe.wait_ge(sem("hn_sq"), n + 1)
                if n >= 2:
                    pe.wait_ge(sem("hn_root"), n // 2)
                mm(dst, ones, squares).then_inc(sem("hn_mm"), 1)

            pe.wait_ge(sem("rows_filled"), 2)
            for pr in range(2):
                pe.wait_ge(sem(f"state_in{pr}"), 32)
                for r in range(2):
                    h = 2 * pr + r
                    mm(ps[n * r:n * r + n, 1, pr * DV:(pr + 1) * DV], s_a[:, h, :], gv_tok[0:n, h, :], True, False)
                for b in range(B):
                    ins = mm(ps[0:2 * n, 1, pr * DV:(pr + 1) * DV], s_row[:, pr, 2 * n * b:2 * n * (b + 1)],
                             ring[pr][:, b, :], False, b == B - 1)
                ins.then_inc(sem("o_s"), 1)
                update(H + pr, gk_pair[:, pr, :])
                for j in range(4 * pr, 4 * pr + 4):
                    head_sum(j, ps[:, 2 + j % 2, :], sq[j % 2][:, 0:TP])

            pe.wait_ge(sem("o_copied"), 1)
            for pr in range(2):
                ins = pe.transpose(ps[:, 1, 2 * n * pr:2 * n * (pr + 1)], o_tok[:, pr * DV:(pr + 1) * DV],
                                   const[0:2 * n, 0:2 * n])
            ins.then_inc(sem("o_back"), 1)
            head_sum(2 * H, ps[:, 2, 0:2 * H * NS], sq[0][:, 0:2 * H * NS])
            pe.wait_ge(sem("hn_root"), H + 1)
            blocks(U_OUT, B_OUT, 2, (sem("ym_hi"), sem("ym_lo")), 0)
            norm(2, B_N3)
            blocks(U_XQ, B_XQ, 2, XN_MADE, 16)

            def k_ready(n):
                pe.wait_ge(sem("kT_act"), n)
                pe.wait_ge(sem("kT_dve"), n)

            pe.wait_ge(evac, B_XQ + ND)
            pe.wait_ge(sem("kv_in0"), 16)
            for k in range(ND):
                for mb in range(2):
                    col = MEM * (k % 2) + 128 * mb
                    ins = pe.transpose(ps[:, k // 2, col:col + 128], kv[0][:, mb, k * 128:k * 128 + 128], ident)
            ins.then_inc(sem("kT_mm"), 1)
            k_ready(1)

            def scores(tb):
                q = 4 * (tb % 2)
                if tb >= 2:
                    pe.wait_ge(sem("av_lo"), tb - 1)
                for h in range(H):
                    for dd in range(2):
                        ins = mm(ps[:, q + h // 2, MEM * (h % 2):MEM * (h % 2) + MEM],
                                 xq[:, 2 * h + dd, tb * 128:tb * 128 + 128], kT[0][:, 2 * h + dd, :], dd == 0, dd == 1)
                ins.then_inc(sem("sc_mm"), 1)

            scores(0)
            scores(1)
            for tb in range(NC):
                q = 4 * (tb % 2)
                pe.wait_ge(sem("p_ready"), tb + 1)
                for k in range(ND):
                    ins = pe.transpose(ps[:, q + 2 + k // 4, 128 * (k % 4):128 * (k % 4) + 128],
                                       prob[tb % 2][:, k // 2, 128 * (k % 2):128 * (k % 2) + 128], ident)
                ins.then_inc(sem("pT_mm"), 1)
                if 1 <= tb < NC - 1:
                    scores(tb + 1)
                pe.wait_ge(sem("kv_in1"), 16)
                pe.wait_ge(sem("pT_copied"), tb + 1)
                for k in range(ND):
                    for mb in range(2):
                        ins = mm(ps[:, q + k // 4, 128 * (k % 4):128 * (k % 4) + 128],
                                 kv[1][:, mb, k * 128:k * 128 + 128], probT[tb % 2][:, 2 * (k // 2) + mb, :],
                                 mb == 0, mb == 1)
                ins.then_inc(sem("av_mm"), 1)
            pe.wait_ge(sem("av_lo"), NC)

            def transpose_sample_k(b):
                buf = b + 2
                pe.wait_ge(sem(f"kv_in{buf % KV_RING}"), 16 * (buf // KV_RING + 1))
                for half in range(2):
                    n = 2 * b + half
                    if n >= 3:
                        pe.wait_ge(sem("kT_dve" if half == 0 else "kT_act"), (n - 3) // 2 + 2)
                    for k in range(4 * half, 4 * half + 4):
                        for mb in range(2):
                            ins = pe.transpose(k_banks(n)[:, k % 4, 128 * mb:128 * mb + 128],
                                               kv[buf % KV_RING][:, mb, k * 128:k * 128 + 128], ident)
                    ins.then_inc(sem("kT_mm"), 1)

            pe.wait_ge(sem("q_padded"), 1)
            transpose_sample_k(0)
            for b in range(B):
                if b + 1 < B:
                    transpose_sample_k(b + 1)
                k_ready(b + 2)
                kt = kT[(b + 1) % 2]
                rows_ = slice(32 * (b // 2), 32 * (b // 2) + 32)
                for k in range(ND):
                    ins = mm(ps[rows_, 4, 0:MEM], q_pad[:, k, b, :], kt[:, k, :], b % 2 == 0 and k == 0,
                             b % 2 == 1 and k == ND - 1)
                ins.then_inc(sem("ssc_mm"), 1)
            pe.wait_ge(sem("p_ready"), NC + 1)
            for mb in range(2):
                ins = pe.transpose(ps[:, 7, 128 * mb:128 * mb + 128], prob[0][:, 0, 128 * mb:128 * mb + 128], ident)
            ins.then_inc(sem("pT_mm"), 1)
            pe.wait_ge(sem("pT_copied"), NC + 1)
            for b in range(B):
                n = 10 + b
                pe.wait_ge(sem(f"kv_in{n % KV_RING}"), 16 * (n // KV_RING + 1))
                for h in range(H):
                    for mb in range(2):
                        ins = mm(ps[0:NS, h, 0:256], p_pad[:, mb, h, b, :], kv[n % KV_RING][:, mb, 256 * h:256 * h + 256],
                                 b == 0 and mb == 0, b == B - 1 and mb == 1)
                ins.then_inc(sem("sav_mm"), 1)
            pe.wait_ge(sem("sav_copied"), 1)
            for k in range(ND):
                ins = pe.transpose(ps[:, 5, NS * k:NS * k + NS], s_av[0:NS, k, :], const[0:NS, 0:NS])
            ins.then_inc(sem("savT_mm"), 1)

            pe.wait_ge(sem("av_lo"), NC + 1)
            blocks(U_XO, B_XO, 2)
            norm(3, B_N4)
            blocks(U_UP2, B_UP2, NF // 2, XN_MADE, 24)
            ffn_down(1, U_DN2, B_DN2)
            norm(4, B_N5)
            pe.wait_ge(evac, B_N5 + 1)
            for c in range(NC + 1):
                n = L if c < NC else NS
                if c == 4:
                    pe.wait_ge(sem("y_copied"), 1)
                for d in range(ND):
                    if c == 0:
                        pe.wait_ge(sem("yf_done"), d + 1)
                    ins = pe.transpose(ps[0:n, 2 * (c % 4) + d // 4, 128 * (d % 4):128 * (d % 4) + 128],
                                       yf[:, d, c * L:c * L + n], ident)
                ins.then_inc(sem("yT_mm"), 1)


_INS = ["x_prompt", "x_sample", "mem_prompt", "cache_mem_k", "cache_mem_v", "state_mlstm_c", "state_mlstm_n",
        "state_mlstm_m", "state_gla_s", "ffn1_norm_g", "ffn1_w_gate", "ffn1_w_up", "ffn1_w_down", "mix_norm_g",
        "w_in", "mlstm_b_i", "mlstm_b_f", "mlstm_out_g", "gla_w_a2", "gla_b_a", "gla_out_g", "w_out",
        "xattn_norm_g", "mem_norm_g", "xattn_w_q", "xattn_w_k", "xattn_w_v", "xattn_w_o", "ffn2_norm_g",
        "ffn2_w_gate", "ffn2_w_up", "ffn2_w_down", "final_norm_g"]
_OUTS = [("y_prompt", (1, TP, D)), ("y_sample", (B, TS, D)), ("mem_k", (1, 1, MEM, H, D // H)),
         ("mem_v", (1, 1, MEM, H, D // H)), ("mlstm_c_p", (1, 1, H, DK, DV)), ("mlstm_n_p", (1, 1, H, DK)),
         ("mlstm_m_p", (1, 1, H)), ("gla_s_p", (1, 1, H, GK, DV)), ("mlstm_c_s", (1, B, H, DK, DV)),
         ("mlstm_n_s", (1, B, H, DK)), ("mlstm_m_s", (1, B, H)), ("gla_s_s", (1, B, H, GK, DV))]


def _constants(np):
    c = np.zeros((128, N_CONST), np.float32)
    c[:, C_ID:C_ID + 128] = np.eye(128)
    c[:, C_ONE:C_ONE + 128] = 1.0
    s, t = np.arange(128)[:, None] % 64, np.arange(64)[None, :]
    for n in range(LEVELS + 1):
        if n == 0:
            mask = s == t
        else:
            half = 1 << (n - 1)
            mask = (s // (2 * half) == t // (2 * half)) & (s % (2 * half) < half) & (t % (2 * half) >= half)
        c[:, C_LEVEL + 64 * n:C_LEVEL + 64 * n + 64] = mask * GK ** -0.5
    s, t = np.arange(128)[:, None], np.arange(128)[None, :]
    c[:, C_CAUSAL:C_CAUSAL + 128] = s <= t
    t = np.arange(T)
    c[:, C_RESTART:C_RESTART + T] = np.where(t < TP, t % L != 0, t % TS != 0)
    c[0:2 * NS, C_OWN:C_OWN + B] = np.arange(2 * NS)[:, None] % NS // TS == np.arange(B)[None, :]
    s, t = np.arange(NS)[:, None], np.arange(NS)[None, :]
    c[0:NS, C_SCAUSAL:C_SCAUSAL + NS] = (s <= t) & (s // TS == t // TS)
    sel = np.zeros((H, H * 128), np.float32)
    for h in range(H):
        sel[h, h * 128:(h + 1) * 128] = 1.0
    return c, sel


def kernel(**inputs):
    import numpy as _np
    import concourse.bacc as _bacc
    from concourse import mybir as _mybir
    from concourse.bass_utils import run_bass_kernel_spmd as _run

    nc = _bacc.Bacc("TRN2", target_bir_lowering=False, num_devices=1)
    given = {name: _np.ascontiguousarray(inputs[name]) for name in _INS}
    given["consts"], given["sel"] = _constants(_np)
    arrays, a, o = {}, {}, {}
    for name, value in given.items():
        arrays[f"in_{name}"] = value
        a[name] = nc.dram_tensor(f"in_{name}", value.shape, _mybir.dt.from_np(value.dtype), kind="ExternalInput").ap()
    for name, shape in _OUTS:
        o[name] = nc.dram_tensor(f"out_{name}", shape, _mybir.dt.float32, kind="ExternalOutput").ap()
    build(nc, a, o)
    r = _run(nc, [arrays], core_ids=[0])
    return tuple(r.results[0][f"out_{name}"] for name, _ in _OUTS)
```
